# Optimizing a Trainium2 kernel written in Bass

```python
import jax, jax.numpy as jnp
from jax import lax
import numpy as np

D_MODEL = 1024
BATCH = 1
SEQ = 1024
DEPTH = 1

D_FF = 2816
GLA_HEADS = 4
GLA_DK = D_MODEL // 2
GLA_DV = D_MODEL
GLA_HK = GLA_DK // GLA_HEADS
GLA_HV = GLA_DV // GLA_HEADS
GLA_GATE_RANK = 16
GLA_GATE_NORMALIZER = 16.0
GLA_CHUNK = 64
CONV_DIM = D_MODEL
CONV_WIDTH = 31
SPLIT_SIZES = (GLA_DK, GLA_DK, GLA_DV, GLA_GATE_RANK, GLA_DV, 2 * CONV_DIM, 2 * D_MODEL)
SPLIT_POINTS = tuple(int(s) for s in np.cumsum(SPLIT_SIZES)[:-1])
MIX_IN_WIDTH = int(sum(SPLIT_SIZES))
EPS = 1e-6

kernel_name = "hybrid_gla_conformer_conv_macaron"

def rms_norm(x, g):
    x32 = x.astype(jnp.float32)
    y = x32 * lax.rsqrt(jnp.mean(x32 * x32, axis=-1, keepdims=True) + EPS)
    return y.astype(x.dtype) * g

def layer_norm(x, g, b):
    x32 = x.astype(jnp.float32)
    mu = jnp.mean(x32, axis=-1, keepdims=True)
    var = jnp.mean(jnp.square(x32 - mu), axis=-1, keepdims=True)
    return ((x32 - mu) * lax.rsqrt(var + EPS)).astype(x.dtype) * g + b

def swiglu_ffn(h, w_in, w_out):
    gate, up = jnp.split(h @ w_in, 2, axis=-1)
    return (jax.nn.silu(gate) * up) @ w_out

def gla_chunked(q, k, v, log_a):
    B, S, H, HK = q.shape
    HV = v.shape[-1]
    n = S // GLA_CHUNK

    def to_chunks(t):
        return t.reshape(B, n, GLA_CHUNK, H, t.shape[-1]).transpose(1, 0, 3, 2, 4)

    qc, kc, vc = to_chunks(q), to_chunks(k), to_chunks(v)
    bc = jnp.cumsum(to_chunks(log_a), axis=-2)
    causal = jnp.tril(jnp.ones((GLA_CHUNK, GLA_CHUNK), dtype=bool))[:, :, None]

    def step(state, inp):
        q_, k_, v_, b_ = inp
        diff = b_[..., :, None, :] - b_[..., None, :, :]
        decay = jnp.exp(jnp.where(causal, diff, -jnp.inf))
        attn = jnp.einsum('bhik,bhjk,bhijk->bhij', q_, k_, decay)
        o = jnp.einsum('bhij,bhjv->bhiv', attn, v_) + jnp.einsum('bhik,bhkv->bhiv', q_ * jnp.exp(b_), state)
        b_last = b_[..., -1:, :]
        k_dec = k_ * jnp.exp(b_last - b_)
        state = jnp.exp(b_last[..., 0, :])[..., None] * state + jnp.einsum('bhjk,bhjv->bhkv', k_dec, v_)
        return state, o

    state0 = jnp.zeros((B, H, HK, HV), jnp.float32)
    _, o = lax.scan(step, state0, (qc, kc, vc, bc))
    return o.transpose(1, 0, 3, 2, 4).reshape(B, S, H, HV)

def causal_depthwise_conv(u, w, b):
    y = lax.conv_general_dilated(
        u, w[:, None, :].astype(u.dtype), window_strides=(1,), padding=((CONV_WIDTH - 1, 0),),
        dimension_numbers=('NWC', 'WIO', 'NWC'), feature_group_count=u.shape[-1])
    return y + b

def token_mixer(h, w_mix_in, gla_w_gate_up, gla_b_gate, gla_norm_g, gla_w_proj,
                conv_dw_w, conv_dw_b, conv_ln_g, conv_ln_b, conv_w_proj, w_mix_out):
    B, S, _ = h.shape
    z = h @ w_mix_in
    q, k, v, g_lr, og, cu, gates = jnp.split(z, SPLIT_POINTS, axis=-1)

    q = q.reshape(B, S, GLA_HEADS, GLA_HK).astype(jnp.float32) * (GLA_HK ** -0.5)
    k = k.reshape(B, S, GLA_HEADS, GLA_HK).astype(jnp.float32)
    v = v.reshape(B, S, GLA_HEADS, GLA_HV).astype(jnp.float32)
    gate_logit = (g_lr @ gla_w_gate_up + gla_b_gate).astype(jnp.float32)
    log_a = (jax.nn.log_sigmoid(gate_logit) / GLA_GATE_NORMALIZER).reshape(B, S, GLA_HEADS, GLA_HK)
    o = gla_chunked(q, k, v, log_a)
    o = rms_norm(o, gla_norm_g.astype(jnp.float32)).reshape(B, S, GLA_DV).astype(h.dtype)
    y_gla = (o * jax.nn.silu(og)) @ gla_w_proj

    ua, ub = jnp.split(cu, 2, axis=-1)
    u = ua * jax.nn.sigmoid(ub)
    u = causal_depthwise_conv(u, conv_dw_w, conv_dw_b)
    u = jax.nn.silu(layer_norm(u, conv_ln_g, conv_ln_b))
    y_conv = u @ conv_w_proj

    gate_a, gate_b = jnp.split(jax.nn.sigmoid(gates), 2, axis=-1)
    return (gate_a * y_gla + gate_b * y_conv) @ w_mix_out

def setup_inputs(seed: int = 0) -> dict:
    key = jax.random.key(seed)
    ks = jax.random.split(key, 24)
    f32 = jnp.float32
    L = DEPTH

    def nrm(k, shape, scale):
        return jax.random.normal(k, shape, f32) * scale

    def gain(k, shape):
        return 1.0 + 0.05 * jax.random.normal(k, shape, f32)

    return {
        "x": jax.random.normal(ks[0], (BATCH, SEQ, D_MODEL), f32),
        "ffn1_pre_g": gain(ks[1], (L, D_MODEL)),
        "ffn1_w_in": nrm(ks[2], (L, D_MODEL, 2 * D_FF), D_MODEL ** -0.5),
        "ffn1_w_out": nrm(ks[3], (L, D_FF, D_MODEL), D_FF ** -0.5),
        "ffn1_post_g": gain(ks[4], (L, D_MODEL)),
        "mix_pre_g": gain(ks[5], (L, D_MODEL)),
        "w_mix_in": nrm(ks[6], (L, D_MODEL, MIX_IN_WIDTH), D_MODEL ** -0.5),
        "gla_w_gate_up": nrm(ks[7], (L, GLA_GATE_RANK, GLA_DK), GLA_GATE_RANK ** -0.5),
        "gla_b_gate": nrm(ks[8], (L, GLA_DK), 0.1),
        "gla_norm_g": gain(ks[9], (L, GLA_HV)),
        "gla_w_proj": nrm(ks[10], (L, GLA_DV, D_MODEL), GLA_DV ** -0.5),
        "conv_dw_w": nrm(ks[11], (L, CONV_WIDTH, CONV_DIM), CONV_WIDTH ** -0.5),
        "conv_dw_b": nrm(ks[12], (L, CONV_DIM), 0.02),
        "conv_ln_g": gain(ks[13], (L, CONV_DIM)),
        "conv_ln_b": nrm(ks[14], (L, CONV_DIM), 0.02),
        "conv_w_proj": nrm(ks[15], (L, CONV_DIM, D_MODEL), CONV_DIM ** -0.5),
        "w_mix_out": nrm(ks[16], (L, D_MODEL, D_MODEL), D_MODEL ** -0.5),
        "mix_post_g": gain(ks[17], (L, D_MODEL)),
        "ffn2_pre_g": gain(ks[18], (L, D_MODEL)),
        "ffn2_w_in": nrm(ks[19], (L, D_MODEL, 2 * D_FF), D_MODEL ** -0.5),
        "ffn2_w_out": nrm(ks[20], (L, D_FF, D_MODEL), D_FF ** -0.5),
        "ffn2_post_g": gain(ks[21], (L, D_MODEL)),
    }

def reference(x, ffn1_pre_g, ffn1_w_in, ffn1_w_out, ffn1_post_g,
              mix_pre_g, w_mix_in, gla_w_gate_up, gla_b_gate, gla_norm_g, gla_w_proj,
              conv_dw_w, conv_dw_b, conv_ln_g, conv_ln_b, conv_w_proj, w_mix_out, mix_post_g,
              ffn2_pre_g, ffn2_w_in, ffn2_w_out, ffn2_post_g):
    for l in range(DEPTH):
        f = swiglu_ffn(rms_norm(x, ffn1_pre_g[l]), ffn1_w_in[l], ffn1_w_out[l])
        x = x + 0.5 * rms_norm(f, ffn1_post_g[l])
        m = token_mixer(rms_norm(x, mix_pre_g[l]), w_mix_in[l], gla_w_gate_up[l], gla_b_gate[l],
                        gla_norm_g[l], gla_w_proj[l], conv_dw_w[l], conv_dw_b[l], conv_ln_g[l],
                        conv_ln_b[l], conv_w_proj[l], w_mix_out[l])
        x = x + rms_norm(m, mix_post_g[l])
        f = swiglu_ffn(rms_norm(x, ffn2_pre_g[l]), ffn2_w_in[l], ffn2_w_out[l])
        x = x + 0.5 * rms_norm(f, ffn2_post_g[l])
    return x


_drawn_inputs = setup_inputs


def setup_inputs(seed=0):
    import zlib

    import numpy as np

    out = dict(_drawn_inputs(seed))
    spreads = {}
    factors = {'conv_dw_b': 2.878, 'conv_ln_b': 5.617, 'ffn2_post_g': 3.473}
    for name, (base, spread) in spreads.items():
        noise = np.random.default_rng([zlib.crc32(name.encode()), seed]).standard_normal(out[name].shape)
        drawn = base * np.exp(spread * noise) if base else spread * noise
        out[name] = __import__('jax').numpy.asarray(drawn.astype(out[name].dtype))
    for name, factor in factors.items():
        out[name] = (out[name] * factor).astype(out[name].dtype)
    return out
```

```python
import concourse.bass as bass
from concourse import mybir
from contextlib import ExitStack

D, SEQ, DFF = 1024, 1024, 2816
HEADS, DK, DV, RANK = 4, 128, 256, 16
TAPS = 31
EPS = 1e-6
P = 128
KT = D // P
TT = SEQ // P
HALF = SEQ // 2
FPAIRS = DFF // P // 2
C_Q, C_K, C_V = 0, HEADS * DK, 2 * HEADS * DK
C_LR = C_V + HEADS * DV
C_OG = C_LR + RANK
C_UA = C_OG + D
C_UB = C_UA + D
C_GA = C_UB + D
C_GB = C_GA + D
V_FFN1, V_MIX, V_FFN2, V_CB, V_LG, V_LB, V_BG, V_GN = 0, 8, 16, 24, 32, 40, 48, 52
VROWS = 54
S_FFN1 = 0
S_LR = S_FFN1 + 2 * FPAIRS
S_HEAD = S_LR + 1
S_GP = S_HEAD + 8 * HEADS
S_CP = S_GP + 4
S_FFN2 = S_CP + 4
S_END = S_FFN2 + 2 * FPAIRS
U_FFN1 = 0
U_LR = U_FFN1 + 4 * FPAIRS
U_HEAD = U_LR + 2
U_GP = U_HEAD + 16 * HEADS
U_CP = U_GP + 8
U_FFN2 = U_CP + 8
G_IN = 0
G_FFN1 = G_IN + 8
G_N1 = G_FFN1 + 8 * FPAIRS
G_HEAD = G_N1 + 8
G_LN = G_HEAD + 16 * HEADS
G_CP = G_LN + 4
G_N2 = G_CP + 8 * 4
G_FFN2 = G_N2 + 8
H_LG, H_KT, H_LV, H_DIAG, H_ST, H_O, H_OT = 0, 1, 2, 9, 10, 12, 14
HU_FFN1, HU_CP = 0, 4 * FPAIRS
HU_FFN2 = HU_CP + 8
O_FFN1, O_CP = 0, 2 * FPAIRS
O_FFN2 = O_CP + 8
O_END = O_FFN2 + 2 * FPAIRS
J_OG0, J_OG1, J_QK, J_V, J_CA, J_CB, J_G0, J_G1 = range(8)


def build(nc, x, ffn1_pre_g, ffn1_w_in, ffn1_w_out, ffn1_post_g, mix_pre_g, w_mix_in, gla_w_gate_up,
          gla_b_gate, gla_norm_g, gla_w_proj, conv_dw_w, conv_dw_b, conv_ln_g, conv_ln_b, conv_w_proj,
          w_mix_out, mix_post_g, ffn2_pre_g, ffn2_w_in, ffn2_w_out, ffn2_post_g, ident_c, masks_c, out):
    F32, FR, U8 = mybir.dt.float32, mybir.dt.float32r, mybir.dt.uint8
    ACT, ALU = mybir.ActivationFunctionType, mybir.AluOpType
    ds = bass.ds
    ctx = ExitStack()

    def ktiles(w):
        return w[0, :, :].rearrange("(k p) n -> p k n", p=P)

    w1v, w2v, wmv = ktiles(ffn1_w_in), ktiles(ffn2_w_in), ktiles(w_mix_in)
    wgv, wcv = ktiles(gla_w_proj), ktiles(conv_w_proj)
    o1v, o2v, omv = ktiles(ffn1_w_out), ktiles(ffn2_w_out), ktiles(w_mix_out)
    xv = x[0, :, :].rearrange("(t p) n -> p t n", p=P)
    outv = out[0, :, :].rearrange("(t p) n -> p t n", p=P)

    def scratch(name, shape):
        return nc.dram_tensor(name, shape, F32, kind="Internal").ap()

    x1_d = scratch("x1_d", (P, TT, D))
    x2_d = scratch("x2_d", (P, TT, D))
    gate_d = scratch("gate_d", (2, KT, P, SEQ))
    ot_d = scratch("ot_d", (KT, P, SEQ))
    c_d = scratch("c_d", (KT, P, SEQ))
    m_d = scratch("m_d", (KT, P, SEQ))

    with ctx:
        BASE = -(-nc.sbuf_base // 32) * 32

        def at(name, kb, shape, dt=F32):
            return nc.alloc_sbuf_tensor_at(name, shape, dt, offset=BASE + int(kb * 1024))

        XH = at("XH", 0, [P, KT, SEQ], FR)
        XL = at("XL", 32, [P, KT, SEQ], FR)
        w_raw = at("w_raw", 64, [P, 2, KT, 256])
        w_h = at("w_h", 80, [P, 2, KT, 256], FR)
        w_l = at("w_l", 96, [P, 2, KT, 256], FR)
        FACC = at("FACC", 112, [P, TT * D])
        H = at("H", 144, [P, 2, 2, SEQ], FR)
        XN = at("XN", 144, [P, 4, D])
        vec_rows = at("vec_rows", 144, [P, P])
        cw_rows = at("cw_rows", 145, [P, 2, P])
        mask_rows = at("mask_rows", 146, [P, 8, P])
        o_raw = at("o_raw", 160, [P, 2, D])
        o_h = at("o_h", 168, [P, 2, D], FR)
        o_l = at("o_l", 176, [P, 2, D], FR)
        xt = at("xt", 184, [P, 2, D])
        junk1 = at("junk1", 196, [P, D])
        junk2 = at("junk2", 200, [P, D])
        gB = at("gB", 192, [P, D])
        sgt = at("sgt", 196, [P, 2, 512])
        hf = at("hf", 200, [P, 2, 512])
        glrT = at("glrT", 112, [RANK, SEQ])
        b_sb = at("b_sb", 116, [P, SEQ])
        q_sb = at("q_sb", 120, [P, SEQ])
        k_sb = at("k_sb", 124, [P, SEQ])
        R = at("R", 128, [P, 3, SEQ])
        ON = at("ON", 128, [P, TT, DV])
        qb = at("qb", 140, [P, SEQ])
        kdT = at("kdT", 144, [P, SEQ])
        v_sb = at("v_sb", 148, [P, TT, DV])
        og = at("og", 156, [P, 2, SEQ])
        S_sb = at("S_sb", 164, [P, TT, DV])
        A_sb = at("A_sb", 172, [P, TT, P])
        ub = at("ub", 176, [P, 2, SEQ + TAPS - 1])
        acc = at("acc", 184.5, [P, 2, SEQ])
        tmp = at("tmp", 192.5, [P, 2, 2, 512])
        wgu = at("wgu", 200.5, [RANK, P])
        junk_o = at("junk_o", 202.5, [P, DV])
        CB = at("CB", 112, [P, KT, SEQ])
        OTF = at("OTF", 144, [P, KT, SEQ])
        sq = at("sq", 176, [P, 2, SEQ])
        gt = at("gt", 184, [P, 2, 2, 512])
        mt = at("mt", 192, [P, 2, 2, 512])
        vr = at("vr", 200, [P, 2, 512])
        ident = at("ident", 204, [P, P])
        masks = at("masks", 204.5, [P, 8, P], U8)
        cw = at("cw", 205.5, [P, 8 * TAPS])
        cols = at("cols", 206.5, [P, 64])
        el = at("el", 206.75, [P, TT])
        st = at("st", 206.8125, [P, 32])
        half_c = at("half_c", 206.9375, [P, 8])
        one_c = at("one_c", 207, [P, 1])
        ones_m = at("ones_m", 207.0625, [P, P])

        PU = nc.alloc_psum_tensor("PU", [P, 2, 2, 512], F32)
        PG = nc.alloc_psum_tensor("PG", [P, 2, 1024], F32)

        def sem(name):
            return ctx.enter_context(nc.semaphore(name))

        raw_full = [sem("raw_full0"), sem("raw_full1")]
        w_hi, w_lo = sem("w_hi"), sem("w_lo")
        o_full = [sem("o_full0"), sem("o_full1")]
        o_hi, o_lo = sem("o_hi"), sem("o_lo")
        unit_done = sem("unit_done")
        unit_free = [sem("unit_free0"), sem("unit_free1")]
        g_done = sem("g_done")
        g_free = [sem("g_free0"), sem("g_free1")]
        sg_ready, h_hi, h_lo, facc_zero = sem("sg_ready"), sem("h_hi"), sem("h_lo"), sem("facc_zero")
        const_in, const_set, rows_in, rows_zero, cols_ps, cols_ready = [sem(n) for n in (
            "const_in", "const_set", "rows_in", "rows_zero", "cols_ps", "cols_ready")]
        x_in = sem("x_in")
        x_full = [sem("x_full0"), sem("x_full1")]
        gb_full, sq1, rs1, post_a, x_new, x_stored = [sem(n) for n in (
            "gb_full", "sq1", "rs1", "post_a", "x_new", "x_stored")]
        sq2, rs2, xn_ready, xt_hi, xt_lo, pow_in = [sem(n) for n in (
            "sq2", "rs2", "xn_ready", "xt_hi", "xt_lo", "pow_in")]
        wgu_full, lg_act, la_done, b_done, d_ready, e_ready, t_ready = [sem(n) for n in (
            "wgu_full", "lg_act", "la_done", "b_done", "d_ready", "e_ready", "t_ready")]
        qb_exp, qb_ready, el_ready, state_step, gla_zero = [sem(n) for n in (
            "qb_exp", "qb_ready", "el_ready", "state_step", "gla_zero")]
        o_sq, o_rs, pool_mul, conv_step, conv_free, ot_stored = [sem(n) for n in (
            "o_sq", "o_rs", "pool_mul", "conv_step", "conv_free", "ot_stored")]
        gate_stored = [sem("gate_stored0"), sem("gate_stored1")]
        c_stored = [sem("c_stored0"), sem("c_stored1")]
        ot_full, c_full, centred, sq_ready, sq_used, var_pow, scaled, c_act, mm_t = [sem(n) for n in (
            "ot_full", "c_full", "centred", "sq_ready", "sq_used", "var_pow", "scaled", "c_act", "mm_t")]
        gt_full = [sem("gt_full0"), sem("gt_full1")]
        mt_full = [sem("mt_full0"), sem("mt_full1")]
        m_stored = [sem("m_stored0"), sem("m_stored1")]
        out_stored = sem("out_stored")

        block = ctx.enter_context(nc.Block())

        @block.sync
        def _(sp):
            def raw(s, par, parts):
                if isinstance(s, int):
                    if s >= 2:
                        sp.wait_ge(w_lo, s - 1)
                else:
                    sp.wait_ge(w_lo, s - 1)
                for dst, src in parts:
                    sp.dma_start(dst, src).then_inc(raw_full[par], 16)

            def two_blocks(s, par, va, ca, vb, cb):
                raw(s, par, [(w_raw[:, par, :, 0:P], va[:, :, ds(ca, P)]),
                             (w_raw[:, par, :, P:2 * P], vb[:, :, ds(cb, P)])])

            def one_block(s, par, va, ca):
                raw(s, par, [(w_raw[:, par, 0:4, 0:P], va[:, 0:4, ds(ca, P)]),
                             (w_raw[:, par, 4:8, 0:P], va[:, 4:8, ds(ca, P)])])

            def wide(s, par, va, ca):
                raw(s, par, [(w_raw[:, par, 0:4, :], va[:, 0:4, ds(ca, 2 * P)]),
                             (w_raw[:, par, 4:8, :], va[:, 4:8, ds(ca, 2 * P)])])

            def oraw(o, r, v, row):
                if not (isinstance(o, int) and o < 2):
                    sp.wait_ge(o_lo, o - 1)
                sp.dma_start(o_raw[:, r:r + 1, :], v[:, ds(row, 1), :]).then_inc(o_full[r], 16)

            def ffn(s0, o0, wv, ov):
                def step(i):
                    for a in range(2):
                        two_blocks(s0 + 2 * i + a, (s0 + a) % 2, wv, (2 * i + a) * P, wv, DFF + (2 * i + a) * P)
                    for a in range(2):
                        oraw(o0 + 2 * i + a, a, ov, 2 * i + a)
                step(0)
                with sp.Fori(1, FPAIRS) as i:
                    step(i)

            def norm(q0, src, dst, done):
                for t in range(TT):
                    if t == 0:
                        for a in range(2):
                            sp.dma_start(xt[:, a, :], src[:, a, :]).then_inc(x_full[a], 16)
                    sp.wait_ge(x_new, q0 + t + 1)
                    sp.dma_start(dst[:, t, :], FACC[:, t * D:(t + 1) * D]).then_inc(done, 16)
                    if t + 2 < TT:
                        sp.dma_start(xt[:, t % 2, :], src[:, t + 2, :]).then_inc(x_full[t % 2], 16)

            for t in range(TT):
                sp.dma_start(FACC[:, t * D:(t + 1) * D], xv[:, t, :]).then_inc(x_in, 16)
            sp.dma_start(ident[:, :], ident_c).then_inc(const_in, 16)
            sp.dma_start(mask_rows[:, :, :], masks_c).then_inc(const_in, 16)
            sp.wait_ge(rows_zero, 2)
            for row, vec, n in ((V_FFN1, ffn1_pre_g, 8), (V_MIX, mix_pre_g, 8), (V_FFN2, ffn2_pre_g, 8),
                                (V_CB, conv_dw_b, 8), (V_LG, conv_ln_g, 8), (V_LB, conv_ln_b, 8),
                                (V_BG, gla_b_gate, 4), (V_GN, gla_norm_g, 2)):
                sp.dma_start(vec_rows[row:row + n, :], vec[0, :].rearrange("(r c) -> r c", c=P)).then_inc(rows_in, 16)
            cwv = conv_dw_w[0, :, :].rearrange("w (c n) -> (w c) n", n=P)
            sp.dma_start(cw_rows[:, 0, :], cwv[0:P, :]).then_inc(rows_in, 16)
            sp.dma_start(cw_rows[0:8 * TAPS - P, 1, :], cwv[P:8 * TAPS, :]).then_inc(rows_in, 16)

            ffn(S_FFN1, O_FFN1, w1v, o1v)
            one_block(S_LR, S_LR % 2, wmv, C_LR)
            one_block(S_HEAD, S_HEAD % 2, wmv, C_OG)
            sp.dma_start(gB[:, :], ffn1_post_g[0, :].partition_broadcast(P)).then_inc(gb_full, 16)
            norm(0, xv, x1_d, x_stored)

            def head(h, first):
                s = S_HEAD + 8 * h
                par = [(S_HEAD + j) % 2 for j in range(8)]
                if not first:
                    one_block(s + J_OG0, par[J_OG0], wmv, C_OG + h * DV)
                one_block(s + J_OG1, par[J_OG1], wmv, C_OG + h * DV + P)
                sp.wait_ge(g_done, G_HEAD + 16 * h + H_LG - 15)
                if first:
                    sp.wait_ge(g_done, G_N1 + 8)
                sp.dma_start(wgu[:, :], gla_w_gate_up[0, :, ds(h * DK, DK)]).then_inc(wgu_full, 16)
                two_blocks(s + J_QK, par[J_QK], wmv, C_Q + h * DK, wmv, C_K + h * DK)
                if not first:
                    store_ot(h - 1)
                wide(s + J_V, par[J_V], wmv, C_V + h * DV)
                if not first:
                    store_c(h - 1)
                for a, j in ((0, J_CA), (1, J_CB)):
                    two_blocks(s + j, par[j], wmv, C_UA + (2 * h + a) * P, wmv, C_UB + (2 * h + a) * P)
                for a, j in ((0, J_G0), (1, J_G1)):
                    two_blocks(s + j, par[j], wmv, C_GA + (2 * h + a) * P, wmv, C_GB + (2 * h + a) * P)

            def store_ot(h):
                for p in range(2):
                    sp.wait_ge(g_free[p], G_HEAD // 2 + 8 * h + 8)
                sp.dma_start(ot_d[ds(2 * h, 2), :, :].rearrange("a p t -> p a t"), og[:, :, :]).then_inc(ot_stored, 16)

            def store_c(h):
                for a in range(2):
                    sp.wait_ge(conv_free, 2 + 2 * h + a + 1)
                    sp.dma_start(c_d[ds(2 * h + a, 1), :, :].rearrange("a p t -> p a t"),
                                 acc[:, a:a + 1, :]).then_inc(c_stored[a], 16)

            head(0, True)
            with sp.Fori(1, HEADS) as h:
                head(h, False)
            wide(S_GP, S_GP % 2, wgv, 0)
            wide(S_GP + 1, (S_GP + 1) % 2, wgv, 2 * P)
            store_ot(HEADS - 1)
            sp.wait_ge(ot_stored, 16 * HEADS)
            sp.wait_ge(g_done, G_LN)
            for k in range(KT):
                sp.dma_start(OTF[:, k, :], ot_d[k, :, :]).then_inc(ot_full, 16)
            store_c(HEADS - 1)
            for a in range(2):
                sp.wait_ge(c_stored[a], 16 * HEADS)
                sp.wait_ge(gate_stored[a], 32 * HEADS)
            for k in range(KT):
                sp.dma_start(CB[:, k, :], c_d[k, :, :]).then_inc(c_full, 16)

            def gates(n, which):
                f, half = n // 2 * 2, n % 2
                sp.dma_start(gt[:, n % 2, :, :],
                             gate_d[which, f:f + 2, :, half * HALF:(half + 1) * HALF].rearrange("a p t -> p a t"))\
                    .then_inc(gt_full[n % 2], 16)

            for n in range(8):
                if n >= 2:
                    sp.wait_ge(unit_free[n % 2], U_GP // 2 + n // 2)
                gates(n, 0)
                if n in (1, 3):
                    s = S_GP + 2 + n // 2
                    wide(s, s % 2, wgv, (s - S_GP) * 2 * P)
                if n == 5:
                    wide(S_CP, S_CP % 2, wcv, 0)
            for a in range(2):
                oraw(O_CP + a, a, omv, a)
            for i in range(4):
                for half in range(2):
                    n = 2 * i + half
                    if n < 2:
                        sp.wait_ge(unit_free[n], U_GP // 2 + 4)
                    else:
                        sp.wait_ge(mm_t, n - 1)
                    gates(n, 1)
                    sp.wait_ge(m_stored[half], 64)
                    sp.dma_start(mt[:, half, :, :],
                                 m_d[2 * i:2 * i + 2, :, half * HALF:(half + 1) * HALF].rearrange("a p t -> p a t"))\
                        .then_inc(mt_full[half], 16)
                s = S_CP + i + 1
                if i < 3:
                    wide(s, s % 2, wcv, (i + 1) * 2 * P)
                    for a in range(2):
                        oraw(O_CP + 2 * (i + 1) + a, a, omv, 2 * (i + 1) + a)
            for a in range(2):
                two_blocks(S_FFN2 + a, (S_FFN2 + a) % 2, w2v, a * P, w2v, DFF + a * P)
            for a in range(2):
                oraw(O_FFN2 + a, a, o2v, a)
            sp.wait_ge(h_lo, HU_FFN2)
            sp.dma_start(gB[:, :], mix_post_g[0, :].partition_broadcast(P)).then_inc(gb_full, 16)
            norm(8, x1_d, x2_d, x_stored)

            def ffn2_step(i):
                for a in range(2):
                    two_blocks(S_FFN2 + 2 * i + a, (S_FFN2 + a) % 2, w2v, (2 * i + a) * P, w2v, DFF + (2 * i + a) * P)
                for a in range(2):
                    oraw(O_FFN2 + 2 * i + a, a, o2v, 2 * i + a)

            sp.dma_start(gB[:, :], ffn2_post_g[0, :].partition_broadcast(P)).then_inc(gb_full, 16)
            with sp.Fori(1, FPAIRS) as i:
                ffn2_step(i)
            sp.wait_ge(x_stored, 32 * TT)
            norm(16, x2_d, outv, out_stored)
            sp.wait_ge(out_stored, 16 * TT)

        @block.tensor
        def _(pe):
            def dense(dst, hi, lo, xh, xl):
                for k in range(KT):
                    pe.matmul(dst, hi(k), xh(k), start=(k == 0), stop=False)
                    pe.matmul(dst, hi(k), xl(k), start=False, stop=False)
                    last = pe.matmul(dst, lo(k), xh(k), start=False, stop=(k == KT - 1))
                return last

            def unit(u, idx, s, par, half, nblk):
                pe.wait_ge(w_lo, s + 1)
                pe.wait_ge(unit_free[idx % 2], u)
                tok = slice(half * HALF, (half + 1) * HALF)
                for b in range(nblk):
                    col = slice(b * P, (b + 1) * P)
                    last = dense(PU[:, idx % 2, b, :], lambda k: w_h[:, par, k, col], lambda k: w_l[:, par, k, col],
                                 lambda k: XH[:, k, tok], lambda k: XL[:, k, tok])
                last.then_inc(unit_done, 1)

            def v_unit(u, idx, s, par, half):
                pe.wait_ge(w_lo, s + 1)
                pe.wait_ge(unit_free[idx % 2], u)
                for j in range(4):
                    tok = slice((4 * half + j) * P, (4 * half + j + 1) * P)
                    last = dense(PU[:, idx % 2, j // 2, (j % 2) * DV:(j % 2 + 1) * DV],
                                 lambda k: XH[:, k, tok], lambda k: XL[:, k, tok],
                                 lambda k: w_h[:, par, k, :], lambda k: w_l[:, par, k, :])
                last.then_inc(unit_done, 1)

            def g_wait(p, n):
                pe.wait_ge(g_free[p], n)

            def out_half(half, n0, o, wait_a, wait_b):
                for tp in range(2):
                    for a in range(2):
                        if tp == 0:
                            pe.wait_ge(h_lo, (wait_a, wait_b)[a])
                            pe.wait_ge(o_lo, o + a + 1)
                        for t in (0, 1):
                            if a == 0:
                                g_wait(t, n0 + 2 * half + tp)
                            tok = slice((4 * half + 2 * tp + t) * P, (4 * half + 2 * tp + t + 1) * P)
                            for n in range(2):
                                dst = PG[:, t, n * 512:(n + 1) * 512]
                                col = slice(n * 512, (n + 1) * 512)
                                pe.matmul(dst, H[:, a, 0, tok], o_h[:, a, col], start=(a == 0), stop=False)
                                pe.matmul(dst, H[:, a, 0, tok], o_l[:, a, col], start=False, stop=False)
                                last = pe.matmul(dst, H[:, a, 1, tok], o_h[:, a, col], start=False, stop=(a == 1))
                            if a == 1:
                                last.then_inc(g_done, 1)

            def ffn(s0, u0, g0, hu0, o0):
                def step(i):
                    u, s = u0 // 2 + 2 * i, s0 + 2 * i
                    pa, pb = s0 % 2, (s0 + 1) % 2
                    g = g0 // 2 + 4 * i
                    hu, o = hu0 + 4 * i, o0 + 2 * i
                    unit(u, 0, s, pa, 0, 2)
                    unit(u, 1, s + 1, pb, 0, 2)
                    out_half(0, g, o, hu + 1, hu + 2)
                    unit(u + 1, 0, s, pa, 1, 2)
                    unit(u + 1, 1, s + 1, pb, 1, 2)
                    out_half(1, g, o, hu + 3, hu + 4)
                with pe.Fori(0, FPAIRS) as i:
                    step(i)

            def transposes(g0, p0):
                for half in range(2):
                    pe.wait_ge(xn_ready, p0 + 4 * half + 4)
                    for fp in range(4):
                        g_wait(fp % 2, g0 // 2 + 2 * half + fp // 2)
                        for fi in range(2):
                            for j in range(4):
                                f = 2 * fp + fi
                                last = pe.transpose(PG[:, fp % 2, fi * 512 + j * P:fi * 512 + (j + 1) * P],
                                                    XN[:, j, f * P:(f + 1) * P], ident[:, :])
                        last.then_inc(g_done, 1)

            def xt_ready(g0):
                for p in range(2):
                    pe.wait_ge(g_free[p], g0 // 2 + 4)

            pe.wait_ge(const_in, 32)
            pe.wait_ge(rows_in, 160)
            pe.transpose(PU[:, 0, 0, 0:P], vec_rows[:, :], ident[:, :])
            for i in range(2):
                last = pe.transpose(PU[:, 0, 1, i * P:(i + 1) * P], cw_rows[:, i, :], ident[:, :])
            last.then_inc(cols_ps, 1)

            transposes(G_IN, 0)
            pe.wait_ge(cols_ready, 3)
            xt_ready(G_IN)
            ffn(S_FFN1, U_FFN1, G_FFN1, HU_FFN1, O_FFN1)

            transposes(G_N1, 8)
            xt_ready(G_N1)
            for half in range(2):
                unit(U_LR // 2, half, S_LR, S_LR % 2, half, 1)
            for p in range(2):
                pe.wait_ge(unit_free[p], U_LR // 2 + 1)
            pe.wait_ge(gla_zero, 2)
            pe.wait_ge(const_set, 3)

            with pe.Fori(0, HEADS) as h:
                s0 = S_HEAD + 8 * h
                u0 = U_HEAD // 2 + 8 * h
                gf = G_HEAD // 2 + 8 * h

                def hu(j, half, nblk=2):
                    unit(u0 + j, half, s0 + j, (S_HEAD + j) % 2, half, nblk)

                def level(lv, m):
                    g_wait(lv % 2, gf + 1 + lv // 2)
                    pe.wait_ge(t_ready, 8 * h + m + 1)
                    for c in range(TT):
                        tok = slice(c * P, (c + 1) * P)
                        last = pe.matmul(PG[:, lv % 2, tok], R[:, m % 3, tok], R[:, m % 3, tok], start=True, stop=True)
                    last.then_inc(g_done, 1)

                pe.wait_ge(wgu_full, 16 * h + 16)
                g_wait(0, gf)
                for n in range(2):
                    last = pe.matmul(PG[:, 0, n * 512:(n + 1) * 512], wgu[:, :], glrT[:, n * 512:(n + 1) * 512],
                                     start=True, stop=True)
                last.then_inc(g_done, 1)
                for j in (J_OG0, J_OG1):
                    for half in range(2):
                        hu(j, half, 1)
                for half in range(2):
                    hu(J_QK, half)
                for half in range(2):
                    v_unit(u0 + J_V, half, s0 + J_V, (S_HEAD + J_V) % 2, half)
                g_wait(1, gf)
                pe.wait_ge(t_ready, 8 * h + 1)
                for c in range(TT):
                    tok = slice(c * P, (c + 1) * P)
                    last = pe.transpose(PG[:, 1, tok], R[:, 0, tok], ident[:, :])
                last.then_inc(g_done, 1)
                level(0, 1)
                level(1, 2)
                hu(J_CA, 0)
                level(2, 3)
                level(3, 4)
                level(4, 5)
                hu(J_CA, 1)
                level(5, 6)
                level(6, 7)
                g_wait(1, gf + 4)
                for c in range(TT):
                    tok = slice(c * P, (c + 1) * P)
                    last = pe.matmul(PG[:, 1, tok], k_sb[:, tok], q_sb[:, tok], start=True, stop=True)
                last.then_inc(g_done, 1)
                hu(J_CB, 0)
                pe.wait_ge(g_free[1], gf + 1)
                for half in range(2):
                    pe.wait_ge(unit_free[half], u0 + J_V + 1)
                for half in range(2):
                    g_wait(half, gf + 5)
                    for c in range(4 * half, min(4 * half + 4, TT - 1)):
                        last = pe.matmul(PG[:, half, (c % 4) * DV:(c % 4 + 1) * DV], kdT[:, c * P:(c + 1) * P],
                                         v_sb[:, c, :], start=True, stop=True)
                    last.then_inc(g_done, 1)
                hu(J_CB, 1)
                pe.wait_ge(qb_ready, h + 1)
                for half in range(2):
                    pe.wait_ge(g_free[half], gf + 5)
                for half in range(2):
                    g_wait(half, gf + 6)
                    for c in range(4 * half, 4 * half + 4):
                        dst = PG[:, half, (c % 4) * DV:(c % 4 + 1) * DV]
                        pe.matmul(dst, A_sb[:, c, :], v_sb[:, c, :], start=True, stop=False)
                        last = pe.matmul(dst, qb[:, c * P:(c + 1) * P], S_sb[:, c, :], start=False, stop=True)
                    last.then_inc(g_done, 1)
                hu(J_G0, 0)
                for half in range(2):
                    g_wait(half, gf + 7)
                for dvt in range(2):
                    for c in range(TT):
                        last = pe.transpose(PG[:, dvt, c * P:(c + 1) * P], ON[:, c, dvt * P:(dvt + 1) * P], ident[:, :])
                    last.then_inc(g_done, 1)
                hu(J_G0, 1)
                for half in range(2):
                    hu(J_G1, half)

            def gp(e):
                for half in range(2):
                    unit(U_GP // 2 + e, half, S_GP + e, (S_GP + e) % 2, half, 2)

            pe.wait_ge(xt_lo, 8)
            gp(0)
            pe.wait_ge(c_full, 128)
            for half in range(2):
                g_wait(half, G_LN // 2)
                for k in range(KT):
                    last = pe.matmul(PG[:, half, 0:512], ones_m[:, :], CB[:, k, half * HALF:(half + 1) * HALF],
                                     start=(k == 0), stop=(k == KT - 1))
                last.then_inc(g_done, 1)
            gp(1)
            for half in range(2):
                g_wait(half, G_LN // 2 + 1)
            for k in range(KT):
                pe.wait_ge(sq_ready, k + 1)
                for half in range(2):
                    last = pe.matmul(PG[:, half, 0:512], ones_m[:, :], sq[:, k % 2, half * HALF:(half + 1) * HALF],
                                     start=(k == 0), stop=(k == KT - 1))
                last.then_inc(sq_used if k < KT - 1 else g_done, 1 if k < KT - 1 else 2)
            gp(2)
            gp(3)

            pe.wait_ge(xt_lo, 16)
            with pe.Fori(0, 2) as ii:
                for a in range(2):
                    i = 2 * ii + a
                    for half in range(2):
                        unit(U_CP // 2 + i, half, S_CP + i, (S_CP + a) % 2, half, 2)
                    hu = HU_CP + 2 * i
                    out_half(0, G_CP // 2 + 4 * i, O_CP + 2 * i, hu + 1, hu + 1)
                    out_half(1, G_CP // 2 + 4 * i, O_CP + 2 * i, hu + 2, hu + 2)
            transposes(G_N2, 16)
            xt_ready(G_N2)
            ffn(S_FFN2, U_FFN2, G_FFN2, HU_FFN2, O_FFN2)

        @block.scalar
        def _(act):
            A = act.activation

            def hi(par, full, used, nblk=2):
                act.wait_ge(raw_full[par], full)
                if used is not None:
                    act.wait_ge(unit_done, used)
                A(w_h[:, par, :, 0:nblk * P], w_raw[:, par, :, 0:nblk * P], ACT.Copy).then_inc(w_hi, 1)

            def full(s, turns):
                return 32 * (s // 2 + 1) + 32 * turns

            def ohi(i, a, o0, g0):
                act.wait_ge(o_full[a], 16 * (o0 // 2 + 1) + 16 * i)
                act.wait_ge(g_done, g0 + 8 * i)
                A(o_h[:, a, :], o_raw[:, a, :], ACT.Copy).then_inc(o_hi, 1)

            def ffn(s0, u0, g0, o0):
                def step(i, ahead):
                    for idx, (a, half) in enumerate(((0, 0), (1, 0), (0, 1), (1, 1))):
                        p, n = idx % 2, u0 // 2 + 2 * i + idx // 2
                        act.wait_ge(unit_done, u0 + 4 * i + idx + 1)
                        act.wait_ge(unit_free[p], n)
                        A(sgt[:, p, :], PU[:, p, 0, :], ACT.Silu).then_inc(sg_ready, 1)
                        act.wait_ge(unit_free[p], n + 1)
                        A(H[:, a, 0, half * HALF:(half + 1) * HALF], hf[:, p, :], ACT.Copy).then_inc(h_hi, 1)
                        if idx == 0:
                            for r in range(2):
                                ohi(i, r, o0, g0)
                        if half == 1 and ahead:
                            s = s0 + 2 + a
                            hi(s % 2, full(s, i), u0 + 4 * i + 3 + a, ahead)
                return step

            def norm(q0, p0, g0, half, pre):
                for step in range(6):
                    j = step
                    n1, n2 = q0 + 4 * half + j, p0 + 4 * half + j - 1
                    if g0 is not None and j < 4:
                        act.wait_ge(g_free[j % 2], g0 // 2 + 2 * half + j // 2 + 1)
                        if n1:
                            act.wait_ge(sq1, n1)
                        if half:
                            act.wait_ge(rs1, n1 - 3)
                        A(junk1[:, :], FACC[:, ds((4 * half + j) * D, D)], ACT.Square,
                          accum_out=st[:, j:j + 1]).then_inc(sq1, 1)
                    j = step - 2
                    if pre and 0 <= j < 4:
                        act.wait_ge(rs2, p0 + 4 * half + j + 1)
                        A(XN[:, j, :], FACC[:, ds((4 * half + j) * D, D)], ACT.Copy,
                          scale=st[:, 20 + j:21 + j]).then_inc(xn_ready, 1)
                    j = step - 1
                    if pre and 0 <= j < 4:
                        if g0 is None:
                            act.wait_ge(x_in, 16 * TT)
                        else:
                            act.wait_ge(x_new, q0 + 4 * half + j + 1)
                        if n2:
                            act.wait_ge(sq2, n2)
                        A(junk2[:, :], FACC[:, ds((4 * half + j) * D, D)], ACT.Square,
                          accum_out=st[:, 12 + j:13 + j]).then_inc(sq2, 1)

            def xt_fill(g0, gain, half):
                for fp in range(4):
                    act.wait_ge(g_done, g0 + 4 * half + fp + 1)
                    for fi in range(2):
                        f = 2 * fp + fi
                        A(XH[:, f, ds(half * HALF, HALF)], PG[:, fp % 2, fi * 512:(fi + 1) * 512], ACT.Copy,
                          scale=cols[:, gain + f:gain + f + 1]).then_inc(xt_hi, 1)

            for s in range(2):
                hi(s, 32, None)
            act.wait_ge(cols_ready, 3)
            for half in range(2):
                norm(0, 0, None, half, True)
                xt_fill(G_IN, V_FFN1, half)
            step = ffn(S_FFN1, U_FFN1, G_FFN1, O_FFN1)
            with act.Fori(0, FPAIRS - 1) as i:
                step(i, 2)
            step(FPAIRS - 1, 1)
            for half in range(2):
                norm(0, 8, G_N1 - 8, half, True)
                xt_fill(G_N1, V_MIX, half)
            act.wait_ge(x_stored, 16 * TT)
            for half in range(2):
                act.wait_ge(unit_done, U_LR + half + 1)
                A(glrT[:, half * HALF:(half + 1) * HALF], PU[0:RANK, half, 0, :], ACT.Copy).then_inc(unit_free[half], 1)

            with act.Fori(0, HEADS) as h:
                u0 = U_HEAD + 16 * h
                un = U_HEAD // 2 + 8 * h
                g0 = G_HEAD + 16 * h

                def ahead(j, nblk=2):
                    s = S_HEAD + j + 1
                    hi(s % 2, full(s, 4 * h), u0 + 2 * j, nblk)

                def to_tmp(j, half, turn, gated):
                    act.wait_ge(unit_done, u0 + 2 * j + half + 1)
                    if turn < 2:
                        act.wait_ge(gate_stored[half], 32 * h)
                    else:
                        act.wait_ge(pool_mul, 8 * h + turn - 1)
                    A(tmp[:, half, 0, :], PU[:, half, gated, :], ACT.Sigmoid)
                    A(tmp[:, half, 1, :], PU[:, half, 0, :], ACT.Copy).then_inc(unit_free[half], 1)

                def exps(first, last):
                    for m in range(first, last):
                        act.wait_ge(d_ready, 8 * h + m + 1)
                        A(R[:, m % 3, :], R[:, m % 3, :], ACT.Exp, scale=1.0 / 16).then_inc(e_ready, 1)

                ahead(J_OG0, 1)
                A(st[:, 28:29], cols[:, ds(V_BG + h, 1)], ACT.Copy).then_inc(lg_act, 1)
                act.wait_ge(lg_act, 4 * h + 1)
                act.wait_ge(g_done, g0 + H_LG + 1)
                A(R[:, 0, :], PG[:, 0, :], ACT.Abs, bias=st[:, 28:29]).then_inc(lg_act, 1)
                act.wait_ge(lg_act, 4 * h + 2)
                A(R[:, 0, :], R[:, 0, :], ACT.Exp, scale=-1.0).then_inc(lg_act, 1)
                act.wait_ge(lg_act, 4 * h + 3)
                A(R[:, 0, :], R[:, 0, :], ACT.Ln, bias=1.0).then_inc(lg_act, 1)
                for half in range(2):
                    to_tmp(J_OG0, half, half, 0)
                ahead(J_OG1)
                for half in range(2):
                    to_tmp(J_OG1, half, 2 + half, 0)
                ahead(J_QK)
                for half in range(2):
                    tok = slice(half * HALF, (half + 1) * HALF)
                    act.wait_ge(unit_done, u0 + 2 * J_QK + half + 1)
                    A(q_sb[:, tok], PU[:, half, 0, :], ACT.Copy, scale=DK ** -0.5)
                    A(k_sb[:, tok], PU[:, half, 1, :], ACT.Copy).then_inc(unit_free[half], 1)
                exps(0, 3)
                A(qb[:, :], b_sb[:, :], ACT.Exp, scale=1.0 / 16).then_inc(qb_exp, 1)
                A(el[:, :], b_sb[:, P - 1:SEQ:P], ACT.Exp, scale=1.0 / 16).then_inc(el_ready, 1)
                ahead(J_V)
                for half in range(2):
                    act.wait_ge(unit_done, u0 + 2 * J_V + half + 1)
                    A(v_sb[:, 4 * half:4 * half + 4, :], PU[:, half, :, :].rearrange("p a (b n) -> p (a b) n", b=2),
                      ACT.Copy).then_inc(unit_free[half], 1)
                act.wait_ge(g_done, g0 + H_KT + 1)
                A(kdT[:, :], PG[:, 1, :], ACT.Copy).then_inc(g_free[1], 1)
                exps(3, 6)
                ahead(J_CA)
                to_tmp(J_CA, 0, 4, 1)
                exps(6, 8)
                to_tmp(J_CA, 1, 5, 1)
                ahead(J_CB)
                for half in range(2):
                    to_tmp(J_CB, half, 6 + half, 1)
                for half in range(2):
                    act.wait_ge(g_done, g0 + H_O + half + 1)
                    for c in range(4):
                        act.wait_ge(o_sq, 8 * h + 4 * half + c)
                        A(junk_o[:, :], PG[:, half, c * DV:(c + 1) * DV], ACT.Square,
                          accum_out=st[:, 4 * half + c:4 * half + c + 1]).then_inc(o_sq, 1)
                    act.wait_ge(o_rs, 2 * h + half + 1)
                    for c in range(4):
                        last = A(ON[:, 4 * half + c, :], PG[:, half, c * DV:(c + 1) * DV], ACT.Copy,
                                 scale=st[:, 20 + 4 * half + c:21 + 4 * half + c])
                    last.then_inc(g_free[half], 1)
                ahead(J_G0)
                for k, j in ((0, J_G0), (1, J_G1)):
                    for half in range(2):
                        act.wait_ge(unit_done, u0 + 2 * j + half + 1)
                        if k == 0:
                            act.wait_ge(pool_mul, 8 * h + 7 + half)
                        else:
                            act.wait_ge(gate_stored[half], 32 * h + 16)
                        A(tmp[:, half, :, :], PU[:, half, :, :], ACT.Sigmoid).then_inc(unit_free[half], 1)
                        act.wait_ge(unit_free[half], un + j + 1)
                        act.dma_start(gate_d[:, ds(2 * h + k, 1), :, half * HALF:(half + 1) * HALF]
                                      .rearrange("a f p t -> p (a f) t"), tmp[:, half, :, :]).then_inc(gate_stored[half], 16)
                    if k == 0:
                        ahead(J_G1)

            act.wait_ge(unit_done, U_GP)
            for k in range(KT):
                act.wait_ge(ot_full, 16 * KT)
                A(XH[:, k, :], OTF[:, k, :], ACT.Copy).then_inc(xt_hi, 1)

            def gp_ahead(e):
                s = S_GP + e + 1
                hi(s % 2, full(s, 0), U_GP + 2 * e)

            def store_m(e):
                for half in range(2):
                    act.wait_ge(unit_free[half], U_GP // 2 + e + 1)
                    act.dma_start(m_d[2 * e:2 * e + 2, :, half * HALF:(half + 1) * HALF].rearrange("a p t -> p a t"),
                                  mt[:, half, :, :]).then_inc(m_stored[half], 16)

            gp_ahead(0)
            store_m(0)
            for k in range(KT):
                if k < KT - 1:
                    act.wait_ge(centred, k + 1)
                else:
                    for p in range(2):
                        act.wait_ge(g_free[p], G_LN // 2 + 1)
                if k >= 2:
                    act.wait_ge(sq_used, k - 1)
                A(sq[:, k % 2, :], CB[:, k, :], ACT.Square).then_inc(sq_ready, 1)
            gp_ahead(1)
            store_m(1)
            gp_ahead(2)
            for k in range(KT):
                act.wait_ge(scaled, k + 1)
                A(CB[:, k, :], CB[:, k, :], ACT.Silu, scale=cols[:, V_LG + k:V_LG + k + 1],
                  bias=cols[:, V_LB + k:V_LB + k + 1]).then_inc(c_act, 1)
            store_m(2)
            gp_ahead(3)
            store_m(3)
            act.wait_ge(unit_done, U_CP)
            for k in range(KT):
                act.wait_ge(c_act, k + 1)
                A(XH[:, k, :], CB[:, k, :], ACT.Copy).then_inc(xt_hi, 1)

            with act.Fori(0, 2) as ii:
                for a in range(2):
                    i = 2 * ii + a
                    s = S_CP + a + 1
                    hi(s % 2, full(s, ii), U_CP + 2 * i)
                    for r in range(2):
                        ohi(i, r, O_CP, G_CP)
                    for half in range(2):
                        act.wait_ge(mm_t, 2 * i + half + 1)
                        A(H[:, :, 0, half * HALF:(half + 1) * HALF], hf[:, :, :], ACT.Copy).then_inc(h_hi, 1)
            hi((S_FFN2 + 1) % 2, full(S_FFN2 + 1, 0), U_FFN2)
            for half in range(2):
                norm(8, 16, G_N2 - 8, half, True)
                xt_fill(G_N2, V_FFN2, half)
            step = ffn(S_FFN2, U_FFN2, G_FFN2, O_FFN2)
            with act.Fori(0, FPAIRS - 1) as i:
                step(i, 2)
            step(FPAIRS - 1, 0)
            for half in range(2):
                norm(16, 0, G_FFN2 + 8 * FPAIRS - 8, half, False)

        @block.vector
        def _(dve):
            TT_, STT, TS = dve.tensor_tensor, dve.scalar_tensor_tensor, dve.tensor_scalar

            def post(q0, half, factor, gbs):
                for j in range(4):
                    t = 4 * half + j
                    f = FACC[:, ds(t * D, D)]
                    dve.wait_ge(rs1, q0 + t + 1)
                    dve.wait_ge(gb_full, 16 * gbs)
                    STT(f, f, st[:, 4 + j:5 + j], gB[:, :], ALU.mult, ALU.mult).then_inc(post_a, 1)
                    dve.wait_ge(post_a, q0 + t + 1)
                    dve.wait_ge(x_full[j % 2], 16 * (q0 // 2 + j // 2 + 1) + 32 * half)
                    STT(f, f, factor, xt[:, j % 2, :], ALU.mult, ALU.add).then_inc(x_new, 1)

            def xt_fill(g0, gain, half, hi0):
                for fp in range(4):
                    for fi in range(2):
                        f = 2 * fp + fi
                        dve.wait_ge(xt_hi, hi0 + 8 * half + f + 1)
                        last = STT(XL[:, f, ds(half * HALF, HALF)], PG[:, fp % 2, fi * 512:(fi + 1) * 512],
                                   cols[:, gain + f:gain + f + 1], XH[:, f, ds(half * HALF, HALF)], ALU.mult, ALU.subtract)
                    last.then_inc(g_free[fp % 2], 1)

            def add_out(t, n):
                dve.wait_ge(g_done, n)
                TT_(FACC[:, t * D:(t + 1) * D], PG[:, t % 2, :], FACC[:, t * D:(t + 1) * D], ALU.add)\
                    .then_inc(g_free[t % 2], 1)

            def ffn(u0, g0, hu0):
                with dve.Fori(0, FPAIRS) as i:
                    for idx, (a, half) in enumerate(((0, 0), (1, 0), (0, 1), (1, 1))):
                        p = idx % 2
                        hu = hu0 + 4 * i + idx
                        dve.wait_ge(sg_ready, (hu0 - 8 * (hu0 > HU_CP)) + 4 * i + idx + 1)
                        TT_(hf[:, p, :], PU[:, p, 1, :], sgt[:, p, :], ALU.mult).then_inc(unit_free[p], 1)
                        dve.wait_ge(h_hi, hu + 1)
                        tok = slice(half * HALF, (half + 1) * HALF)
                        TT_(H[:, a, 1, tok], hf[:, p, :], H[:, a, 0, tok], ALU.subtract).then_inc(h_lo, 1)
                        if a == 1:
                            for t in range(4 * half, 4 * half + 4):
                                add_out(t, g0 + 8 * i + t + 1)

            dve.wait_ge(const_in, 32)
            dve.tensor_copy(masks[:, :, :], mask_rows[:, :, :]).then_inc(cols_ready, 1)
            dve.wait_ge(cols_ps, 1)
            dve.tensor_copy(cols[:, 0:VROWS], PU[:, 0, 0, 0:VROWS]).then_inc(cols_ready, 1)
            dve.tensor_copy(cw[:, :], PU[:, 0, 1, 0:8 * TAPS]).then_inc(cols_ready, 1)
            dve.wait_ge(cols_ready, 2)
            for half in range(2):
                xt_fill(G_IN, V_FFN1, half, 0)
            dve.wait_ge(xn_ready, 8)
            dve.memset(FACC[:, :], 0.0)
            ffn(U_FFN1, G_FFN1, HU_FFN1)
            for half in range(2):
                post(0, half, 0.5, 1)
                xt_fill(G_N1, V_MIX, half, 16)
            dve.wait_ge(const_set, 3)
            dve.memset(A_sb[:, :, :], 0.0).then_inc(gla_zero, 1)
            dve.memset(S_sb[:, 0, :], 0.0).then_inc(gla_zero, 1)
            for a in range(2):
                dve.memset(ub[:, a, 0:TAPS - 1], 0.0).then_inc(conv_free, 1)

            bc = b_sb[:, :].rearrange("p (c n) -> p c n", n=P)

            with dve.Fori(0, HEADS) as h:
                g0 = G_HEAD + 16 * h
                gf = G_HEAD // 2 + 8 * h
                un = U_HEAD // 2 + 8 * h

                def minus(m):
                    r = R[:, m % 3, :]
                    if m == 0:
                        TT_(r.rearrange("p (c n) -> p c n", n=P), bc[:, :, P - 1:P].to_broadcast([P, TT, P]), bc,
                            ALU.subtract).then_inc(d_ready, 1)
                        return
                    n = 1 << (m - 1)
                    bv = b_sb[:, :].rearrange("p (c s n) -> p c s n", s=2, n=n)
                    rv = r.rearrange("p (c s n) -> p c s n", s=2, n=n)
                    mid = bv[:, :, 0, n - 1:n].to_broadcast([P, SEQ // (2 * n), n])
                    TT_(rv[:, :, 1, :], bv[:, :, 1, :], mid, ALU.subtract)
                    TT_(rv[:, :, 0, :], mid, bv[:, :, 0, :], ALU.subtract).then_inc(d_ready, 1)

                def times(m):
                    dve.wait_ge(e_ready, 8 * h + m + 1)
                    r = R[:, m % 3, :]
                    if m == 0:
                        TT_(r, r, k_sb[:, :], ALU.mult).then_inc(t_ready, 1)
                        return
                    n = 1 << (m - 1)
                    rv, qv, kv = [y.rearrange("p (c s n) -> p c s n", s=2, n=n) for y in (r, q_sb[:, :], k_sb[:, :])]
                    TT_(rv[:, :, 1, :], rv[:, :, 1, :], qv[:, :, 1, :], ALU.mult)
                    TT_(rv[:, :, 0, :], rv[:, :, 0, :], kv[:, :, 0, :], ALU.mult).then_inc(t_ready, 1)

                def select(lv):
                    dve.wait_ge(gla_zero, 2)
                    if lv:
                        dve.wait_ge(g_free[(lv - 1) % 2], gf + (H_LV + lv - 1) // 2 + 1)
                    dve.wait_ge(g_done, g0 + H_LV + lv + 1)
                    dve.nop(nofuse=True)
                    dve.copy_predicated(A_sb[:, :, :], masks[:, lv:lv + 1, :].to_broadcast([P, TT, P]),
                                        PG[:, lv % 2, :].rearrange("p (c n) -> p c n", n=P)).then_inc(g_free[lv % 2], 1)

                dve.wait_ge(g_done, g0 + H_LG + 1)
                dve.wait_ge(lg_act, 4 * h + 2)
                TS(R[:, 1, :], PG[:, 0, :], cols[:, ds(V_BG + h, 1)], 0.0, ALU.add, ALU.min).then_inc(g_free[0], 1)
                dve.wait_ge(g_free[0], gf + 1)
                dve.wait_ge(lg_act, 4 * h + 4)
                TT_(R[:, 1, :], R[:, 1, :], R[:, 0, :], ALU.subtract).then_inc(la_done, 1)
                dve.wait_ge(la_done, h + 1)
                for c in range(TT):
                    tok = slice(c * P, (c + 1) * P)
                    last = dve.tensor_tensor_scan(b_sb[:, tok], one_c[:, 0:1].to_broadcast([P, P]), R[:, 1, tok], 0.0,
                                                  ALU.mult, ALU.add)
                last.then_inc(b_done, 1)
                dve.wait_ge(b_done, h + 1)
                for m in range(3):
                    minus(m)
                for half in range(2):
                    dve.wait_ge(unit_free[half], un + J_QK + 1)
                for m in range(3):
                    times(m)
                dve.wait_ge(qb_exp, h + 1)
                TT_(qb[:, :], qb[:, :], q_sb[:, :], ALU.mult).then_inc(qb_ready, 1)
                dve.wait_ge(g_done, g0 + H_KT + 1)
                minus(3)
                select(0)
                minus(4)
                select(1)
                minus(5)
                for m in (3, 4, 5):
                    times(m)
                select(2)
                minus(6)
                select(3)
                minus(7)
                select(4)
                times(6)
                times(7)
                select(5)
                select(6)
                select(7)
                dve.wait_ge(el_ready, h + 1)
                n = 0
                for c in range(TT - 1):
                    if c in (0, 4):
                        dve.wait_ge(g_done, g0 + H_ST + c // 4 + 1)
                    if c == 4:
                        dve.wait_ge(g_free[0], gf + 6)
                    elif c:
                        dve.wait_ge(state_step, 5 * h + n)
                    op = STT(S_sb[:, c + 1, :], S_sb[:, c, :], el[:, c:c + 1], PG[:, c // 4, (c % 4) * DV:(c % 4 + 1) * DV],
                             ALU.mult, ALU.add)
                    if c in (3, 6):
                        op.then_inc(g_free[c // 4], 1)
                    else:
                        op.then_inc(state_step, 1)
                        n += 1

                def conv(a):
                    dve.wait_ge(pool_mul, 8 * h + 6 + 2 * a)
                    dve.wait_ge(c_stored[a], 16 * h)
                    per = 2 * TAPS - 1
                    for w in range(TAPS):
                        for half in range(2):
                            n = 2 * w + half
                            o = acc[:, a, half * HALF:(half + 1) * HALF]
                            src = ub[:, a, half * HALF + w:half * HALF + w + HALF]
                            tap = cw[:, ds(8 * w + a + 2 * h, 1)]
                            if w == 0:
                                op = TS(o, src, tap, cols[:, ds(V_CB + a + 2 * h, 1)], ALU.mult, ALU.add)
                            else:
                                dve.wait_ge(conv_step, per * (2 * h + a) + n - 1)
                                op = STT(o, src, tap, o, ALU.mult, ALU.add)
                            op.then_inc(conv_step if n < per else conv_free, 1)

                conv(0)
                for d in range(2):
                    dve.wait_ge(g_done, g0 + H_OT + d + 1)
                    dve.wait_ge(pool_mul, 8 * h + 4)
                    STT(og[:, d, :], PG[:, d, :], cols[:, V_GN + d:V_GN + d + 1], og[:, d, :], ALU.mult, ALU.mult)\
                        .then_inc(g_free[d], 1)
                conv(1)

            for k in range(KT):
                dve.wait_ge(xt_hi, 32 + k + 1)
                TT_(XL[:, k, :], OTF[:, k, :], XH[:, k, :], ALU.subtract).then_inc(xt_lo, 1)

            def gated(e):
                for half in range(2):
                    dve.wait_ge(unit_done, U_GP + 2 * e + half + 1)
                    dve.wait_ge(gt_full[half], 16 * (e + 1))
                    if e:
                        dve.wait_ge(m_stored[half], 16 * e)
                    TT_(mt[:, half, :, :], PU[:, half, :, :], gt[:, half, :, :], ALU.mult).then_inc(unit_free[half], 1)

            gated(0)
            dve.wait_ge(g_done, G_LN + 2)
            for k in range(KT):
                if k < KT - 1:
                    v = CB[:, k, :].rearrange("p (a n) -> p a n", a=2)
                    TT_(v, v, PG[:, :, 0:512], ALU.subtract).then_inc(centred, 1)
                else:
                    for half in range(2):
                        v = CB[:, k, half * HALF:(half + 1) * HALF]
                        TT_(v, v, PG[:, half, 0:512], ALU.subtract).then_inc(g_free[half], 1)
            gated(1)
            dve.wait_ge(g_done, G_LN + 4)
            for half in range(2):
                TS(vr[:, half, :], PG[:, half, 0:512], EPS, None, ALU.add).then_inc(g_free[half], 1)
            dve.wait_ge(var_pow, 2)
            for k in range(KT):
                v = CB[:, k, :]
                TT_(v, v, vr[:, :, :].rearrange("p a n -> p (a n)"), ALU.mult).then_inc(scaled, 1)
            gated(2)
            gated(3)
            for k in range(KT):
                dve.wait_ge(xt_hi, 40 + k + 1)
                TT_(XL[:, k, :], CB[:, k, :], XH[:, k, :], ALU.subtract).then_inc(xt_lo, 1)
            dve.wait_ge(xt_lo, 2 * KT)
            dve.memset(FACC[:, :], 0.0)
            with dve.Fori(0, 4) as i:
                for half in range(2):
                    n = 2 * i + half
                    dve.wait_ge(unit_done, U_CP + n + 1)
                    dve.wait_ge(gt_full[half], 64 + 16 * (i + 1))
                    TT_(gt[:, half, :, :], PU[:, half, :, :], gt[:, half, :, :], ALU.mult).then_inc(unit_free[half], 1)
                    dve.wait_ge(unit_free[half], U_CP // 2 + i + 1)
                    dve.wait_ge(mt_full[half], 16 * (i + 1))
                    TT_(hf[:, :, :], gt[:, half, :, :], mt[:, half, :, :], ALU.add).then_inc(mm_t, 1)
                    dve.wait_ge(h_hi, HU_CP + n + 1)
                    tok = slice(half * HALF, (half + 1) * HALF)
                    TT_(H[:, :, 1, tok], hf[:, :, :], H[:, :, 0, tok], ALU.subtract).then_inc(h_lo, 1)
                for t in range(TT):
                    add_out(t, G_CP + 8 * i + t + 1)
            for half in range(2):
                post(8, half, 1.0, 2)
                xt_fill(G_N2, V_FFN2, half, 48)
            dve.wait_ge(x_stored, 32 * TT)
            dve.wait_ge(xn_ready, 24)
            dve.memset(FACC[:, :], 0.0)
            ffn(U_FFN2, G_FFN2, HU_FFN2)
            for half in range(2):
                post(16, half, 0.5, 3)

        @block.gpsimd
        def _(pool):
            PT, PS = pool.tensor_tensor, pool.tensor_scalar

            def lo(s, par, nblk=2):
                pool.wait_ge(w_hi, s + 1)
                c = slice(0, nblk * P)
                PT(w_l[:, par, :, c], w_raw[:, par, :, c], w_h[:, par, :, c], ALU.subtract).then_inc(w_lo, 1)

            def olo(o, a):
                pool.wait_ge(o_hi, o + 1)
                PT(o_l[:, a, :], o_raw[:, a, :], o_h[:, a, :], ALU.subtract).then_inc(o_lo, 1)

            def rstd(src, dst, n, scale, pows, done, eps=EPS):
                pool.nop(nofuse=True)
                PS(src, src, scale, eps, ALU.mult, ALU.add).then_inc(pow_in, 1)
                pool.wait_ge(pow_in, pows)
                PT(dst, src, half_c[:, 0:n], ALU.pow).then_inc(done, 1)

            def norm(q0, p0, k0, half, branch, pre):
                k = k0 + (4 * half if not (branch and pre) else 8 * half)
                n = 0
                for step in range(5):
                    if branch and step < 4:
                        n += 1
                        if half:
                            pool.wait_ge(post_a, q0 + step + 1)
                        pool.wait_ge(sq1, q0 + 4 * half + step + 1)
                        rstd(st[:, step:step + 1], st[:, 4 + step:5 + step], 1, 1.0 / D, k + n, rs1)
                    if pre and step:
                        n += 1
                        j = step - 1
                        pool.wait_ge(sq2, p0 + 4 * half + j + 1)
                        rstd(st[:, 12 + j:13 + j], st[:, 20 + j:21 + j], 1, 1.0 / D, k + n, rs2)

            pool.memset(vec_rows[:, :], 0.0).then_inc(rows_zero, 1)
            pool.memset(cw_rows[:, :, :], 0.0).then_inc(rows_zero, 1)
            pool.memset(half_c[:, :], -0.5).then_inc(const_set, 1)
            pool.memset(one_c[:, :], 1.0).then_inc(const_set, 1)
            pool.memset(ones_m[:, :], 1.0 / D).then_inc(const_set, 1)
            pool.wait_ge(const_set, 3)
            for half in range(2):
                norm(0, 0, 0, half, False, True)
            lo(0, 0)
            lo(1, 1)

            def ffn(s0, o0):
                def step(i, nblk):
                    for a in range(2):
                        olo(o0 + 2 * i + a, a)
                    if nblk:
                        for a in range(2):
                            lo(s0 + 2 * i + 2 + a, (s0 + a) % 2, nblk)
                return step

            step = ffn(S_FFN1, O_FFN1)
            with pool.Fori(0, FPAIRS - 1) as i:
                step(i, 2)
            step(FPAIRS - 1, 1)
            for half in range(2):
                norm(0, 8, 8, half, True, True)

            with pool.Fori(0, HEADS) as h:
                s0 = S_HEAD + 8 * h
                un = U_HEAD // 2 + 8 * h

                def ahead(j, nblk=2):
                    lo(s0 + j + 1, (S_HEAD + j + 1) % 2, nblk)

                ahead(J_OG0, 1)
                for half in range(2):
                    pool.wait_ge(ot_stored, 16 * h)
                for d, j in ((0, J_OG0), (1, J_OG1)):
                    for half in range(2):
                        pool.wait_ge(unit_free[half], un + j + 1)
                        PT(og[:, d, half * HALF:(half + 1) * HALF], tmp[:, half, 0, :], tmp[:, half, 1, :], ALU.mult)\
                            .then_inc(pool_mul, 1)
                    ahead(j + 1)
                ahead(J_V)
                ahead(J_CA)
                for a, j in ((0, J_CA), (1, J_CB)):
                    pool.wait_ge(conv_free, 2 * h + a + 1)
                    for half in range(2):
                        pool.wait_ge(unit_free[half], un + j + 1)
                        PT(ub[:, a, TAPS - 1 + half * HALF:TAPS - 1 + (half + 1) * HALF], tmp[:, half, 0, :],
                           tmp[:, half, 1, :], ALU.mult).then_inc(pool_mul, 1)
                    if a == 0:
                        ahead(J_CB)
                for half in range(2):
                    pool.wait_ge(o_sq, 8 * h + 4 * half + 4)
                    rstd(st[:, 4 * half:4 * half + 4], st[:, 20 + 4 * half:24 + 4 * half], 4, 1.0 / DV,
                         24 + 2 * h + half + 1, o_rs)
                ahead(J_G0)
                ahead(J_G1)

            for e in range(2):
                lo(S_GP + e + 1, (S_GP + e + 1) % 2)
            for half in range(2):
                pool.wait_ge(g_free[half], G_LN // 2 + 2)
            for half in range(2):
                PT(vr[:, half, :], vr[:, half, :], half_c[:, 0:1].to_broadcast([P, 512]), ALU.pow).then_inc(var_pow, 1)
            for e in range(2, 4):
                lo(S_GP + e + 1, (S_GP + e + 1) % 2)
            with pool.Fori(0, 2) as ii:
                for a in range(2):
                    i = 2 * ii + a
                    lo(S_CP + i + 1, (S_CP + a + 1) % 2)
                    for r in range(2):
                        olo(O_CP + 2 * i + r, r)
            lo(S_FFN2 + 1, (S_FFN2 + 1) % 2)
            for half in range(2):
                norm(8, 16, 32, half, True, True)
            step = ffn(S_FFN2, O_FFN2)
            with pool.Fori(0, FPAIRS - 1) as i:
                step(i, 2)
            step(FPAIRS - 1, 0)
            for half in range(2):
                norm(16, 0, 48, half, True, False)


INPUTS = ["x", "ffn1_pre_g", "ffn1_w_in", "ffn1_w_out", "ffn1_post_g", "mix_pre_g", "w_mix_in", "gla_w_gate_up",
          "gla_b_gate", "gla_norm_g", "gla_w_proj", "conv_dw_w", "conv_dw_b", "conv_ln_g", "conv_ln_b",
          "conv_w_proj", "w_mix_out", "mix_post_g", "ffn2_pre_g", "ffn2_w_in", "ffn2_w_out", "ffn2_post_g"]


def kernel(**inputs):
    import numpy as np
    import concourse.bacc as bacc
    from concourse.bass_utils import run_bass_kernel_spmd

    nc = bacc.Bacc("TRN2", target_bir_lowering=False, num_devices=1)
    j, i = np.arange(P)[:, None], np.arange(P)[None, :]
    levels = [(j // (2 * n) == i // (2 * n)) & (j % (2 * n) < n) & (i % (2 * n) >= n) for n in (1 << l for l in range(7))]
    masks = np.stack(levels + [i == j], axis=1).astype(np.float32)
    arrays = {f"in_{n}": np.ascontiguousarray(inputs[n]) for n in INPUTS}
    arrays["c_ident"] = np.eye(P, dtype=np.float32)
    arrays["c_masks"] = np.ascontiguousarray(masks)
    args = [nc.dram_tensor(n, a.shape, mybir.dt.from_np(a.dtype), kind="ExternalInput").ap() for n, a in arrays.items()]
    out = nc.dram_tensor("out_dram", (1, SEQ, D), mybir.dt.float32, kind="ExternalOutput").ap()
    build(nc, *args, out)
    r = run_bass_kernel_spmd(nc, [arrays], core_ids=[0])
    return r.results[0]["out_dram"]
```

```python
import concourse.bass as bass
from concourse import mybir
from contextlib import ExitStack

D, SEQ, DFF = 1024, 1024, 2816
HEADS, DK, DV, RANK = 4, 128, 256, 16
TAPS = 31
EPS = 1e-6
P = 128
KT = D // P
TT = SEQ // P
HALF = SEQ // 2
FPAIRS = DFF // P // 2
C_Q, C_K, C_V = 0, HEADS * DK, 2 * HEADS * DK
C_LR = C_V + HEADS * DV
C_OG = C_LR + RANK
C_UA = C_OG + D
C_UB = C_UA + D
C_GA = C_UB + D
C_GB = C_GA + D
V_FFN1, V_MIX, V_FFN2, V_CB, V_LG, V_LB, V_BG, V_GN = 0, 8, 16, 24, 32, 40, 48, 52
VROWS = 54
S_FFN1 = 0
S_LR = S_FFN1 + 2 * FPAIRS
S_HEAD = S_LR + 1
S_GP = S_HEAD + 8 * HEADS
S_CP = S_GP + 4
S_FFN2 = S_CP + 4
S_END = S_FFN2 + 2 * FPAIRS
U_IN0 = 0
U_FFN1 = U_IN0 + 4
U_N1A = U_FFN1 + 4 + 4 * FPAIRS
U_X = U_N1A + 4
U_N1B = U_X + 2
U_LR2 = U_N1B + 4
U_HEAD = U_LR2
U_GP = U_HEAD + 16 * HEADS
U_CP = U_GP + 8
U_N2A = U_CP + 8
U_FFN2 = U_N2A + 4
G_FFN1 = 0
G_HEAD = G_FFN1 + 8 * FPAIRS
G_LN = G_HEAD + 16 * HEADS
G_CP = G_LN + 4
G_FFN2 = G_CP + 8 * 4
H_LG, H_KT, H_LV, H_DIAG, H_ST, H_O, H_OT = 0, 1, 2, 9, 10, 12, 14
HU_FFN1, HU_CP = 0, 4 * FPAIRS
HU_FFN2 = HU_CP + 8
O_FFN1, O_CP = 0, 2 * FPAIRS
O_FFN2 = O_CP + 8
O_END = O_FFN2 + 2 * FPAIRS
CPLACE = [0, 1, 2, 5, 6, 7, 3, 4]
GP_KS = [6, 7, 0, 1, 2, 3, 4, 5]
J_OG0, J_OG1, J_QK, J_V, J_CA, J_CB, J_G0, J_G1 = range(8)


def ffn_unit(u0, i, idx):
    if isinstance(i, int) and i == 0:
        return u0 + idx + (4 if idx >= 2 else 0)
    return u0 + 8 + 4 * (i - 1) + idx


def ffn_unit2(u0, i, idx):
    if isinstance(i, int) and i == 0:
        return (u0 + (4 if idx >= 2 else 0) + idx) // 2
    return u0 // 2 + 4 + 2 * (i - 1) + idx // 2


def head_unit(h, j, half):
    if isinstance(h, int) and h == 0 and j == J_OG0 and half == 0:
        return U_X
    return U_HEAD + 16 * h + 2 * j + half


def head_unit2(h, j, half):
    if isinstance(h, int) and h == 0 and j == J_OG0 and half == 0:
        return U_X // 2
    return U_HEAD // 2 + 8 * h + j


def build(nc, x, ffn1_pre_g, ffn1_w_in, ffn1_w_out, ffn1_post_g, mix_pre_g, w_mix_in, gla_w_gate_up,
          gla_b_gate, gla_norm_g, gla_w_proj, conv_dw_w, conv_dw_b, conv_ln_g, conv_ln_b, conv_w_proj,
          w_mix_out, mix_post_g, ffn2_pre_g, ffn2_w_in, ffn2_w_out, ffn2_post_g, ident_c, masks_c, out):
    F32, FR, U8 = mybir.dt.float32, mybir.dt.float32r, mybir.dt.uint8
    ACT, ALU = mybir.ActivationFunctionType, mybir.AluOpType
    ds = bass.ds
    ctx = ExitStack()

    def ktiles(w):
        return w[0, :, :].rearrange("(k p) n -> p k n", p=P)

    w1v, w2v, wmv = ktiles(ffn1_w_in), ktiles(ffn2_w_in), ktiles(w_mix_in)
    wgv, wcv = ktiles(gla_w_proj), ktiles(conv_w_proj)
    o1v, o2v, omv = ktiles(ffn1_w_out), ktiles(ffn2_w_out), ktiles(w_mix_out)
    xv = x[0, :, :].rearrange("(t p) n -> p t n", p=P)
    outv = out[0, :, :].rearrange("(t p) n -> p t n", p=P)

    def scratch(name, shape):
        return nc.dram_tensor(name, shape, F32, kind="Internal").ap()

    x1_d = scratch("x1_d", (P, TT, D))
    x2_d = scratch("x2_d", (P, TT, D))
    gate_d = scratch("gate_d", (2, KT, P, SEQ))
    ot_d = scratch("ot_d", (KT, P, SEQ))
    c_d = scratch("c_d", (KT, P, SEQ))
    m_d = scratch("m_d", (KT, P, SEQ))

    with ctx:
        BASE = -(-nc.sbuf_base // 32) * 32

        def at(name, kb, shape, dt=F32):
            return nc.alloc_sbuf_tensor_at(name, shape, dt, offset=BASE + int(kb * 1024))

        XH = at("XH", 0, [P, KT, SEQ], FR)
        XL = at("XL", 32, [P, KT, SEQ], FR)
        w_raw = at("w_raw", 64, [P, 2, KT, 256])
        w_h = at("w_h", 80, [P, 2, KT, 256], FR)
        w_l = at("w_l", 96, [P, 2, KT, 256], FR)
        FACC = at("FACC", 112, [P, TT * D])
        H = at("H", 144, [P, 2, 2, SEQ], FR)
        vec_rows = at("vec_rows", 184, [P, P])
        cw_rows = at("cw_rows", 185, [P, 2, P])
        mask_rows = at("mask_rows", 186, [P, 8, P])
        o_raw = at("o_raw", 160, [P, 2, D])
        o_h = at("o_h", 168, [P, 2, D], FR)
        o_l = at("o_l", 176, [P, 2, D], FR)
        xt = at("xt", 184, [P, 2, D])
        junk_s = [at("junk_s1", 196, [P, D]), at("junk_s2", 200, [P, D])]
        junk_w = [at("junk_w1", 160, [P, D]), at("junk_w2", 164, [P, D])]
        gB = at("gB", 192, [P, D])
        sgt = at("sgt", 196, [P, 2, 512])
        hf = at("hf", 200, [P, 2, 512])
        glrT = at("glrT", 112, [RANK, SEQ])
        b_sb = at("b_sb", 116, [P, SEQ])
        q_sb = at("q_sb", 120, [P, SEQ])
        k_sb = at("k_sb", 124, [P, SEQ])
        R = at("R", 128, [P, 3, SEQ])
        ON = at("ON", 128, [P, TT, DV])
        qb = at("qb", 140, [P, SEQ])
        kdT = at("kdT", 144, [P, SEQ])
        v_sb = at("v_sb", 148, [P, TT, DV])
        og = at("og", 156, [P, 2, SEQ])
        S_sb = at("S_sb", 164, [P, TT, DV])
        A_sb = at("A_sb", 172, [P, TT, P])
        ub = at("ub", 176, [P, 2, SEQ + TAPS - 1])
        acc = at("acc", 184.5, [P, 2, SEQ])
        tmp = at("tmp", 192.5, [P, 2, 2, 512])
        wgu = at("wgu", 200.5, [RANK, P])
        junk_o = at("junk_o", 202.5, [P, DV])
        CB = at("CB", 144, [P, KT, SEQ])
        OTF = at("OTF", 112, [P, KT - 2, SEQ])
        sq = at("sq", 176, [P, 2, SEQ])
        gt = at("gt", 184, [P, 2, 2, 512])
        mt = at("mt", 192, [P, 2, 2, 512])
        vr = at("vr", 200, [P, 2, 512])
        ident = at("ident", 204, [P, P])
        masks = at("masks", 204.5, [P, 8, P], U8)
        cw = at("cw", 205.5, [P, 8 * TAPS])
        cols = at("cols", 206.5, [P, 64])
        el = at("el", 206.75, [P, TT])
        st = at("st", 206.8125, [P, 32])
        half_c = at("half_c", 206.9375, [P, 8])
        one_c = at("one_c", 207, [P, 1])
        ones_m = at("ones_m", 207.0625, [P, P])

        PU = nc.alloc_psum_tensor("PU", [P, 2, 2, 512], F32)
        PG = nc.alloc_psum_tensor("PG", [P, 2, 1024], F32)

        def sem(name):
            return ctx.enter_context(nc.semaphore(name))

        raw_full = [sem("raw_full0"), sem("raw_full1")]
        w_hi, w_lo = sem("w_hi"), sem("w_lo")
        o_full = [sem("o_full0"), sem("o_full1")]
        o_hi, o_lo = sem("o_hi"), sem("o_lo")
        unit_done = sem("unit_done")
        unit_free = [sem("unit_free0"), sem("unit_free1")]
        g_done = sem("g_done")
        g_free = [sem("g_free0"), sem("g_free1")]
        sg_ready, h_hi, h_lo = sem("sg_ready"), sem("h_hi"), sem("h_lo")
        ident_in, mask_in, const_set, rows_in, rows_zero, cols_ps, cols_ready = [sem(n) for n in (
            "ident_in", "mask_in", "const_set", "rows_in", "rows_zero", "cols_ps", "cols_ready")]
        x_in = [sem(f"x_in{t}") for t in range(TT)]
        x_full = [sem("x_full0"), sem("x_full1")]
        gb_full, sq1, rs1, post_a, x_new = [sem(n) for n in ("gb_full", "sq1", "rs1", "post_a", "x_new")]
        x_stored = [sem(f"x_stored{t}") for t in range(TT)]
        sq2, rs2, xn_ready, xt_hi, pow_in = [sem(n) for n in ("sq2", "rs2", "xn_ready", "xt_hi", "pow_in")]
        wgu_full, lg_act, la_done, b_done, d_ready, e_ready, t_ready = [sem(n) for n in (
            "wgu_full", "lg_act", "la_done", "b_done", "d_ready", "e_ready", "t_ready")]
        qb_exp, qb_ready, el_ready, state_step, gla_zero = [sem(n) for n in (
            "qb_exp", "qb_ready", "el_ready", "state_step", "gla_zero")]
        o_sq, o_rs, pool_mul, conv_step, conv_free, ot_stored = [sem(n) for n in (
            "o_sq", "o_rs", "pool_mul", "conv_step", "conv_free", "ot_stored")]
        gate_stored = [sem("gate_stored0"), sem("gate_stored1")]
        c_stored = [sem("c_stored0"), sem("c_stored1")]
        ot_full, ot_lo0, ot_lo1, ct_lo, c_early, c_late, c_sum = [sem(n) for n in (
            "ot_full", "ot_lo0", "ot_lo1", "ct_lo", "c_early", "c_late", "c_sum")]
        centred, sq_ready, sq_sum, rs_ready, diag_ready, scaled, c_act, mm_t = [sem(n) for n in (
            "centred", "sq_ready", "sq_sum", "rs_ready", "diag_ready", "scaled", "c_act", "mm_t")]
        gt_full = [sem("gt_full0"), sem("gt_full1")]
        mt_full = [sem("mt_full0"), sem("mt_full1")]
        m_stored = [sem("m_stored0"), sem("m_stored1")]
        out_stored = sem("out_stored")

        block = ctx.enter_context(nc.Block())

        @block.sync
        def _(sp):
            def raw(s, par, parts):
                if isinstance(s, int):
                    if s >= 2:
                        sp.wait_ge(w_lo, s - 1)
                else:
                    sp.wait_ge(w_lo, s - 1)
                for dst, src in parts:
                    sp.dma_start(dst, src).then_inc(raw_full[par], 16)

            def two_blocks(s, par, va, ca, vb, cb):
                raw(s, par, [(w_raw[:, par, :, 0:P], va[:, :, ds(ca, P)]),
                             (w_raw[:, par, :, P:2 * P], vb[:, :, ds(cb, P)])])

            def one_block(s, par, va, ca):
                raw(s, par, [(w_raw[:, par, 0:4, 0:P], va[:, 0:4, ds(ca, P)]),
                             (w_raw[:, par, 4:8, 0:P], va[:, 4:8, ds(ca, P)])])

            def wide(s, par, va, ca):
                raw(s, par, [(w_raw[:, par, 0:4, :], va[:, 0:4, ds(ca, 2 * P)]),
                             (w_raw[:, par, 4:8, :], va[:, 4:8, ds(ca, 2 * P)])])

            def oraw(o, r, v, row):
                if not (isinstance(o, int) and o < 2):
                    sp.wait_ge(o_lo, o - 1)
                sp.dma_start(o_raw[:, r:r + 1, :], v[:, ds(row, 1), :]).then_inc(o_full[r], 16)

            def norm(q0, src, dst, done):
                for a in range(2):
                    sp.dma_start(xt[:, a, :], src[:, a, :]).then_inc(x_full[a], 16)
                for t in range(TT):
                    sp.wait_ge(x_new, q0 + t + 1)
                    sp.dma_start(dst[:, t, :], FACC[:, t * D:(t + 1) * D]).then_inc(done[t], 16)
                    if t + 2 < TT:
                        sp.dma_start(xt[:, t % 2, :], src[:, t + 2, :]).then_inc(x_full[t % 2], 16)

            def load_x(tiles):
                for t in tiles:
                    sp.dma_start(FACC[:, t * D:(t + 1) * D], xv[:, t, :]).then_inc(x_in[t], 16)

            load_x(range(1))
            sp.dma_start(ident[:, :], ident_c).then_inc(ident_in, 16)
            load_x(range(1, 4))
            for a in range(2):
                two_blocks(S_FFN1 + a, a, w1v, a * P, w1v, DFF + a * P)
            sp.wait_ge(rows_zero, 2)
            for row, vec, n in ((V_FFN1, ffn1_pre_g, 8), (V_MIX, mix_pre_g, 8), (V_FFN2, ffn2_pre_g, 8),
                                (V_CB, conv_dw_b, 8), (V_LG, conv_ln_g, 8), (V_LB, conv_ln_b, 8),
                                (V_BG, gla_b_gate, 4), (V_GN, gla_norm_g, 2)):
                sp.dma_start(vec_rows[row:row + n, :], vec[0, :].rearrange("(r c) -> r c", c=P)).then_inc(rows_in, 16)
            cwv = conv_dw_w[0, :, :].rearrange("w (c n) -> (w c) n", n=P)
            sp.dma_start(cw_rows[:, 0, :], cwv[0:P, :]).then_inc(rows_in, 16)
            sp.dma_start(cw_rows[0:8 * TAPS - P, 1, :], cwv[P:8 * TAPS, :]).then_inc(rows_in, 16)
            load_x(range(4, TT))
            sp.dma_start(mask_rows[:, :, :], masks_c).then_inc(mask_in, 16)

            def ffn(s0, o0, wv, ov):
                with sp.Fori(1, FPAIRS) as i:
                    for a in range(2):
                        two_blocks(s0 + 2 * i + a, (s0 + a) % 2, wv, (2 * i + a) * P, wv, DFF + (2 * i + a) * P)
                    for a in range(2):
                        oraw(o0 + 2 * i + a, a, ov, 2 * i + a)

            for a in range(2):
                oraw(O_FFN1 + a, a, o1v, a)
            ffn(S_FFN1, O_FFN1, w1v, o1v)
            one_block(S_LR, S_LR % 2, wmv, C_LR)
            one_block(S_HEAD, S_HEAD % 2, wmv, C_OG)
            sp.dma_start(gB[:, :], ffn1_post_g[0, :].partition_broadcast(P)).then_inc(gb_full, 16)
            sp.wait_ge(cols_ready, 3)
            norm(0, xv, x1_d, x_stored)

            def head(h, first):
                s = S_HEAD + 8 * h
                par = [(S_HEAD + j) % 2 for j in range(8)]
                if not first:
                    one_block(s + J_OG0, par[J_OG0], wmv, C_OG + h * DV)
                one_block(s + J_OG1, par[J_OG1], wmv, C_OG + h * DV + P)
                if first:
                    sp.wait_ge(unit_done, U_LR2)
                else:
                    sp.wait_ge(g_done, G_HEAD + 16 * h - 15)
                sp.dma_start(wgu[:, :], gla_w_gate_up[0, :, ds(h * DK, DK)]).then_inc(wgu_full, 16)
                two_blocks(s + J_QK, par[J_QK], wmv, C_Q + h * DK, wmv, C_K + h * DK)
                if not first:
                    store_ot(h - 1)
                wide(s + J_V, par[J_V], wmv, C_V + h * DV)
                if not first:
                    store_c(h - 1)
                for a, j in ((0, J_CA), (1, J_CB)):
                    two_blocks(s + j, par[j], wmv, C_UA + (2 * h + a) * P, wmv, C_UB + (2 * h + a) * P)
                for a, j in ((0, J_G0), (1, J_G1)):
                    two_blocks(s + j, par[j], wmv, C_GA + (2 * h + a) * P, wmv, C_GB + (2 * h + a) * P)

            def store_ot(h):
                for p in range(2):
                    sp.wait_ge(g_free[p], G_HEAD // 2 + 8 * h + 8)
                sp.dma_start(ot_d[ds(2 * h, 2), :, :].rearrange("a p t -> p a t"), og[:, :, :]).then_inc(ot_stored, 16)

            def store_c(h):
                for a in range(2):
                    sp.wait_ge(conv_free, 2 + 2 * h + a + 1)
                    sp.dma_start(c_d[ds(2 * h + a, 1), :, :].rearrange("a p t -> p a t"),
                                 acc[:, a:a + 1, :]).then_inc(c_stored[a], 16)

            head(0, True)
            with sp.Fori(1, HEADS) as h:
                head(h, False)
            wide(S_GP, S_GP % 2, wgv, 0)
            wide(S_GP + 1, (S_GP + 1) % 2, wgv, 2 * P)
            sp.wait_ge(g_done, G_LN)
            sp.wait_ge(ot_stored, 16 * (HEADS - 1))
            for k in range(KT - 2):
                sp.dma_start(OTF[:, k, :], ot_d[k, :, :]).then_inc(ot_full, 16)
            for a in range(2):
                sp.wait_ge(c_stored[a], 16 * (HEADS - 1))
            for k in range(KT - 2):
                sp.dma_start(CB[:, CPLACE[k], :], c_d[k, :, :]).then_inc(c_early, 16)
            store_c(HEADS - 1)
            for a in range(2):
                sp.wait_ge(c_stored[a], 16 * HEADS)
                sp.wait_ge(gate_stored[a], 32 * HEADS)

            def gates(n, which):
                f, half = n // 2 * 2, n % 2
                sp.dma_start(gt[:, n % 2, :, :],
                             gate_d[which, f:f + 2, :, half * HALF:(half + 1) * HALF].rearrange("a p t -> p a t"))\
                    .then_inc(gt_full[n % 2], 16)

            for n in range(8):
                if n >= 2:
                    sp.wait_ge(unit_free[n % 2], U_GP // 2 + n // 2)
                gates(n, 0)
                if n == 1:
                    sp.wait_ge(ot_lo0, 2)
                    sp.wait_ge(ot_lo1, 2)
                    for k in (KT - 2, KT - 1):
                        sp.dma_start(CB[:, CPLACE[k], :], c_d[k, :, :]).then_inc(c_late, 16)
                if n in (1, 3):
                    s = S_GP + 2 + n // 2
                    wide(s, s % 2, wgv, (s - S_GP) * 2 * P)
                if n == 5:
                    wide(S_CP, S_CP % 2, wcv, 0)
            for i in range(4):
                for half in range(2):
                    n = 2 * i + half
                    if n < 2:
                        sp.wait_ge(unit_free[n], U_GP // 2 + 4)
                    else:
                        sp.wait_ge(mm_t, n - 1)
                    gates(n, 1)
                    sp.wait_ge(m_stored[half], 64)
                    sp.dma_start(mt[:, half, :, :],
                                 m_d[2 * i:2 * i + 2, :, half * HALF:(half + 1) * HALF].rearrange("a p t -> p a t"))\
                        .then_inc(mt_full[half], 16)
                s = S_CP + i + 1
                if i == 0:
                    sp.wait_ge(ct_lo, 2 * KT)
                    for a in range(2):
                        oraw(O_CP + a, a, omv, a)
                if i < 3:
                    wide(s, s % 2, wcv, (i + 1) * 2 * P)
                    for a in range(2):
                        oraw(O_CP + 2 * (i + 1) + a, a, omv, 2 * (i + 1) + a)
            for a in range(2):
                two_blocks(S_FFN2 + a, (S_FFN2 + a) % 2, w2v, a * P, w2v, DFF + a * P)
            for a in range(2):
                oraw(O_FFN2 + a, a, o2v, a)
            sp.wait_ge(h_lo, HU_FFN2)
            sp.dma_start(gB[:, :], mix_post_g[0, :].partition_broadcast(P)).then_inc(gb_full, 16)
            norm(8, x1_d, x2_d, x_stored)

            sp.dma_start(gB[:, :], ffn2_post_g[0, :].partition_broadcast(P)).then_inc(gb_full, 16)
            ffn(S_FFN2, O_FFN2, w2v, o2v)
            for t in range(TT):
                sp.wait_ge(x_stored[t], 32)
            norm(16, x2_d, outv, [out_stored] * TT)
            sp.wait_ge(out_stored, 16 * TT)

        @block.tensor
        def _(pe):
            def dense(dst, hi, lo, xh, xl, ks=range(KT), ready=None):
                for n, k in enumerate(ks):
                    if ready and n in ready:
                        pe.wait_ge(*ready[n])
                    pe.matmul(dst, hi(k), xh(k), start=(n == 0), stop=False)
                    pe.matmul(dst, hi(k), xl(k), start=False, stop=False)
                    last = pe.matmul(dst, lo(k), xh(k), start=False, stop=(n == KT - 1))
                return last

            def unit(u, p, s, par, half, nblk, ready=None, ks=range(KT)):
                pe.wait_ge(w_lo, s + 1)
                pe.wait_ge(unit_free[p], u)
                tok = slice(half * HALF, (half + 1) * HALF)
                for b in range(nblk):
                    col = slice(b * P, (b + 1) * P)
                    last = dense(PU[:, p, b, :], lambda k: w_h[:, par, k, col], lambda k: w_l[:, par, k, col],
                                 lambda k: XH[:, k, tok], lambda k: XL[:, k, tok], ks, None if b else ready)
                last.then_inc(unit_done, 1)

            def v_unit(u, idx, s, par, half):
                pe.wait_ge(w_lo, s + 1)
                pe.wait_ge(unit_free[idx % 2], u)
                for j in range(4):
                    tok = slice((4 * half + j) * P, (4 * half + j + 1) * P)
                    last = dense(PU[:, idx % 2, j // 2, (j % 2) * DV:(j % 2 + 1) * DV],
                                 lambda k: XH[:, k, tok], lambda k: XL[:, k, tok],
                                 lambda k: w_h[:, par, k, :], lambda k: w_l[:, par, k, :])
                last.then_inc(unit_done, 1)

            def g_wait(p, n):
                pe.wait_ge(g_free[p], n)

            def out_half(half, n0, o, wait_a, wait_b, between=None):
                for tp in range(2):
                    if between:
                        between(tp)
                    for a in range(2):
                        if tp == 0:
                            pe.wait_ge(h_lo, (wait_a, wait_b)[a])
                            pe.wait_ge(o_lo, o + a + 1)
                        for t in (0, 1):
                            if a == 0:
                                g_wait(t, n0 + 2 * half + tp)
                            tok = slice((4 * half + 2 * tp + t) * P, (4 * half + 2 * tp + t + 1) * P)
                            for n in range(2):
                                dst = PG[:, t, n * 512:(n + 1) * 512]
                                col = slice(n * 512, (n + 1) * 512)
                                pe.matmul(dst, H[:, a, 0, tok], o_h[:, a, col], start=(a == 0), stop=False)
                                pe.matmul(dst, H[:, a, 0, tok], o_l[:, a, col], start=False, stop=False)
                                last = pe.matmul(dst, H[:, a, 1, tok], o_h[:, a, col], start=False, stop=(a == 1))
                            if a == 1:
                                last.then_inc(g_done, 1)

            def transposes(u, p0, half, fps):
                if fps[0] == 0:
                    pe.wait_ge(xn_ready, p0 + 4 * half + 4)
                for fp in fps:
                    pe.wait_ge(unit_free[fp % 2], u // 2 + fp // 2)
                    for fi in range(2):
                        f = 2 * fp + fi
                        for j in range(4):
                            c = (4 * half + j) * D + f * P
                            last = pe.transpose(PU[:, fp % 2, fi, j * P:(j + 1) * P], FACC[:, c:c + P], ident[:, :])
                    last.then_inc(unit_done, 1)

            def filled(u):
                return {2 * fp: (unit_free[fp % 2], (u + fp) // 2 + 1) for fp in range(4)}

            def ffn(s0, u0, g0, hu0, o0, p0, u_next=None):
                def step(i, between0=None, between1=None):
                    s, hu, o, g = s0 + 2 * i, hu0 + 4 * i, o0 + 2 * i, g0 // 2 + 4 * i
                    first = isinstance(i, int) and i == 0

                    def ab(idx, ready=None):
                        unit(ffn_unit2(u0, i, idx), idx % 2, s + idx % 2, (s0 + idx) % 2, idx // 2, 2, ready)

                    ab(0, filled(u0 - 4) if first else None)
                    ab(1)
                    out_half(0, g, o, hu + 1, hu + 2, between0)
                    ab(2, filled(u0 + 2) if first else None)
                    ab(3)
                    out_half(1, g, o, hu + 3, hu + 4, between1)

                step(0, between0=lambda tp: transposes(u0 + 2, p0, 1, (2 * tp, 2 * tp + 1)))
                with pe.Fori(1, FPAIRS - 1) as i:
                    step(i)
                step(FPAIRS - 1, between1=None if u_next is None else
                     lambda tp: transposes(u_next, p0 + 8, 0, (2 * tp, 2 * tp + 1)))

            pe.wait_ge(ident_in, 16)
            pe.wait_ge(rows_in, 160)
            pe.transpose(PG[:, 0, 0:P], vec_rows[:, :], ident[:, :])
            for i in range(2):
                last = pe.transpose(PG[:, 0, 512 + i * P:512 + (i + 1) * P], cw_rows[:, i, :], ident[:, :])
            last.then_inc(cols_ps, 1)

            transposes(U_IN0, 0, 0, range(4))
            pe.wait_ge(cols_ready, 2)
            ffn(S_FFN1, U_FFN1, G_FFN1, HU_FFN1, O_FFN1, 0, U_N1A)
            pe.wait_ge(const_set, 3)

            def head(h, first):
                s0 = S_HEAD + 8 * h
                u0 = U_HEAD // 2 + 8 * h
                gf = G_HEAD // 2 + 8 * h

                def hu(j, half, nblk=2):
                    unit(u0 + j, half, s0 + j, (S_HEAD + j) % 2, half, nblk)

                def level(lv, m):
                    g_wait(lv % 2, gf + 1 + lv // 2)
                    pe.wait_ge(t_ready, 8 * h + m + 1)
                    for c in range(TT):
                        tok = slice(c * P, (c + 1) * P)
                        last = pe.matmul(PG[:, lv % 2, tok], R[:, m % 3, tok], R[:, m % 3, tok], start=True, stop=True)
                    last.then_inc(g_done, 1)

                if first:
                    unit(U_X // 2, 0, S_HEAD, S_HEAD % 2, 0, 1, filled(U_N1A))
                    unit(U_X // 2, 1, S_LR, S_LR % 2, 0, 1)
                    transposes(U_N1B, 8, 1, range(4))
                    unit(U_LR2 // 2, 0, S_LR, S_LR % 2, 1, 1, filled(U_N1B))
                    unit(U_LR2 // 2, 1, S_HEAD, S_HEAD % 2, 1, 1)
                    pe.wait_ge(unit_free[0], U_LR2 // 2 + 1)
                pe.wait_ge(wgu_full, 16 * h + 16)
                g_wait(0, gf)
                for n in range(2):
                    last = pe.matmul(PG[:, 0, n * 512:(n + 1) * 512], wgu[:, :], glrT[:, n * 512:(n + 1) * 512],
                                     start=True, stop=True)
                last.then_inc(g_done, 1)
                for j in (J_OG0, J_OG1):
                    for half in range(2):
                        if not (first and j == J_OG0):
                            hu(j, half, 1)
                for half in range(2):
                    hu(J_QK, half)
                for half in range(2):
                    v_unit(u0 + J_V, half, s0 + J_V, (S_HEAD + J_V) % 2, half)
                g_wait(1, gf)
                pe.wait_ge(t_ready, 8 * h + 1)
                for c in range(TT):
                    tok = slice(c * P, (c + 1) * P)
                    last = pe.transpose(PG[:, 1, tok], R[:, 0, tok], ident[:, :])
                last.then_inc(g_done, 1)
                level(0, 1)
                level(1, 2)
                hu(J_CA, 0)
                level(2, 3)
                level(3, 4)
                level(4, 5)
                hu(J_CA, 1)
                level(5, 6)
                level(6, 7)
                g_wait(1, gf + 4)
                for c in range(TT):
                    tok = slice(c * P, (c + 1) * P)
                    last = pe.matmul(PG[:, 1, tok], k_sb[:, tok], q_sb[:, tok], start=True, stop=True)
                last.then_inc(g_done, 1)
                hu(J_CB, 0)
                pe.wait_ge(g_free[1], gf + 1)
                for half in range(2):
                    pe.wait_ge(unit_free[half], u0 + J_V + 1)
                for half in range(2):
                    g_wait(half, gf + 5)
                    for c in range(4 * half, min(4 * half + 4, TT - 1)):
                        last = pe.matmul(PG[:, half, (c % 4) * DV:(c % 4 + 1) * DV], kdT[:, c * P:(c + 1) * P],
                                         v_sb[:, c, :], start=True, stop=True)
                    last.then_inc(g_done, 1)
                hu(J_CB, 1)
                pe.wait_ge(qb_ready, h + 1)
                for half in range(2):
                    pe.wait_ge(g_free[half], gf + 5)
                for half in range(2):
                    g_wait(half, gf + 6)
                    for c in range(4 * half, 4 * half + 4):
                        dst = PG[:, half, (c % 4) * DV:(c % 4 + 1) * DV]
                        pe.matmul(dst, A_sb[:, c, :], v_sb[:, c, :], start=True, stop=False)
                        last = pe.matmul(dst, qb[:, c * P:(c + 1) * P], S_sb[:, c, :], start=False, stop=True)
                    last.then_inc(g_done, 1)
                hu(J_G0, 0)
                for half in range(2):
                    g_wait(half, gf + 7)
                for dvt in range(2):
                    for c in range(TT):
                        last = pe.transpose(PG[:, dvt, c * P:(c + 1) * P], ON[:, c, dvt * P:(dvt + 1) * P], ident[:, :])
                    last.then_inc(g_done, 1)
                hu(J_G0, 1)
                for half in range(2):
                    hu(J_G1, half)

            head(0, True)
            with pe.Fori(1, HEADS) as h:
                head(h, False)

            def gp(e, half):
                ready = {n: ((ot_lo0, ot_lo1)[half], n + 1) for n in range(KT)} if e == 0 else None
                unit(U_GP // 2 + e, half, S_GP + e, (S_GP + e) % 2, half, 2, ready, GP_KS)

            gp(0, 0)
            gp(0, 1)
            pe.wait_ge(c_sum, KT - 1)
            for half in range(2):
                g_wait(half, G_LN // 2)
                pe.matmul(PG[:, half, 0:512], ones_m[:, :], vr[:, half, :], start=True, stop=True).then_inc(g_done, 1)
            gp(1, 0)
            gp(1, 1)
            pe.wait_ge(sq_sum, KT - 1)
            g_wait(0, G_LN // 2 + 1)
            for c in range(TT):
                last = pe.matmul(PG[:, 0, c:c + 1], vr[:, c // 4, (c % 4) * P:(c % 4 + 1) * P], ones_m[:, 0:1],
                                 start=True, stop=True)
            last.then_inc(g_done, 1)
            gp(2, 0)
            pe.wait_ge(diag_ready, 1)
            g_wait(1, G_LN // 2 + 1)
            for half in range(2):
                last = pe.matmul(PG[:, 1, half * 512:(half + 1) * 512], ones_m[:, :], vr[:, half, :], start=True, stop=True)
            last.then_inc(g_done, 1)
            gp(2, 1)
            gp(3, 0)
            gp(3, 1)

            for i in range(4):
                for half in range(2):
                    ready = {n: (ct_lo, 8 * half + n + 1) for n in range(KT)} if i == 0 else None
                    unit(U_CP // 2 + i, half, S_CP + i, (S_CP + i) % 2, half, 2, ready)
                hu = HU_CP + 2 * i
                out_half(0, G_CP // 2 + 4 * i, O_CP + 2 * i, hu + 1, hu + 1)
                out_half(1, G_CP // 2 + 4 * i, O_CP + 2 * i, hu + 2, hu + 2)
            transposes(U_N2A, 16, 0, range(4))
            ffn(S_FFN2, U_FFN2, G_FFN2, HU_FFN2, O_FFN2, 16)

        @block.scalar
        def _(act):
            A = act.activation

            def hi(par, full, used, nblk=2):
                act.wait_ge(raw_full[par], full)
                if used is not None:
                    act.wait_ge(unit_done, used)
                A(w_h[:, par, :, 0:nblk * P], w_raw[:, par, :, 0:nblk * P], ACT.Copy).then_inc(w_hi, 1)

            def full(s, turns):
                return 32 * (s // 2 + 1) + 32 * turns

            def ohi(i, a, o0, g0):
                act.wait_ge(o_full[a], 16 * (o0 // 2 + 1) + 16 * i)
                if not (isinstance(i, int) and g0 + 8 * i == 0):
                    act.wait_ge(g_done, g0 + 8 * i)
                A(o_h[:, a, :], o_raw[:, a, :], ACT.Copy).then_inc(o_hi, 1)

            def facc(t):
                return FACC[:, t * D:(t + 1) * D]

            def square1(t, q0, g, junk):
                act.wait_ge(g_free[t % 2], g)
                if q0 + t:
                    act.wait_ge(sq1, q0 + t)
                if t >= 4:
                    act.wait_ge(rs1, q0 + t - 3)
                A(junk[0][:, :], facc(t), ACT.Square, accum_out=st[:, t % 4:t % 4 + 1]).then_inc(sq1, 1)

            def square2(t, p0, junk):
                if p0:
                    act.wait_ge(x_new, p0 - 8 + t + 1)
                else:
                    act.wait_ge(x_in[t], 16)
                if p0 + t:
                    act.wait_ge(sq2, p0 + t)
                A(junk[1][:, :], facc(t), ACT.Square, accum_out=st[:, 12 + t % 4:13 + t % 4]).then_inc(sq2, 1)

            def scale(t, p0):
                if p0:
                    act.wait_ge(x_stored[t], 2 * p0)
                act.wait_ge(rs2, p0 + t + 1)
                A(facc(t), facc(t), ACT.Copy, scale=st[:, 20 + t % 4:21 + t % 4]).then_inc(xn_ready, 1)

            def fill(u, gain, half, fps=range(4)):
                for fp in fps:
                    act.wait_ge(unit_done, u + fp + 1)
                    for fi in range(2):
                        f = 2 * fp + fi
                        A(XH[:, f, half * HALF:(half + 1) * HALF], PU[:, fp % 2, fi, :], ACT.Copy,
                          scale=cols[:, gain + f:gain + f + 1]).then_inc(xt_hi, 1)

            def evacuate(i, idx, u0):
                p, a, half = idx % 2, idx % 2, idx // 2
                act.wait_ge(unit_done, ffn_unit(u0, i, idx) + 1)
                act.wait_ge(unit_free[p], ffn_unit2(u0, i, idx))
                A(sgt[:, p, :], PU[:, p, 0, :], ACT.Silu).then_inc(sg_ready, 1)
                act.wait_ge(unit_free[p], ffn_unit2(u0, i, idx) + 1)
                A(H[:, a, 0, half * HALF:(half + 1) * HALF], hf[:, p, :], ACT.Copy).then_inc(h_hi, 1)

            def ffn(s0, u0, g0, o0, gain, last_turn):
                def ahead(i, a, nblk=2):
                    s = s0 + 2 + a
                    hi(s % 2, full(s, i), ffn_unit(u0, i, 2 + a) + 1, nblk)

                def step(i, after_b0=None):
                    evacuate(i, 0, u0)
                    for r in range(2):
                        ohi(i, r, o0, g0)
                    evacuate(i, 1, u0)
                    if after_b0:
                        after_b0()
                    evacuate(i, 2, u0)
                    ahead(i, 0)
                    evacuate(i, 3, u0)
                    ahead(i, 1)

                step(0, lambda: fill(u0 + 2, gain, 1))
                with act.Fori(1, FPAIRS - 1) as i:
                    step(i)
                i = FPAIRS - 1
                evacuate(i, 0, u0)
                for r in range(2):
                    ohi(i, r, o0, g0)
                evacuate(i, 1, u0)
                last_turn(i, lambda a, nblk: ahead(i, a, nblk), g0 // 2 + 4 * i)

            square2(0, 0, junk_s)
            for t in range(1, 4):
                square2(t, 0, junk_s)
                scale(t - 1, 0)
            scale(3, 0)
            hi(0, 32, None)
            act.wait_ge(cols_ready, 2)
            fill(U_IN0, V_FFN1, 0)
            hi(1, 32, None)
            for t in range(4, 8):
                square2(t, 0, junk_s)
                if t > 4:
                    scale(t - 1, 0)
            scale(7, 0)

            def ffn1_last(i, ahead, g):
                def s1(t):
                    square1(t, 0, g + t // 2 + 1, junk_w)

                def s2(t):
                    square2(t, 8, junk_w)

                s1(0), s1(1), s2(0), s1(2), s2(1), s1(3), s2(2), s2(3)
                for t in range(4):
                    scale(t, 8)
                evacuate(i, 2, U_FFN1)
                ahead(0, 1)
                evacuate(i, 3, U_FFN1)
                ahead(1, 1)
                fill(U_N1A, V_MIX, 0, (0, 1))
                s1(4), s1(5)
                fill(U_N1A, V_MIX, 0, (2, 3))
                s2(4), s1(6), s2(5), scale(4, 8), s1(7), s2(6), scale(5, 8), s2(7), scale(6, 8), scale(7, 8)

            ffn(S_FFN1, U_FFN1, G_FFN1, O_FFN1, V_FFN1, ffn1_last)

            def head(h, first):
                u0 = U_HEAD + 16 * h
                un = U_HEAD // 2 + 8 * h
                g0 = G_HEAD + 16 * h

                def ahead(j, nblk=2):
                    s = S_HEAD + j + 1
                    used = u0 + 2 * j
                    if first and j == J_OG0:
                        used = U_LR2 + 1
                    hi(s % 2, full(s, 4 * h), used, nblk)

                def to_tmp(j, half, turn, gated):
                    act.wait_ge(unit_done, head_unit(h, j, half) + 1)
                    if turn < 2:
                        act.wait_ge(gate_stored[half], 32 * h)
                    else:
                        act.wait_ge(pool_mul, 8 * h + turn - 1)
                    A(tmp[:, half, 0, :], PU[:, half, gated, :], ACT.Sigmoid)
                    A(tmp[:, half, 1, :], PU[:, half, 0, :], ACT.Copy).then_inc(unit_free[half], 1)

                def exps(first, last):
                    for m in range(first, last):
                        act.wait_ge(d_ready, 8 * h + m + 1)
                        A(R[:, m % 3, :], R[:, m % 3, :], ACT.Exp, scale=1.0 / 16).then_inc(e_ready, 1)

                if first:
                    to_tmp(J_OG0, 0, 0, 0)
                    act.wait_ge(unit_done, U_X + 2)
                    A(glrT[:, 0:HALF], PU[0:RANK, 1, 0, :], ACT.Copy).then_inc(unit_free[1], 1)
                    fill(U_N1B, V_MIX, 1)
                    act.wait_ge(unit_done, U_LR2 + 1)
                    A(glrT[:, HALF:SEQ], PU[0:RANK, 0, 0, :], ACT.Copy).then_inc(unit_free[0], 1)
                ahead(J_OG0, 1)
                if first:
                    to_tmp(J_OG0, 1, 1, 0)
                A(st[:, 28:29], cols[:, ds(V_BG + h, 1)], ACT.Copy).then_inc(lg_act, 1)
                act.wait_ge(lg_act, 4 * h + 1)
                act.wait_ge(g_done, g0 + H_LG + 1)
                A(R[:, 0, :], PG[:, 0, :], ACT.Abs, bias=st[:, 28:29]).then_inc(lg_act, 1)
                act.wait_ge(lg_act, 4 * h + 2)
                A(R[:, 0, :], R[:, 0, :], ACT.Exp, scale=-1.0).then_inc(lg_act, 1)
                act.wait_ge(lg_act, 4 * h + 3)
                A(R[:, 0, :], R[:, 0, :], ACT.Ln, bias=1.0).then_inc(lg_act, 1)
                if not first:
                    for half in range(2):
                        to_tmp(J_OG0, half, half, 0)
                ahead(J_OG1)
                for half in range(2):
                    to_tmp(J_OG1, half, 2 + half, 0)
                ahead(J_QK)
                for half in range(2):
                    tok = slice(half * HALF, (half + 1) * HALF)
                    act.wait_ge(unit_done, u0 + 2 * J_QK + half + 1)
                    A(q_sb[:, tok], PU[:, half, 0, :], ACT.Copy, scale=DK ** -0.5)
                    A(k_sb[:, tok], PU[:, half, 1, :], ACT.Copy).then_inc(unit_free[half], 1)
                exps(0, 3)
                A(qb[:, :], b_sb[:, :], ACT.Exp, scale=1.0 / 16).then_inc(qb_exp, 1)
                A(el[:, :], b_sb[:, P - 1:SEQ:P], ACT.Exp, scale=1.0 / 16).then_inc(el_ready, 1)
                ahead(J_V)
                for half in range(2):
                    act.wait_ge(unit_done, u0 + 2 * J_V + half + 1)
                    A(v_sb[:, 4 * half:4 * half + 4, :], PU[:, half, :, :].rearrange("p a (b n) -> p (a b) n", b=2),
                      ACT.Copy).then_inc(unit_free[half], 1)
                act.wait_ge(g_done, g0 + H_KT + 1)
                A(kdT[:, :], PG[:, 1, :], ACT.Copy).then_inc(g_free[1], 1)
                exps(3, 6)
                ahead(J_CA)
                to_tmp(J_CA, 0, 4, 1)
                exps(6, 8)
                to_tmp(J_CA, 1, 5, 1)
                ahead(J_CB)
                for half in range(2):
                    to_tmp(J_CB, half, 6 + half, 1)
                for half in range(2):
                    act.wait_ge(g_done, g0 + H_O + half + 1)
                    for c in range(4):
                        act.wait_ge(o_sq, 8 * h + 4 * half + c)
                        A(junk_o[:, :], PG[:, half, c * DV:(c + 1) * DV], ACT.Square,
                          accum_out=st[:, 4 * half + c:4 * half + c + 1]).then_inc(o_sq, 1)
                    act.wait_ge(o_rs, 2 * h + half + 1)
                    for c in range(4):
                        last = A(ON[:, 4 * half + c, :], PG[:, half, c * DV:(c + 1) * DV], ACT.Copy,
                                 scale=st[:, 20 + 4 * half + c:21 + 4 * half + c])
                    last.then_inc(g_free[half], 1)
                ahead(J_G0)
                for k, j in ((0, J_G0), (1, J_G1)):
                    for half in range(2):
                        act.wait_ge(unit_done, u0 + 2 * j + half + 1)
                        if k == 0:
                            act.wait_ge(pool_mul, 8 * h + 7 + half)
                        else:
                            act.wait_ge(gate_stored[half], 32 * h + 16)
                        A(tmp[:, half, :, :], PU[:, half, :, :], ACT.Sigmoid).then_inc(unit_free[half], 1)
                        act.wait_ge(unit_free[half], un + j + 1)
                        act.dma_start(gate_d[:, ds(2 * h + k, 1), :, half * HALF:(half + 1) * HALF]
                                      .rearrange("a f p t -> p (a f) t"), tmp[:, half, :, :]).then_inc(gate_stored[half], 16)
                    if k == 0:
                        ahead(J_G1)

            head(0, True)
            with act.Fori(1, HEADS) as h:
                head(h, False)

            for half in range(2):
                act.wait_ge(unit_done, U_GP - 1 + half)
                for k in GP_KS:
                    if k >= KT - 2:
                        act.wait_ge(g_free[k % 2], G_LN // 2)
                        src = og[:, k % 2, half * HALF:(half + 1) * HALF]
                    else:
                        act.wait_ge(ot_full, 16 * (KT - 2))
                        src = OTF[:, k, half * HALF:(half + 1) * HALF]
                    A(XH[:, k, half * HALF:(half + 1) * HALF], src, ACT.Copy).then_inc(xt_hi, 1)

            def gp_ahead(e):
                s = S_GP + e + 1
                hi(s % 2, full(s, 0), U_GP + 2 * e)

            def store_m(e, half):
                act.wait_ge(unit_free[half], U_GP // 2 + e + 1)
                act.dma_start(m_d[2 * e:2 * e + 2, :, half * HALF:(half + 1) * HALF].rearrange("a p t -> p a t"),
                              mt[:, half, :, :]).then_inc(m_stored[half], 16)

            gp_ahead(0)
            store_m(0, 0)
            store_m(0, 1)
            gp_ahead(1)
            for k in range(KT):
                if k < KT - 1:
                    act.wait_ge(centred, k + 1)
                else:
                    for p in range(2):
                        act.wait_ge(g_free[p], G_LN // 2 + 1)
                if k == 0:
                    A(vr[:, :, :].rearrange("p a n -> p (a n)"), CB[:, CPLACE[0], :], ACT.Square).then_inc(sq_ready, 1)
                    continue
                if k >= 3:
                    act.wait_ge(sq_sum, k - 2)
                A(sq[:, k % 2, :], CB[:, CPLACE[k], :], ACT.Square).then_inc(sq_ready, 1)
            for half in range(2):
                store_m(1, half)
            gp_ahead(2)
            store_m(2, 0)
            for k in range(KT):
                if k < KT - 1:
                    act.wait_ge(scaled, k + 1)
                else:
                    act.wait_ge(g_free[1], G_LN // 2 + 2)
                c = CB[:, CPLACE[k], :]
                A(c, c, ACT.Silu, scale=cols[:, V_LG + k:V_LG + k + 1],
                  bias=cols[:, V_LB + k:V_LB + k + 1]).then_inc(c_act, 1)
            store_m(2, 1)
            gp_ahead(3)
            for half in range(2):
                act.wait_ge(unit_done, U_CP - 1 + half)
                for k in range(KT):
                    act.wait_ge(c_act, k + 1)
                    A(XH[:, k, half * HALF:(half + 1) * HALF], CB[:, CPLACE[k], half * HALF:(half + 1) * HALF],
                      ACT.Copy).then_inc(xt_hi, 1)
                store_m(3, half)

            for i in range(4):
                s = S_CP + i + 1
                hi(s % 2, full(s, 0), U_CP + 2 * i)
                for r in range(2):
                    ohi(i, r, O_CP, G_CP)
                for half in range(2):
                    act.wait_ge(mm_t, 2 * i + half + 1)
                    A(H[:, :, 0, half * HALF:(half + 1) * HALF], hf[:, :, :], ACT.Copy).then_inc(h_hi, 1)
            hi((S_FFN2 + 1) % 2, full(S_FFN2 + 1, 0), U_CP + 8)

            def s1(t):
                square1(t, 8, G_CP // 2 + 12 + t // 2 + 1, junk_s)

            def s2(t):
                square2(t, 16, junk_s)

            def sc(t):
                scale(t, 16)

            s1(0), s1(1), s2(0), s1(2), s2(1), s1(3), s2(2), s1(4), s2(3)
            sc(0), s1(5), sc(1), s2(4), sc(2), s1(6), sc(3), s2(5), s1(7)
            fill(U_N2A, V_FFN2, 0)
            s2(6), sc(4), s2(7), sc(5), sc(6), sc(7)

            def ffn2_last(i, ahead, g):
                for t in range(4):
                    square1(t, 16, g + t // 2 + 1, junk_w)
                evacuate(i, 2, U_FFN2)
                evacuate(i, 3, U_FFN2)
                for t in range(4, 8):
                    square1(t, 16, g + t // 2 + 1, junk_w)

            ffn(S_FFN2, U_FFN2, G_FFN2, O_FFN2, V_FFN2, ffn2_last)

        @block.vector
        def _(dve):
            TT_, STT, TS = dve.tensor_tensor, dve.scalar_tensor_tensor, dve.tensor_scalar

            def post(t, q0, factor, gbs):
                f = FACC[:, t * D:(t + 1) * D]
                dve.wait_ge(rs1, q0 + t + 1)
                dve.wait_ge(gb_full, 16 * gbs)
                STT(f, f, st[:, 4 + t % 4:5 + t % 4], gB[:, :], ALU.mult, ALU.mult).then_inc(post_a, 1)
                dve.wait_ge(post_a, q0 + t + 1)
                dve.wait_ge(x_full[t % 2], 16 * (q0 // 2 + t // 2 + 1))
                STT(f, f, factor, xt[:, t % 2, :], ALU.mult, ALU.add).then_inc(x_new, 1)

            def fill(gain, half, hi0, fps=range(4)):
                for fp in fps:
                    for fi in range(2):
                        f = 2 * fp + fi
                        dve.wait_ge(xt_hi, hi0 + 8 * half + f + 1)
                        last = STT(XL[:, f, half * HALF:(half + 1) * HALF], PU[:, fp % 2, fi, :],
                                   cols[:, gain + f:gain + f + 1], XH[:, f, half * HALF:(half + 1) * HALF],
                                   ALU.mult, ALU.subtract)
                    last.then_inc(unit_free[fp % 2], 1)

            def add_out(t, n, first=False):
                f = FACC[:, t * D:(t + 1) * D]
                dve.wait_ge(g_done, n)
                if first:
                    dve.tensor_copy(f, PG[:, t % 2, :]).then_inc(g_free[t % 2], 1)
                else:
                    TT_(f, PG[:, t % 2, :], f, ALU.add).then_inc(g_free[t % 2], 1)

            def hidden(i, idx, u0, hu0):
                p, a, half = idx % 2, idx % 2, idx // 2
                sg0 = hu0 - 8 * (hu0 > HU_CP)
                dve.wait_ge(sg_ready, sg0 + 4 * i + idx + 1)
                TT_(hf[:, p, :], PU[:, p, 1, :], sgt[:, p, :], ALU.mult).then_inc(unit_free[p], 1)
                dve.wait_ge(h_hi, hu0 + 4 * i + idx + 1)
                tok = slice(half * HALF, (half + 1) * HALF)
                TT_(H[:, a, 1, tok], hf[:, p, :], H[:, a, 0, tok], ALU.subtract).then_inc(h_lo, 1)

            def ffn(u0, g0, hu0, gain, hi0, last_turn):
                for idx in (0, 1):
                    hidden(0, idx, u0, hu0)
                for fp in (0, 2):
                    fill(gain, 1, hi0, (fp, fp + 1))
                    for t in (fp, fp + 1):
                        add_out(t, g0 + t + 1, True)
                for idx in (2, 3):
                    hidden(0, idx, u0, hu0)
                for t in range(4, 8):
                    add_out(t, g0 + t + 1, True)
                with dve.Fori(1, FPAIRS - 1) as i:
                    for half in range(2):
                        for idx in (2 * half, 2 * half + 1):
                            hidden(i, idx, u0, hu0)
                        for t in range(4 * half, 4 * half + 4):
                            add_out(t, g0 + 8 * i + t + 1)
                i = FPAIRS - 1
                for idx in (0, 1):
                    hidden(i, idx, u0, hu0)
                last_turn(i, lambda t: add_out(t, g0 + 8 * i + t + 1))

            dve.wait_ge(cols_ps, 1)
            dve.tensor_copy(cols[:, 0:VROWS], PG[:, 0, 0:VROWS]).then_inc(cols_ready, 1)
            dve.tensor_copy(cw[:, :], PG[:, 0, 512:512 + 8 * TAPS]).then_inc(cols_ready, 1)
            dve.wait_ge(cols_ready, 2)
            fill(V_FFN1, 0, 0)
            dve.wait_ge(mask_in, 16)
            dve.tensor_copy(masks[:, :, :], mask_rows[:, :, :]).then_inc(cols_ready, 1)

            def ffn1_last(i, add):
                def ps(t):
                    post(t, 0, 0.5, 1)

                add(0), add(1), ps(0), add(2), ps(1), add(3), ps(2), ps(3)
                for idx in (2, 3):
                    hidden(i, idx, U_FFN1, HU_FFN1)
                fill(V_MIX, 0, 16, (0, 1))
                add(4), add(5)
                fill(V_MIX, 0, 16, (2, 3))
                ps(4), add(6), ps(5), add(7), ps(6), ps(7)

            ffn(U_FFN1, G_FFN1, HU_FFN1, V_FFN1, 0, ffn1_last)
            dve.wait_ge(const_set, 3)
            dve.wait_ge(cols_ready, 3)
            dve.memset(A_sb[:, :, :], 0.0).then_inc(gla_zero, 1)
            for a in range(2):
                dve.memset(ub[:, a, 0:TAPS - 1], 0.0).then_inc(conv_free, 1)
            fill(V_MIX, 1, 16)
            dve.memset(S_sb[:, 0, :], 0.0).then_inc(gla_zero, 1)

            bc = b_sb[:, :].rearrange("p (c n) -> p c n", n=P)

            with dve.Fori(0, HEADS) as h:
                g0 = G_HEAD + 16 * h
                gf = G_HEAD // 2 + 8 * h
                un = U_HEAD // 2 + 8 * h

                def minus(m):
                    r = R[:, m % 3, :]
                    if m == 0:
                        TT_(r.rearrange("p (c n) -> p c n", n=P), bc[:, :, P - 1:P].to_broadcast([P, TT, P]), bc,
                            ALU.subtract).then_inc(d_ready, 1)
                        return
                    n = 1 << (m - 1)
                    bv = b_sb[:, :].rearrange("p (c s n) -> p c s n", s=2, n=n)
                    rv = r.rearrange("p (c s n) -> p c s n", s=2, n=n)
                    mid = bv[:, :, 0, n - 1:n].to_broadcast([P, SEQ // (2 * n), n])
                    TT_(rv[:, :, 1, :], bv[:, :, 1, :], mid, ALU.subtract)
                    TT_(rv[:, :, 0, :], mid, bv[:, :, 0, :], ALU.subtract).then_inc(d_ready, 1)

                def times(m):
                    dve.wait_ge(e_ready, 8 * h + m + 1)
                    r = R[:, m % 3, :]
                    if m == 0:
                        TT_(r, r, k_sb[:, :], ALU.mult).then_inc(t_ready, 1)
                        return
                    n = 1 << (m - 1)
                    rv, qv, kv = [y.rearrange("p (c s n) -> p c s n", s=2, n=n) for y in (r, q_sb[:, :], k_sb[:, :])]
                    TT_(rv[:, :, 1, :], rv[:, :, 1, :], qv[:, :, 1, :], ALU.mult)
                    TT_(rv[:, :, 0, :], rv[:, :, 0, :], kv[:, :, 0, :], ALU.mult).then_inc(t_ready, 1)

                def select(lv):
                    dve.wait_ge(gla_zero, 2)
                    if lv:
                        dve.wait_ge(g_free[(lv - 1) % 2], gf + (H_LV + lv - 1) // 2 + 1)
                    dve.wait_ge(g_done, g0 + H_LV + lv + 1)
                    dve.nop(nofuse=True)
                    dve.copy_predicated(A_sb[:, :, :], masks[:, lv:lv + 1, :].to_broadcast([P, TT, P]),
                                        PG[:, lv % 2, :].rearrange("p (c n) -> p c n", n=P)).then_inc(g_free[lv % 2], 1)

                dve.wait_ge(g_done, g0 + H_LG + 1)
                dve.wait_ge(lg_act, 4 * h + 2)
                TS(R[:, 1, :], PG[:, 0, :], cols[:, ds(V_BG + h, 1)], 0.0, ALU.add, ALU.min).then_inc(g_free[0], 1)
                dve.wait_ge(g_free[0], gf + 1)
                dve.wait_ge(lg_act, 4 * h + 4)
                TT_(R[:, 1, :], R[:, 1, :], R[:, 0, :], ALU.subtract).then_inc(la_done, 1)
                dve.wait_ge(la_done, h + 1)
                for c in range(TT):
                    tok = slice(c * P, (c + 1) * P)
                    last = dve.tensor_tensor_scan(b_sb[:, tok], one_c[:, 0:1].to_broadcast([P, P]), R[:, 1, tok], 0.0,
                                                  ALU.mult, ALU.add)
                last.then_inc(b_done, 1)
                dve.wait_ge(b_done, h + 1)
                for m in range(3):
                    minus(m)
                for half in range(2):
                    dve.wait_ge(unit_free[half], un + J_QK + 1)
                for m in range(3):
                    times(m)
                dve.wait_ge(qb_exp, h + 1)
                TT_(qb[:, :], qb[:, :], q_sb[:, :], ALU.mult).then_inc(qb_ready, 1)
                dve.wait_ge(g_done, g0 + H_KT + 1)
                minus(3)
                select(0)
                minus(4)
                select(1)
                minus(5)
                for m in (3, 4, 5):
                    times(m)
                select(2)
                minus(6)
                select(3)
                minus(7)
                select(4)
                times(6)
                times(7)
                select(5)
                select(6)
                select(7)
                dve.wait_ge(el_ready, h + 1)
                n = 0
                for c in range(TT - 1):
                    if c in (0, 4):
                        dve.wait_ge(g_done, g0 + H_ST + c // 4 + 1)
                    if c == 4:
                        dve.wait_ge(g_free[0], gf + 6)
                    elif c:
                        dve.wait_ge(state_step, 5 * h + n)
                    op = STT(S_sb[:, c + 1, :], S_sb[:, c, :], el[:, c:c + 1], PG[:, c // 4, (c % 4) * DV:(c % 4 + 1) * DV],
                             ALU.mult, ALU.add)
                    if c in (3, 6):
                        op.then_inc(g_free[c // 4], 1)
                    else:
                        op.then_inc(state_step, 1)
                        n += 1

                def conv(a):
                    dve.wait_ge(pool_mul, 8 * h + 6 + 2 * a)
                    dve.wait_ge(c_stored[a], 16 * h)
                    per = 2 * TAPS - 1
                    for w in range(TAPS):
                        for half in range(2):
                            n = 2 * w + half
                            o = acc[:, a, half * HALF:(half + 1) * HALF]
                            src = ub[:, a, half * HALF + w:half * HALF + w + HALF]
                            tap = cw[:, ds(8 * w + a + 2 * h, 1)]
                            if w == 0:
                                op = TS(o, src, tap, cols[:, ds(V_CB + a + 2 * h, 1)], ALU.mult, ALU.add)
                            else:
                                dve.wait_ge(conv_step, per * (2 * h + a) + n - 1)
                                op = STT(o, src, tap, o, ALU.mult, ALU.add)
                            op.then_inc(conv_step if n < per else conv_free, 1)

                conv(0)
                for d in range(2):
                    dve.wait_ge(g_done, g0 + H_OT + d + 1)
                    dve.wait_ge(pool_mul, 8 * h + 4)
                    STT(og[:, d, :], PG[:, d, :], cols[:, V_GN + d:V_GN + d + 1], og[:, d, :], ALU.mult, ALU.mult)\
                        .then_inc(g_free[d], 1)
                conv(1)

            for n, k in enumerate(GP_KS):
                tok = slice(HALF, SEQ)
                dve.wait_ge(xt_hi, 40 + n + 1)
                src = og[:, k % 2, tok] if k >= KT - 2 else OTF[:, k, tok]
                TT_(XL[:, k, tok], src, XH[:, k, tok], ALU.subtract).then_inc(ot_lo1, 1)

            def gated(e, half):
                dve.wait_ge(unit_done, U_GP + 2 * e + half + 1)
                dve.wait_ge(gt_full[half], 16 * (e + 1))
                if e:
                    dve.wait_ge(m_stored[half], 16 * e)
                TT_(mt[:, half, :, :], PU[:, half, :, :], gt[:, half, :, :], ALU.mult).then_inc(unit_free[half], 1)

            vrf = vr[:, :, :].rearrange("p a n -> p (a n)")

            def c_tile(k):
                return CB[:, CPLACE[k], :]

            def channel_sum(k):
                dve.wait_ge(c_early, 16 * (KT - 2))
                if k >= KT - 2:
                    dve.wait_ge(c_late, 32)
                if k == 1:
                    TT_(vrf, c_tile(0), c_tile(1), ALU.add).then_inc(c_sum, 1)
                else:
                    dve.wait_ge(c_sum, k - 1)
                    TT_(vrf, vrf, c_tile(k), ALU.add).then_inc(c_sum, 1)

            dve.wait_ge(gate_stored[1], 32 * HEADS)
            for k in range(1, KT - 2):
                channel_sum(k)
            gated(0, 0)
            for k in (KT - 2, KT - 1):
                channel_sum(k)
            gated(0, 1)
            def square_sum(k):
                dve.wait_ge(sq_ready, k + 1)
                if k > 1:
                    dve.wait_ge(sq_sum, k - 1)
                TT_(vrf, vrf, sq[:, k % 2, :], ALU.add).then_inc(sq_sum, 1)

            dve.wait_ge(g_done, G_LN + 2)
            for k in range(KT):
                if k < KT - 1:
                    v = c_tile(k).rearrange("p (a n) -> p a n", a=2)
                    TT_(v, v, PG[:, :, 0:512], ALU.subtract).then_inc(centred, 1)
                else:
                    for half in range(2):
                        v = CB[:, CPLACE[k], half * HALF:(half + 1) * HALF]
                        TT_(v, v, PG[:, half, 0:512], ALU.subtract).then_inc(g_free[half], 1)
                if k >= 2:
                    square_sum(k - 1)
            gated(1, 0)
            square_sum(KT - 1)
            dve.wait_ge(g_done, G_LN + 3)
            TS(st[:, 0:TT], PG[:, 0, 0:TT], EPS, None, ALU.add).then_inc(g_free[0], 1)
            gated(1, 1)
            dve.wait_ge(rs_ready, 1)
            for c in range(TT):
                last = TS(vr[:, c // 4, (c % 4) * P:(c % 4 + 1) * P], ident[:, :], st[:, 8 + c:9 + c], float(D),
                          ALU.mult, ALU.mult)
            last.then_inc(diag_ready, 1)
            gated(2, 0)
            dve.wait_ge(g_done, G_LN + 4)
            for k in range(KT):
                TT_(c_tile(k), c_tile(k), PG[:, 1, :], ALU.mult).then_inc(scaled if k < KT - 1 else g_free[1], 1)
            gated(2, 1)
            gated(3, 0)
            for half in range(2):
                for k in range(KT):
                    tok = slice(half * HALF, (half + 1) * HALF)
                    dve.wait_ge(xt_hi, 48 + 8 * half + k + 1)
                    TT_(XL[:, k, tok], CB[:, CPLACE[k], tok], XH[:, k, tok], ALU.subtract).then_inc(ct_lo, 1)
                if half == 0:
                    gated(3, 1)

            def post2(t):
                post(t, 8, 1.0, 2)

            for i in range(4):
                for half in range(2):
                    n = 2 * i + half
                    dve.wait_ge(unit_done, U_CP + n + 1)
                    dve.wait_ge(gt_full[half], 64 + 16 * (i + 1))
                    TT_(gt[:, half, :, :], PU[:, half, :, :], gt[:, half, :, :], ALU.mult).then_inc(unit_free[half], 1)
                    dve.wait_ge(unit_free[half], U_CP // 2 + i + 1)
                    dve.wait_ge(mt_full[half], 16 * (i + 1))
                    TT_(hf[:, :, :], gt[:, half, :, :], mt[:, half, :, :], ALU.add).then_inc(mm_t, 1)
                    dve.wait_ge(h_hi, HU_CP + n + 1)
                    tok = slice(half * HALF, (half + 1) * HALF)
                    TT_(H[:, :, 1, tok], hf[:, :, :], H[:, :, 0, tok], ALU.subtract).then_inc(h_lo, 1)
                for t in range(TT):
                    add_out(t, G_CP + 8 * i + t + 1, i == 0)
                    if i == 3 and t:
                        post2(t - 1)
            fill(V_FFN2, 0, 64)
            post2(7)

            def ffn2_last(i, add):
                def ps(t):
                    post(t, 16, 0.5, 3)

                add(0), add(1), ps(0), add(2), ps(1), add(3), ps(2), ps(3)
                for idx in (2, 3):
                    hidden(i, idx, U_FFN2, HU_FFN2)
                add(4), add(5), ps(4), add(6), ps(5), add(7), ps(6), ps(7)

            ffn(U_FFN2, G_FFN2, HU_FFN2, V_FFN2, 64, ffn2_last)

        @block.gpsimd
        def _(pool):
            PT, PS = pool.tensor_tensor, pool.tensor_scalar

            def lo(s, par, nblk=2):
                pool.wait_ge(w_hi, s + 1)
                c = slice(0, nblk * P)
                PT(w_l[:, par, :, c], w_raw[:, par, :, c], w_h[:, par, :, c], ALU.subtract).then_inc(w_lo, 1)

            def olo(o, a):
                pool.wait_ge(o_hi, o + 1)
                PT(o_l[:, a, :], o_raw[:, a, :], o_h[:, a, :], ALU.subtract).then_inc(o_lo, 1)

            def rstd(src, dst, n, scale, pows, done):
                pool.nop(nofuse=True)
                PS(src, src, scale, EPS, ALU.mult, ALU.add).then_inc(pow_in, 1)
                pool.wait_ge(pow_in, pows)
                PT(dst, src, half_c[:, 0:n], ALU.pow).then_inc(done, 1)

            def rs(kind, t, q0, pows):
                j = t % 4
                if kind == 1:
                    if t >= 4:
                        pool.wait_ge(post_a, q0 + t - 3)
                    pool.wait_ge(sq1, q0 + t + 1)
                    rstd(st[:, j:j + 1], st[:, 4 + j:5 + j], 1, 1.0 / D, pows, rs1)
                else:
                    pool.wait_ge(sq2, q0 + t + 1)
                    rstd(st[:, 12 + j:13 + j], st[:, 20 + j:21 + j], 1, 1.0 / D, pows, rs2)

            def staggered(q0, p0, ts, pows):
                for t in (*ts, None):
                    if t is not None:
                        pows += 1
                        rs(1, t, q0, pows)
                    if t is None or t > ts[0]:
                        pows += 1
                        rs(2, ts[-1] if t is None else t - 1, p0, pows)

            pool.memset(vec_rows[:, :], 0.0).then_inc(rows_zero, 1)
            pool.memset(cw_rows[:, :, :], 0.0).then_inc(rows_zero, 1)
            pool.memset(half_c[:, :], -0.5).then_inc(const_set, 1)
            pool.memset(one_c[:, :], 1.0).then_inc(const_set, 1)
            pool.memset(ones_m[:, :], 1.0 / D).then_inc(const_set, 1)
            pool.wait_ge(const_set, 3)
            for t in range(4):
                rs(2, t, 0, t + 1)
            lo(0, 0)
            lo(1, 1)
            for t in range(4, 8):
                rs(2, t, 0, t + 1)

            def ffn(s0, o0):
                with pool.Fori(0, FPAIRS - 1) as i:
                    for a in range(2):
                        olo(o0 + 2 * i + a, a)
                    for a in range(2):
                        lo(s0 + 2 * i + 2 + a, (s0 + a) % 2)
                for a in range(2):
                    olo(o0 + 2 * (FPAIRS - 1) + a, a)

            ffn(S_FFN1, O_FFN1)
            staggered(0, 8, range(4), 8)
            lo(S_LR, S_LR % 2, 1)
            lo(S_HEAD, S_HEAD % 2, 1)
            staggered(0, 8, range(4, 8), 16)

            with pool.Fori(0, HEADS) as h:
                s0 = S_HEAD + 8 * h
                un = U_HEAD // 2 + 8 * h

                def ahead(j, nblk=2):
                    lo(s0 + j + 1, (S_HEAD + j + 1) % 2, nblk)

                ahead(J_OG0, 1)
                for half in range(2):
                    pool.wait_ge(ot_stored, 16 * h)
                for d, j in ((0, J_OG0), (1, J_OG1)):
                    for half in range(2):
                        pool.wait_ge(unit_free[half], un + j + 1)
                        PT(og[:, d, half * HALF:(half + 1) * HALF], tmp[:, half, 0, :], tmp[:, half, 1, :], ALU.mult)\
                            .then_inc(pool_mul, 1)
                    ahead(j + 1)
                ahead(J_V)
                ahead(J_CA)
                for a, j in ((0, J_CA), (1, J_CB)):
                    pool.wait_ge(conv_free, 2 * h + a + 1)
                    for half in range(2):
                        pool.wait_ge(unit_free[half], un + j + 1)
                        PT(ub[:, a, TAPS - 1 + half * HALF:TAPS - 1 + (half + 1) * HALF], tmp[:, half, 0, :],
                           tmp[:, half, 1, :], ALU.mult).then_inc(pool_mul, 1)
                    if a == 0:
                        ahead(J_CB)
                for half in range(2):
                    pool.wait_ge(o_sq, 8 * h + 4 * half + 4)
                    rstd(st[:, 4 * half:4 * half + 4], st[:, 20 + 4 * half:24 + 4 * half], 4, 1.0 / DV,
                         24 + 2 * h + half + 1, o_rs)
                ahead(J_G0)
                ahead(J_G1)

            for n, k in enumerate(GP_KS):
                tok = slice(0, HALF)
                pool.wait_ge(xt_hi, 32 + n + 1)
                src = og[:, k % 2, tok] if k >= KT - 2 else OTF[:, k, tok]
                PT(XL[:, k, tok], src, XH[:, k, tok], ALU.subtract).then_inc(ot_lo0, 1)
            lo(S_GP + 1, (S_GP + 1) % 2)
            lo(S_GP + 2, (S_GP + 2) % 2)
            pool.wait_ge(g_free[0], G_LN // 2 + 2)
            PT(st[:, 8:8 + TT], st[:, 0:TT], half_c[:, :], ALU.pow).then_inc(rs_ready, 1)
            lo(S_GP + 3, (S_GP + 3) % 2)
            lo(S_CP, S_CP % 2)
            for i in range(4):
                lo(S_CP + i + 1, (S_CP + i + 1) % 2)
                for r in range(2):
                    olo(O_CP + 2 * i + r, r)
            staggered(8, 16, range(8), 32)
            lo(S_FFN2 + 1, (S_FFN2 + 1) % 2)
            ffn(S_FFN2, O_FFN2)
            for t in range(8):
                rs(1, t, 16, 48 + t + 1)


INPUTS = ["x", "ffn1_pre_g", "ffn1_w_in", "ffn1_w_out", "ffn1_post_g", "mix_pre_g", "w_mix_in", "gla_w_gate_up",
          "gla_b_gate", "gla_norm_g", "gla_w_proj", "conv_dw_w", "conv_dw_b", "conv_ln_g", "conv_ln_b",
          "conv_w_proj", "w_mix_out", "mix_post_g", "ffn2_pre_g", "ffn2_w_in", "ffn2_w_out", "ffn2_post_g"]


def kernel(**inputs):
    import numpy as np
    import concourse.bacc as bacc
    from concourse.bass_utils import run_bass_kernel_spmd

    nc = bacc.Bacc("TRN2", target_bir_lowering=False, num_devices=1)
    j, i = np.arange(P)[:, None], np.arange(P)[None, :]
    levels = [(j // (2 * n) == i // (2 * n)) & (j % (2 * n) < n) & (i % (2 * n) >= n) for n in (1 << l for l in range(7))]
    masks = np.stack(levels + [i == j], axis=1).astype(np.float32)
    arrays = {f"in_{n}": np.ascontiguousarray(inputs[n]) for n in INPUTS}
    arrays["c_ident"] = np.eye(P, dtype=np.float32)
    arrays["c_masks"] = np.ascontiguousarray(masks)
    args = [nc.dram_tensor(n, a.shape, mybir.dt.from_np(a.dtype), kind="ExternalInput").ap() for n, a in arrays.items()]
    out = nc.dram_tensor("out_dram", (1, SEQ, D), mybir.dt.float32, kind="ExternalOutput").ap()
    build(nc, *args, out)
    r = run_bass_kernel_spmd(nc, [arrays], core_ids=[0])
    return r.results[0]["out_dram"]
```

```python
import concourse.bass as bass
from concourse import mybir
from contextlib import ExitStack

D, SEQ, DFF = 1024, 1024, 2816
HEADS, DK, DV, RANK = 4, 128, 256, 16
TAPS = 31
EPS = 1e-6
P = 128
KT = D // P
TT = SEQ // P
HALF = SEQ // 2
FPAIRS = DFF // P // 2
C_Q, C_K, C_V = 0, HEADS * DK, 2 * HEADS * DK
C_LR = C_V + HEADS * DV
C_OG = C_LR + RANK
C_UA = C_OG + D
C_UB = C_UA + D
C_GA = C_UB + D
C_GB = C_GA + D
V_FFN1, V_MIX, V_FFN2, V_CB, V_LG, V_LB, V_BG, V_GN = 0, 8, 16, 24, 32, 40, 48, 52
VROWS = 54
S_FFN1 = 0
S_HEAD = S_FFN1 + 2 * FPAIRS
S_GP = S_HEAD + 8 * HEADS
S_CP = S_GP + 4
S_FFN2 = S_CP + 4
S_END = S_FFN2 + 2 * FPAIRS
U_IN0 = 0
U_FFN1 = U_IN0 + 4
U_X = U_FFN1 + 4 * FPAIRS
U_N1B = U_X + 2
U_HEAD = U_N1B + 2
U_GP = U_HEAD + 16 * HEADS
U_CP = U_GP + 8
U_N2A = U_CP + 8
U_FFN2 = U_N2A + 4
G_FFN1 = 0
G_N1A = G_FFN1 + 4 + 16 * FPAIRS - 8
G_HEAD = G_FFN1 + 4 + 16 * FPAIRS + 4
G_LN = G_HEAD + 16 * HEADS
G_CP = G_LN + 4
G_FFN2 = G_CP + 16 * 4
H_LG, H_KT, H_LV, H_DIAG, H_ST, H_O, H_OT = 0, 1, 2, 9, 10, 12, 14
HU_FFN1, HU_CP = 0, 4 * FPAIRS
HU_FFN2 = HU_CP + 8
O_FFN1, O_CP = 0, 2 * FPAIRS
O_FFN2 = O_CP + 8
O_END = O_FFN2 + 2 * FPAIRS
CPLACE = [0, 1, 2, 5, 6, 7, 3, 4]
GP_KS = [6, 7, 0, 1, 2, 3, 4, 5]
CT_KS = [7, 3, 0, 1, 2, 4, 5, 6]
POOL_TILES = (1, 3, 5)
J_OG0, J_OG1, J_QK, J_V, J_CA, J_CB, J_G0, J_G1 = range(8)


def build(nc, x, ffn1_pre_g, ffn1_w_in, ffn1_w_out, ffn1_post_g, mix_pre_g, w_mix_in, gla_w_gate_up,
          gla_b_gate, gla_norm_g, gla_w_proj, conv_dw_w, conv_dw_b, conv_ln_g, conv_ln_b, conv_w_proj,
          w_mix_out, mix_post_g, ffn2_pre_g, ffn2_w_in, ffn2_w_out, ffn2_post_g, ident_c, masks_c, out):
    F32, FR, U8 = mybir.dt.float32, mybir.dt.float32r, mybir.dt.uint8
    ACT, ALU = mybir.ActivationFunctionType, mybir.AluOpType
    ds = bass.ds
    ctx = ExitStack()

    def ktiles(w):
        return w[0, :, :].rearrange("(k p) n -> p k n", p=P)

    w1v, w2v, wmv = ktiles(ffn1_w_in), ktiles(ffn2_w_in), ktiles(w_mix_in)
    wgv, wcv = ktiles(gla_w_proj), ktiles(conv_w_proj)
    o1v, o2v, omv = ktiles(ffn1_w_out), ktiles(ffn2_w_out), ktiles(w_mix_out)
    xv = x[0, :, :].rearrange("(t p) n -> p t n", p=P)
    outv = out[0, :, :].rearrange("(t p) n -> p t n", p=P)

    def scratch(name, shape):
        return nc.dram_tensor(name, shape, F32, kind="Internal").ap()

    x1_d = scratch("x1_d", (P, TT, D))
    x2_d = scratch("x2_d", (P, TT, D))
    gate_d = scratch("gate_d", (2, KT, P, SEQ))
    ot_d = scratch("ot_d", (KT, P, SEQ))
    c_d = scratch("c_d", (KT, P, SEQ))
    m_d = scratch("m_d", (KT, P, SEQ))

    with ctx:
        BASE = -(-nc.sbuf_base // 32) * 32

        def at(name, kb, shape, dt=F32):
            return nc.alloc_sbuf_tensor_at(name, shape, dt, offset=BASE + int(kb * 1024))

        XH = at("XH", 0, [P, KT, SEQ], FR)
        XL = at("XL", 32, [P, KT, SEQ], FR)
        w_raw = at("w_raw", 64, [P, 2, KT, 256])
        w_h = at("w_h", 80, [P, 2, KT, 256], FR)
        w_l = at("w_l", 96, [P, 2, KT, 256], FR)
        FACC = at("FACC", 112, [P, TT * D])
        H = at("H", 144, [P, 2, 2, SEQ], FR)
        vec_rows = at("vec_rows", 184, [P, P])
        cw_rows = at("cw_rows", 185, [P, 2, P])
        mask_rows = at("mask_rows", 186, [P, 8, P])
        o_raw = at("o_raw", 160, [P, 2, D])
        o_h = at("o_h", 168, [P, 2, D], FR)
        o_l = at("o_l", 176, [P, 2, D], FR)
        xt = at("xt", 184, [P, 2, D])
        junk_s, xt_s = at("junk_s", 196, [P, D]), at("xt_s", 200.25, [P, D])
        junk_w, xt_w = at("junk_w", 160, [P, D]), at("xt_w", 164, [P, D])
        gB = at("gB", 192, [P, D])
        sgt = at("sgt", 196, [P, 2, 512])
        hf = at("hf", 200.25, [P, 2, 512])
        glrT = at("glrT", 112, [RANK, SEQ])
        b_sb = at("b_sb", 116, [P, SEQ])
        q_sb = at("q_sb", 120, [P, SEQ])
        k_sb = at("k_sb", 124, [P, SEQ])
        R = at("R", 128, [P, 3, SEQ])
        ON = at("ON", 128, [P, TT, DV])
        qb = at("qb", 140, [P, SEQ])
        kdT = at("kdT", 144, [P, SEQ])
        v_sb = at("v_sb", 148, [P, TT, DV])
        og = at("og", 156, [P, 2, SEQ])
        S_sb = at("S_sb", 164, [P, TT, DV])
        A_sb = at("A_sb", 172, [P, TT, P])
        ub = at("ub", 176, [P, 2, SEQ + TAPS - 1])
        acc = at("acc", 184.25, [P, 2, SEQ])
        tmp = at("tmp", 192.25, [P, 2, 2, 512])
        wgu = at("wgu", 200.5, [RANK, P])
        junk_o = at("junk_o", 202.5, [P, DV])
        CB = at("CB", 144, [P, KT, SEQ])
        OTF = at("OTF", 112, [P, KT - 2, SEQ])
        sq = at("sq", 176, [P, 2, SEQ])
        gt = at("gt", 184, [P, 2, 2, 512])
        mt = at("mt", 192.25, [P, 2, 2, 512])
        vr = at("vr", 200.25, [P, 2, 512])
        ident = at("ident", 204.25, [P, P])
        masks = at("masks", 204.75, [P, 8, P], U8)
        cw = at("cw", 205.75, [P, 8 * TAPS])
        cols = at("cols", 206.75, [P, 64])
        el = at("el", 207, [P, TT])
        st = at("st", 207.0625, [P, 32])
        half_c = at("half_c", 207.1875, [P, 8])
        one_c = at("one_c", 207.25, [P, 1])
        ones_m = at("ones_m", 207.3125, [P, P])

        PU = nc.alloc_psum_tensor("PU", [P, 2, 2, 512], F32)
        PG = nc.alloc_psum_tensor("PG", [P, 2, 1024], F32)

        def sem(name):
            return ctx.enter_context(nc.semaphore(name))

        raw_full = [sem("raw_full0"), sem("raw_full1")]
        w_hi, w_lo = sem("w_hi"), sem("w_lo")
        o_full = [sem("o_full0"), sem("o_full1")]
        o_hi, o_lo = sem("o_hi"), sem("o_lo")
        unit_done = sem("unit_done")
        unit_free = [sem("unit_free0"), sem("unit_free1")]
        g_done = sem("g_done")
        g_free = [sem("g_free0"), sem("g_free1")]
        sg_ready, h_hi, h_lo = sem("sg_ready"), sem("h_hi"), sem("h_lo")
        ident_in, mask_in, const_set, rows_in, rows_zero, cols_ps, cols_ready = [sem(n) for n in (
            "ident_in", "mask_in", "const_set", "rows_in", "rows_zero", "cols_ps", "cols_ready")]
        x_in = [sem(f"x_in{t}") for t in range(TT)]
        x_full = [sem(f"x_full{b}") for b in range(3)]
        gb_full, sq1, rs1, post_a, x_new = [sem(n) for n in ("gb_full", "sq1", "rs1", "post_a", "x_new")]
        pre_mul, gain_in = sem("pre_mul"), sem("gain_in")
        x_stored = [sem(f"x_stored{t}") for t in range(TT)]
        sq2, rs2, xn_ready, xt_hi, pow_in = [sem(n) for n in ("sq2", "rs2", "xn_ready", "xt_hi", "pow_in")]
        wgu_full, lg_act, la_done, b_done, d_ready, e_ready, t_ready = [sem(n) for n in (
            "wgu_full", "lg_act", "la_done", "b_done", "d_ready", "e_ready", "t_ready")]
        qb_exp, qb_ready, el_ready, state_step, gla_zero = [sem(n) for n in (
            "qb_exp", "qb_ready", "el_ready", "state_step", "gla_zero")]
        o_sq, o_rs, pool_mul, conv_step, conv_free, ot_stored = [sem(n) for n in (
            "o_sq", "o_rs", "pool_mul", "conv_step", "conv_free", "ot_stored")]
        gate_stored = [sem("gate_stored0"), sem("gate_stored1")]
        c_stored = [sem("c_stored0"), sem("c_stored1")]
        ot_full, ot_lo, ct_lo, c_early, c_late, c_sum = [sem(n) for n in (
            "ot_full", "ot_lo", "ct_lo", "c_early", "c_late", "c_sum")]
        m_ready, centred, sq_ready, sq_sum, rs_ready, diag_ready, scaled, c_act, mm_t = [sem(n) for n in (
            "m_ready", "centred", "sq_ready", "sq_sum", "rs_ready", "diag_ready", "scaled", "c_act", "mm_t")]
        gt_full = [sem("gt_full0"), sem("gt_full1")]
        mt_full = [sem("mt_full0"), sem("mt_full1")]
        m_stored = [sem("m_stored0"), sem("m_stored1")]
        out_stored = sem("out_stored")

        block = ctx.enter_context(nc.Block())

        @block.sync
        def _(sp):
            def raw(s, par, parts):
                if isinstance(s, int):
                    if s >= 2:
                        sp.wait_ge(w_lo, s - 1)
                else:
                    sp.wait_ge(w_lo, s - 1)
                for dst, src in parts:
                    sp.dma_start(dst, src).then_inc(raw_full[par], 16)

            def two_blocks(s, par, va, ca, vb, cb):
                raw(s, par, [(w_raw[:, par, :, 0:P], va[:, :, ds(ca, P)]),
                             (w_raw[:, par, :, P:2 * P], vb[:, :, ds(cb, P)])])

            def one_block(s, par, va, ca):
                raw(s, par, [(w_raw[:, par, 0:4, 0:P], va[:, 0:4, ds(ca, P)]),
                             (w_raw[:, par, 4:8, 0:P], va[:, 4:8, ds(ca, P)])])

            def wide(s, par, va, ca):
                raw(s, par, [(w_raw[:, par, 0:4, :], va[:, 0:4, ds(ca, 2 * P)]),
                             (w_raw[:, par, 4:8, :], va[:, 4:8, ds(ca, 2 * P)])])

            def oraw(o, r, v, row):
                if not (isinstance(o, int) and o < 2):
                    sp.wait_ge(o_lo, o - 1)
                sp.dma_start(o_raw[:, r:r + 1, :], v[:, ds(row, 1), :]).then_inc(o_full[r], 16)

            def norm(q0, src, dst, done, second, last):
                third = xt_s if q0 == 8 else xt_w

                def load(t):
                    buf = third[:, :] if t % 3 == 2 else xt[:, t % 3, :]
                    sp.dma_start(buf, src[:, t, :]).then_inc(x_full[t % 3], 16)

                load(0)
                if second:
                    sp.wait_ge(*second)
                load(1)
                sp.wait_ge(*last)
                load(2)
                for t in range(TT):
                    sp.wait_ge(x_new, q0 + t + 1)
                    sp.dma_start(dst[:, t, :], FACC[:, t * D:(t + 1) * D]).then_inc(done[t], 16)
                    if t + 3 < TT:
                        load(t + 3)

            def load_x(tiles):
                for t in tiles:
                    sp.dma_start(FACC[:, t * D:(t + 1) * D], xv[:, t, :]).then_inc(x_in[t], 16)

            def load_rows(row, vec, n, done):
                sp.dma_start(vec_rows[row:row + n, :], vec[0, :].rearrange("(r c) -> r c", c=P)).then_inc(done, 16)

            load_x(range(1))
            sp.dma_start(ident[:, :], ident_c).then_inc(ident_in, 16)
            load_x(range(1, 3))
            sp.wait_ge(rows_zero, 2)
            load_rows(V_FFN1, ffn1_pre_g, 8, gain_in)
            load_x(range(3, 4))
            two_blocks(S_FFN1, 0, w1v, 0, w1v, DFF)
            for row, vec, n in ((V_MIX, mix_pre_g, 8), (V_FFN2, ffn2_pre_g, 8),
                                (V_CB, conv_dw_b, 8), (V_LG, conv_ln_g, 8), (V_LB, conv_ln_b, 8),
                                (V_BG, gla_b_gate, 4), (V_GN, gla_norm_g, 2)):
                load_rows(row, vec, n, rows_in)
            cwv = conv_dw_w[0, :, :].rearrange("w (c n) -> (w c) n", n=P)
            sp.dma_start(cw_rows[:, 0, :], cwv[0:P, :]).then_inc(rows_in, 16)
            sp.dma_start(cw_rows[0:8 * TAPS - P, 1, :], cwv[P:8 * TAPS, :]).then_inc(rows_in, 16)
            two_blocks(S_FFN1 + 1, 1, w1v, P, w1v, DFF + P)
            load_x(range(4, TT))
            sp.dma_start(mask_rows[:, :, :], masks_c).then_inc(mask_in, 16)

            def ffn(s0, o0, wv, ov):
                with sp.Fori(1, FPAIRS) as i:
                    for a in range(2):
                        two_blocks(s0 + 2 * i + a, (s0 + a) % 2, wv, (2 * i + a) * P, wv, DFF + (2 * i + a) * P)
                    for a in range(2):
                        oraw(o0 + 2 * i + a, a, ov, 2 * i + a)

            for a in range(2):
                oraw(O_FFN1 + a, a, o1v, a)
            ffn(S_FFN1, O_FFN1, w1v, o1v)
            two_blocks(S_HEAD, S_HEAD % 2, wmv, C_LR, wmv, C_OG)
            one_block(S_HEAD + 1, (S_HEAD + 1) % 2, wmv, C_OG + P)
            sp.dma_start(gB[:, :], ffn1_post_g[0, :].partition_broadcast(P)).then_inc(gb_full, 16)
            sp.wait_ge(cols_ready, 4)
            norm(0, xv, x1_d, x_stored, None, (o_lo, O_CP))

            def head(h, first):
                s = S_HEAD + 8 * h
                par = [(S_HEAD + j) % 2 for j in range(8)]
                if not first:
                    one_block(s + J_OG0, par[J_OG0], wmv, C_OG + h * DV)
                    one_block(s + J_OG1, par[J_OG1], wmv, C_OG + h * DV + P)
                else:
                    two_blocks(s + J_QK, par[J_QK], wmv, C_Q + h * DK, wmv, C_K + h * DK)
                if first:
                    sp.wait_ge(unit_done, U_N1B + 4)
                else:
                    sp.wait_ge(g_done, G_HEAD + 16 * h - 15)
                sp.dma_start(wgu[:, :], gla_w_gate_up[0, :, ds(h * DK, DK)]).then_inc(wgu_full, 16)
                if not first:
                    two_blocks(s + J_QK, par[J_QK], wmv, C_Q + h * DK, wmv, C_K + h * DK)
                    store_ot(h - 1)
                wide(s + J_V, par[J_V], wmv, C_V + h * DV)
                if not first:
                    store_c(h - 1)
                for a, j in ((0, J_CA), (1, J_CB)):
                    two_blocks(s + j, par[j], wmv, C_UA + (2 * h + a) * P, wmv, C_UB + (2 * h + a) * P)
                for a, j in ((0, J_G0), (1, J_G1)):
                    two_blocks(s + j, par[j], wmv, C_GA + (2 * h + a) * P, wmv, C_GB + (2 * h + a) * P)

            def store_ot(h):
                for p in range(2):
                    sp.wait_ge(g_free[p], G_HEAD // 2 + 8 * h + 8)
                sp.dma_start(ot_d[ds(2 * h, 2), :, :].rearrange("a p t -> p a t"), og[:, :, :]).then_inc(ot_stored, 16)

            def store_c(h):
                for a in range(2):
                    sp.wait_ge(conv_free, 2 + 2 * h + a + 1)
                    sp.dma_start(c_d[ds(2 * h + a, 1), :, :].rearrange("a p t -> p a t"),
                                 acc[:, a:a + 1, :]).then_inc(c_stored[a], 16)

            head(0, True)
            with sp.Fori(1, HEADS) as h:
                head(h, False)
            wide(S_GP, S_GP % 2, wgv, 0)
            wide(S_GP + 1, (S_GP + 1) % 2, wgv, 2 * P)
            sp.wait_ge(g_done, G_LN)
            sp.wait_ge(ot_stored, 16 * (HEADS - 1))
            for k in range(KT - 2):
                sp.dma_start(OTF[:, k, :], ot_d[k, :, :]).then_inc(ot_full, 16)
            for a in range(2):
                sp.wait_ge(c_stored[a], 16 * (HEADS - 1))
            for k in range(KT - 2):
                sp.dma_start(CB[:, CPLACE[k], :], c_d[k, :, :]).then_inc(c_early, 16)
            wide(S_GP + 2, S_GP % 2, wgv, 4 * P)
            store_c(HEADS - 1)
            wide(S_GP + 3, (S_GP + 1) % 2, wgv, 6 * P)
            for a in range(2):
                sp.wait_ge(c_stored[a], 16 * HEADS)
                sp.wait_ge(gate_stored[a], 32 * HEADS)

            def gates(n, which):
                f, half = n // 2 * 2, n % 2
                sp.dma_start(gt[:, n % 2, :, :],
                             gate_d[which, f:f + 2, :, half * HALF:(half + 1) * HALF].rearrange("a p t -> p a t"))\
                    .then_inc(gt_full[n % 2], 16)

            for n in range(8):
                if 2 <= n < 4:
                    sp.wait_ge(m_ready, n - 1)
                elif n >= 4:
                    sp.wait_ge(unit_free[n % 2], U_GP // 2 + n // 2)
                gates(n, 0)
                if n == 1:
                    sp.wait_ge(ot_lo, KT + 2)
                    for k in (KT - 2, KT - 1):
                        sp.dma_start(CB[:, CPLACE[k], :], c_d[k, :, :]).then_inc(c_late, 16)
                if n == 3:
                    wide(S_CP, S_CP % 2, wcv, 0)
            wide(S_CP + 1, (S_CP + 1) % 2, wcv, 2 * P)
            for i in range(4):
                for half in range(2):
                    n = 2 * i + half
                    if n < 2:
                        sp.wait_ge(unit_free[n], U_GP // 2 + 4)
                    else:
                        sp.wait_ge(mm_t, n - 1)
                    gates(n, 1)
                    sp.wait_ge(m_stored[half], 64)
                    sp.dma_start(mt[:, half, :, :],
                                 m_d[2 * i:2 * i + 2, :, half * HALF:(half + 1) * HALF].rearrange("a p t -> p a t"))\
                        .then_inc(mt_full[half], 16)
                s = S_CP + i + 1
                if i == 0:
                    sp.wait_ge(ct_lo, KT + 2)
                    for a in range(2):
                        oraw(O_CP + a, a, omv, a)
                if i < 3:
                    if i:
                        wide(s, s % 2, wcv, (i + 1) * 2 * P)
                    for a in range(2):
                        oraw(O_CP + 2 * (i + 1) + a, a, omv, 2 * (i + 1) + a)
            for a in range(2):
                two_blocks(S_FFN2 + a, (S_FFN2 + a) % 2, w2v, a * P, w2v, DFF + a * P)
            for a in range(2):
                oraw(O_FFN2 + a, a, o2v, a)
            sp.wait_ge(mm_t, 7)
            sp.dma_start(gB[:, :], mix_post_g[0, :].partition_broadcast(P)).then_inc(gb_full, 16)
            norm(8, x1_d, x2_d, x_stored, (mm_t, 8), (h_lo, HU_FFN2))

            sp.dma_start(gB[:, :], ffn2_post_g[0, :].partition_broadcast(P)).then_inc(gb_full, 16)
            ffn(S_FFN2, O_FFN2, w2v, o2v)
            for t in range(TT):
                sp.wait_ge(x_stored[t], 32)
            norm(16, x2_d, outv, [out_stored] * TT, None, (o_lo, O_END))
            sp.wait_ge(out_stored, 16 * TT)

        @block.tensor
        def _(pe):
            def dense(dst, hi, lo, xh, xl, ks=range(KT), ready=None, halfway=None):
                for n, k in enumerate(ks):
                    if halfway and n == KT // 2:
                        halfway()
                    if ready and n in ready:
                        pe.wait_ge(*ready[n])
                    pe.matmul(dst, hi(k), xh(k), start=(n == 0), stop=False)
                    pe.matmul(dst, hi(k), xl(k), start=False, stop=False)
                    last = pe.matmul(dst, lo(k), xh(k), start=False, stop=(n == KT - 1))
                return last

            def unit(u, p, s, par, half, nblk, ready=None, ks=range(KT), between=None, late=None):
                pe.wait_ge(w_lo, s + 1)
                pe.wait_ge(unit_free[p], u)
                tok = slice(half * HALF, (half + 1) * HALF)
                for b in range(nblk):
                    if b and between:
                        between()
                    col = slice(b * P, (b + 1) * P)
                    last = dense(PU[:, p, b, :], lambda k: w_h[:, par, k, col], lambda k: w_l[:, par, k, col],
                                 lambda k: XH[:, k, tok], lambda k: XL[:, k, tok], ks, None if b else ready, late if b else None)
                last.then_inc(unit_done, 1)

            def v_unit(u, idx, s, par, half):
                pe.wait_ge(w_lo, s + 1)
                pe.wait_ge(unit_free[idx % 2], u)
                for j in range(4):
                    tok = slice((4 * half + j) * P, (4 * half + j + 1) * P)
                    last = dense(PU[:, idx % 2, j // 2, (j % 2) * DV:(j % 2 + 1) * DV],
                                 lambda k: XH[:, k, tok], lambda k: XL[:, k, tok],
                                 lambda k: w_h[:, par, k, :], lambda k: w_l[:, par, k, :])
                last.then_inc(unit_done, 1)

            def g_wait(p, n):
                pe.wait_ge(g_free[p], n)

            def out_half(half, n0, o, wait_a, wait_b, fresh, tps=(0, 1)):
                for tp in tps:
                    for a in range(2):
                        if tp == 0:
                            pe.wait_ge(h_lo, (wait_a, wait_b)[a])
                            pe.wait_ge(o_lo, o + a + 1)
                        for t in (0, 1):
                            tok = slice((4 * half + 2 * tp + t) * P, (4 * half + 2 * tp + t + 1) * P)
                            for n in range(2):
                                if a == 0:
                                    g_wait(t, n0 + 2 * tp - (1 if n == 0 and not (fresh and tp == 0) else 0))
                                dst = PG[:, t, n * 512:(n + 1) * 512]
                                col = slice(n * 512, (n + 1) * 512)
                                pe.matmul(dst, H[:, a, 0, tok], o_h[:, a, col], start=(a == 0), stop=False)
                                pe.matmul(dst, H[:, a, 0, tok], o_l[:, a, col], start=False, stop=False)
                                last = pe.matmul(dst, H[:, a, 1, tok], o_h[:, a, col], start=False, stop=(a == 1))
                                if a == 1:
                                    last.then_inc(g_done, 1)

            def transposes(banks, free, done, n, p0, half, fps):
                if fps[0] == 0:
                    pe.wait_ge(xn_ready, p0 + 4 * half + 4)
                for fp in fps:
                    if n // 2 + fp // 2:
                        pe.wait_ge(free[fp % 2], n // 2 + fp // 2)
                    for fi in range(2):
                        f = 2 * fp + fi
                        for j in range(4):
                            c = (4 * half + j) * D + f * P
                            last = pe.transpose(banks(fp % 2, fi)[:, j * P:(j + 1) * P], FACC[:, c:c + P], ident[:, :])
                    last.then_inc(done, 1)

            def u_transposes(u, p0, half, fps=range(4)):
                transposes(lambda p, b: PU[:, p, b, :], unit_free, unit_done, u, p0, half, fps)

            def g_transposes(g, p0, half, fps):
                transposes(lambda p, b: PG[:, p, b * 512:(b + 1) * 512], g_free, g_done, g, p0, half, fps)

            def filled(free, n):
                return {2 * fp: (free[fp % 2], n // 2 + fp // 2 + 1) for fp in range(4)}

            def ffn(s0, u0, g0, hu0, o0, p0, next_first):
                def parts(i, first=False):
                    s, hu, o, g = s0 + 2 * i, hu0 + 4 * i, o0 + 2 * i, g0 // 2 + 2 + 8 * i

                    def ab(idx, ready=None, between=None, late=None):
                        unit(u0 // 2 + 2 * i + idx // 2, idx % 2, s + idx % 2, (s0 + idx) % 2, idx // 2, 2, ready,
                             between=between, late=late)

                    def out0(tps=(0, 1)):
                        out_half(0, g, o, hu + 1, hu + 2, first, tps)

                    def out1(shift=0):
                        out_half(1, g + 4 + shift, o, hu + 3, hu + 4, shift > 0)

                    return ab, out0, out1

                def rest(ab, out0, out1, ready=None):
                    ab(2, ready)
                    out0((0,))
                    ab(3)
                    out0((1,))
                    out1()

                ab, out0, out1 = parts(0, True)
                ab(0, filled(unit_free, u0 - 4))
                ab(1, between=lambda: g_transposes(g0, p0, 1, (0, 1)), late=lambda: g_transposes(g0, p0, 1, (2, 3)))
                rest(ab, out0, out1, filled(g_free, g0))
                with pe.Fori(1, FPAIRS - 1) as i:
                    ab, out0, out1 = parts(i)
                    ab(0)
                    ab(1)
                    rest(ab, out0, out1)
                ab, out0, out1 = parts(FPAIRS - 1)
                ab(0)
                ab(1)
                out0()
                ab(2)
                if next_first:
                    ab(3, between=lambda: g_transposes(G_N1A, p0 + 8, 0, (0, 1)),
                       late=lambda: g_transposes(G_N1A, p0 + 8, 0, (2, 3)))
                    out1(2)
                else:
                    ab(3)
                    out1()

            pe.wait_ge(ident_in, 16)
            pe.wait_ge(gain_in, 16)
            pe.transpose(PG[:, 1, 0:8], vec_rows[0:8, :], ident[0:8, 0:8]).then_inc(cols_ps, 1)
            u_transposes(U_IN0, 0, 0)
            pe.wait_ge(rows_in, 144)
            pe.transpose(PG[:, 0, 0:P], vec_rows[:, :], ident[:, :])
            for i in range(2):
                last = pe.transpose(PG[:, 0, 512 + i * P:512 + (i + 1) * P], cw_rows[:, i, :], ident[:, :])
            last.then_inc(cols_ps, 1)
            pe.wait_ge(cols_ready, 3)
            ffn(S_FFN1, U_FFN1, G_FFN1, HU_FFN1, O_FFN1, 0, True)
            pe.wait_ge(const_set, 3)

            def head(h, first):
                s0 = S_HEAD + 8 * h
                u0 = U_HEAD // 2 + 8 * h
                gf = G_HEAD // 2 + 8 * h

                def hu(j, half, nblk=2):
                    unit(u0 + j, half, s0 + j, (S_HEAD + j) % 2, half, nblk)

                def level(lv, m):
                    g_wait(lv % 2, gf + 1 + lv // 2)
                    pe.wait_ge(t_ready, 8 * h + m + 1)
                    for c in range(TT):
                        tok = slice(c * P, (c + 1) * P)
                        right = R[:, m % 3, tok].rearrange("p (s a n) -> p s a n", a=2, n=1 << lv)[:, :, 1, :]
                        last = pe.matmul(PG[:, lv % 2, c * P // 2:(c + 1) * P // 2], R[:, m % 3, tok], right,
                                         start=True, stop=True)
                    last.then_inc(g_done, 1)

                if first:
                    s1 = S_HEAD + 1
                    unit(U_X // 2, 0, S_HEAD, S_HEAD % 2, 0, 2, filled(g_free, G_N1A))
                    unit(U_X // 2, 1, s1, s1 % 2, 0, 1)
                    u_transposes(U_N1B, 8, 1)
                    unit(U_HEAD // 2 + 1, 0, S_HEAD, S_HEAD % 2, 1, 2, filled(unit_free, U_N1B))
                    unit(U_HEAD // 2 + 1, 1, s1, s1 % 2, 1, 1)
                    pe.wait_ge(unit_free[0], U_HEAD // 2 + 2)
                pe.wait_ge(wgu_full, 16 * h + 16)
                g_wait(0, gf)
                for n in range(2):
                    last = pe.matmul(PG[:, 0, n * 512:(n + 1) * 512], wgu[:, :], glrT[:, n * 512:(n + 1) * 512],
                                     start=True, stop=True)
                last.then_inc(g_done, 1)
                if not first:
                    for j in (J_OG0, J_OG1):
                        for half in range(2):
                            hu(j, half, 1)
                for half in range(2):
                    hu(J_QK, half)
                for half in range(2):
                    v_unit(u0 + J_V, half, s0 + J_V, (S_HEAD + J_V) % 2, half)
                g_wait(1, gf)
                pe.wait_ge(t_ready, 8 * h + 1)
                for c in range(TT):
                    tok = slice(c * P, (c + 1) * P)
                    last = pe.transpose(PG[:, 1, tok], R[:, 0, tok], ident[:, :])
                last.then_inc(g_done, 1)
                level(0, 1)
                level(1, 2)
                hu(J_CA, 0)
                level(2, 3)
                level(3, 4)
                level(4, 5)
                hu(J_CA, 1)
                level(5, 6)
                level(6, 7)
                g_wait(1, gf + 4)
                for c in range(TT):
                    tok = slice(c * P, (c + 1) * P)
                    last = pe.matmul(PG[:, 1, tok], k_sb[:, tok], q_sb[:, tok], start=True, stop=True)
                last.then_inc(g_done, 1)
                hu(J_CB, 0)
                pe.wait_ge(g_free[1], gf + 1)
                for half in range(2):
                    pe.wait_ge(unit_free[half], u0 + J_V + 1)
                for half in range(2):
                    g_wait(half, gf + 5)
                    for c in range(4 * half, min(4 * half + 4, TT - 1)):
                        last = pe.matmul(PG[:, half, (c % 4) * DV:(c % 4 + 1) * DV], kdT[:, c * P:(c + 1) * P],
                                         v_sb[:, c, :], start=True, stop=True)
                    last.then_inc(g_done, 1)
                hu(J_CB, 1)
                pe.wait_ge(qb_ready, h + 1)
                for half in range(2):
                    pe.wait_ge(g_free[half], gf + 5)
                for half in range(2):
                    g_wait(half, gf + 6)
                    for c in range(4 * half, 4 * half + 4):
                        dst = PG[:, half, (c % 4) * DV:(c % 4 + 1) * DV]
                        pe.matmul(dst, A_sb[:, c, :], v_sb[:, c, :], start=True, stop=False)
                        last = pe.matmul(dst, qb[:, c * P:(c + 1) * P], S_sb[:, c, :], start=False, stop=True)
                    last.then_inc(g_done, 1)
                hu(J_G0, 0)
                for half in range(2):
                    g_wait(half, gf + 7)
                for dvt in range(2):
                    for c in range(TT):
                        last = pe.transpose(PG[:, dvt, c * P:(c + 1) * P], ON[:, c, dvt * P:(dvt + 1) * P], ident[:, :])
                    last.then_inc(g_done, 1)
                hu(J_G0, 1)
                for half in range(2):
                    hu(J_G1, half)

            head(0, True)
            with pe.Fori(1, HEADS) as h:
                head(h, False)

            def gp(e, half, between=None):
                ready = {n: (ot_lo, KT * half + n + 1) for n in range(KT)} if e == 0 else None
                unit(U_GP // 2 + e, half, S_GP + e, (S_GP + e) % 2, half, 2, ready, GP_KS, between)

            def mean():
                pe.wait_ge(c_sum, KT - 1)
                for half in range(2):
                    g_wait(half, G_LN // 2)
                    pe.matmul(PG[:, half, 0:512], ones_m[:, :], vr[:, half, :], start=True, stop=True).then_inc(g_done, 1)

            def variance():
                pe.wait_ge(sq_sum, KT - 1)
                g_wait(0, G_LN // 2 + 1)
                for c in range(TT):
                    last = pe.matmul(PG[:, 0, c:c + 1], vr[:, c // 4, (c % 4) * P:(c % 4 + 1) * P], ones_m[:, 0:1],
                                     start=True, stop=True)
                last.then_inc(g_done, 1)

            def rows():
                pe.wait_ge(diag_ready, 1)
                g_wait(1, G_LN // 2 + 1)
                for half in range(2):
                    last = pe.matmul(PG[:, 1, half * 512:(half + 1) * 512], ones_m[:, :], vr[:, half, :],
                                     start=True, stop=True)
                last.then_inc(g_done, 1)

            gp(0, 0)
            gp(0, 1)
            gp(1, 0)
            gp(1, 1)
            mean()
            gp(2, 0)
            gp(2, 1)
            variance()
            gp(3, 0, rows)
            gp(3, 1)

            for i in range(4):
                for half in range(2):
                    ready = {n: (ct_lo, 8 * half + n + 1) for n in range(KT)} if i == 0 else None
                    unit(U_CP // 2 + i, half, S_CP + i, (S_CP + i) % 2, half, 2, ready, CT_KS)
                hu = HU_CP + 2 * i
                out_half(0, G_CP // 2 + 8 * i, O_CP + 2 * i, hu + 1, hu + 1, i == 0)
                out_half(1, G_CP // 2 + 8 * i + 4, O_CP + 2 * i, hu + 2, hu + 2, False)
            u_transposes(U_N2A, 16, 0)
            ffn(S_FFN2, U_FFN2, G_FFN2, HU_FFN2, O_FFN2, 16, False)

        @block.scalar
        def _(act):
            A = act.activation

            def hi(par, full, used, nblk=2):
                act.wait_ge(raw_full[par], full)
                if used is not None:
                    act.wait_ge(unit_done, used)
                A(w_h[:, par, :, 0:nblk * P], w_raw[:, par, :, 0:nblk * P], ACT.Copy).then_inc(w_hi, 1)

            def full(s, turns):
                return 32 * (s // 2 + 1) + 32 * turns

            def ohi(i, a, o0, g):
                act.wait_ge(o_full[a], 16 * (o0 // 2 + 1) + 16 * i)
                if not (isinstance(g, int) and g == 0):
                    act.wait_ge(g_done, g)
                A(o_h[:, a, :], o_raw[:, a, :], ACT.Copy).then_inc(o_hi, 1)

            def facc(t):
                return FACC[:, t * D:(t + 1) * D]

            squares = [0, 0]

            def square(t, kind, junk):
                for n, done in zip(squares, (sq1, sq2)):
                    if n:
                        act.wait_ge(done, n)
                squares[kind] += 1
                A(junk[:, :], facc(t), ACT.Square, accum_out=st[:, 12 * kind + t % 4:12 * kind + t % 4 + 1])\
                    .then_inc((sq1, sq2)[kind], 1)

            def square1(t, q0, g, junk):
                act.wait_ge(g_free[t % 2], g + 2 * (t % 4 // 2) + 2)
                if t >= 4:
                    act.wait_ge(rs1, q0 + t - 3)
                square(t, 0, junk)

            def square2(t, p0, junk):
                if p0:
                    act.wait_ge(x_new, p0 - 8 + t + 1)
                else:
                    act.wait_ge(x_in[t], 16)
                square(t, 1, junk)

            def scale(t, p0):
                act.wait_ge(x_stored[t], 2 * p0)
                act.wait_ge(rs2, p0 + t + 1)
                A(facc(t), facc(t), ACT.Copy, scale=st[:, 20 + t % 4:21 + t % 4]).then_inc(xn_ready, 1)

            def fill(banks, done, n, gain, half, fps=range(4)):
                for fp in fps:
                    act.wait_ge(done, n + fp + 1)
                    for fi in range(2):
                        f = 2 * fp + fi
                        A(XH[:, f, half * HALF:(half + 1) * HALF], banks(fp % 2, fi), ACT.Copy,
                          scale=cols[:, gain + f:gain + f + 1]).then_inc(xt_hi, 1)

            def u_fill(u, gain, half, fps=range(4)):
                fill(lambda p, b: PU[:, p, b, :], unit_done, u, gain, half, fps)

            def g_fill(g, gain, half):
                fill(lambda p, b: PG[:, p, b * 512:(b + 1) * 512], g_done, g, gain, half)

            def evacuate(i, idx, u0):
                p, a, half = idx % 2, idx % 2, idx // 2
                act.wait_ge(unit_done, u0 + 4 * i + idx + 1)
                act.wait_ge(unit_free[p], u0 // 2 + 2 * i + idx // 2)
                A(sgt[:, p, :], PU[:, p, 0, :], ACT.Silu).then_inc(sg_ready, 1)
                act.wait_ge(unit_free[p], u0 // 2 + 2 * i + idx // 2 + 1)
                A(H[:, a, 0, half * HALF:(half + 1) * HALF], hf[:, p, :], ACT.Copy).then_inc(h_hi, 1)

            def ffn(s0, u0, g0, o0, gain, last_turn):
                def ahead(i, a, nblk=2):
                    s = s0 + 2 + a
                    hi(s % 2, full(s, i), u0 + 4 * i + 3 + a, nblk)

                def step(i, after_a0=None):
                    evacuate(i, 0, u0)
                    for r in range(2):
                        ohi(i, r, o0, g0 + 4 + 16 * i if after_a0 is None else g0)
                    if after_a0:
                        after_a0()
                    evacuate(i, 1, u0)
                    evacuate(i, 2, u0)
                    ahead(i, 0)
                    evacuate(i, 3, u0)
                    ahead(i, 1)

                step(0, lambda: g_fill(g0, gain, 1))
                with act.Fori(1, FPAIRS - 1) as i:
                    step(i)
                i = FPAIRS - 1
                evacuate(i, 0, u0)
                for r in range(2):
                    ohi(i, r, o0, g0 + 4 + 16 * i)
                evacuate(i, 1, u0)
                last_turn(i, lambda a, nblk: ahead(i, a, nblk), g0 // 2 + 2 + 8 * i)

            for t in range(4):
                square2(t, 0, junk_s)
            act.wait_ge(cols_ready, 1)
            u_fill(U_IN0, V_FFN1, 0, (0, 1))
            hi(0, 32, None)
            u_fill(U_IN0, V_FFN1, 0, (2, 3))
            for t in range(4, 8):
                square2(t, 0, junk_s)
            hi(1, 32, None)
            act.wait_ge(sq2, TT)

            def ffn1_last(i, ahead, g):
                def s1(t):
                    square1(t, 0, g + 6 * (t // 4), junk_w)

                def s2(t):
                    square2(t, 8, junk_w)

                s1(0), s1(1), s2(0), s1(2), s2(1), s1(3), s2(2), scale(0, 8), scale(1, 8), s2(3), scale(2, 8), scale(3, 8)
                evacuate(i, 2, U_FFN1)
                ahead(0, 2)
                g_fill(G_N1A, V_MIX, 0)
                evacuate(i, 3, U_FFN1)
                ahead(1, 1)
                s1(4), s1(5), s2(4), s1(6), s2(5), s1(7), scale(4, 8), s2(6), scale(5, 8), scale(6, 8), s2(7)

            ffn(S_FFN1, U_FFN1, G_FFN1, O_FFN1, V_FFN1, ffn1_last)

            def to_gate(h, k, half):
                j = J_G0 + k
                act.wait_ge(unit_done, U_HEAD + 16 * h + 2 * j + half + 1)
                if k == 0:
                    act.wait_ge(pool_mul, 8 * h + 7 + half)
                else:
                    act.wait_ge(gate_stored[half], 32 * h + 16)
                A(tmp[:, half, :, :], PU[:, half, :, :], ACT.Sigmoid).then_inc(unit_free[half], 1)
                act.wait_ge(unit_free[half], U_HEAD // 2 + 8 * h + j + 1)
                act.dma_start(gate_d[:, ds(2 * h + k, 1), :, half * HALF:(half + 1) * HALF]
                              .rearrange("a f p t -> p (a f) t"), tmp[:, half, :, :]).then_inc(gate_stored[half], 16)

            def head(h, first):
                u0 = U_HEAD + 16 * h
                g0 = G_HEAD + 16 * h

                def ahead(j, nblk=2):
                    s = S_HEAD + j + 1
                    used = u0 + 2 * j
                    if first and j == J_OG1:
                        used = U_HEAD + 3
                    hi(s % 2, full(s, 4 * h), used, nblk)

                def to_tmp(j, half, turn, gated):
                    act.wait_ge(unit_done, u0 + 2 * j + half + 1)
                    if turn < 2:
                        act.wait_ge(gate_stored[half], 32 * h)
                    else:
                        act.wait_ge(pool_mul, 8 * h + turn - 1)
                    A(tmp[:, half, 0, :], PU[:, half, gated, :], ACT.Sigmoid)
                    A(tmp[:, half, 1, :], PU[:, half, 0, :], ACT.Copy).then_inc(unit_free[half], 1)

                def exps(first, last):
                    for m in range(first, last):
                        act.wait_ge(d_ready, 8 * h + m + 1)
                        A(R[:, m % 3, :], R[:, m % 3, :], ACT.Exp, scale=1.0 / 16).then_inc(e_ready, 1)

                if first:
                    def og_tmp(half, d, muls):
                        act.wait_ge(unit_done, (U_X, U_HEAD + 2)[half] + d + 1)
                        if muls:
                            act.wait_ge(pool_mul, muls)
                        bank = PU[:, d, 1 - d, :]
                        A(tmp[:, d, 0, :], bank, ACT.Sigmoid)
                        op = A(tmp[:, d, 1, :], bank, ACT.Copy)
                        if d == 0:
                            op = A(glrT[:, half * HALF:(half + 1) * HALF], PU[0:RANK, 0, 0, :], ACT.Copy)
                        op.then_inc(unit_free[d], 1)

                    og_tmp(0, 0, 0)
                    scale(7, 8)
                    og_tmp(0, 1, 0)
                    u_fill(U_N1B, V_MIX, 1)
                    og_tmp(1, 0, 1)
                    ahead(J_OG1)
                    og_tmp(1, 1, 2)
                else:
                    to_gate(h - 1, 1, 1)
                    ahead(J_OG0, 1)
                A(st[:, 28:29], cols[:, ds(V_BG + h, 1)], ACT.Copy).then_inc(lg_act, 1)
                act.wait_ge(lg_act, 4 * h + 1)
                act.wait_ge(g_done, g0 + H_LG + 1)
                A(R[:, 0, :], PG[:, 0, :], ACT.Abs, bias=st[:, 28:29]).then_inc(lg_act, 1)
                act.wait_ge(lg_act, 4 * h + 2)
                A(R[:, 0, :], R[:, 0, :], ACT.Exp, scale=-1.0).then_inc(lg_act, 1)
                act.wait_ge(lg_act, 4 * h + 3)
                A(R[:, 0, :], R[:, 0, :], ACT.Ln, bias=1.0).then_inc(lg_act, 1)
                if not first:
                    for half in range(2):
                        to_tmp(J_OG0, half, half, 0)
                    ahead(J_OG1)
                    for half in range(2):
                        to_tmp(J_OG1, half, 2 + half, 0)
                ahead(J_QK)
                for half in range(2):
                    tok = slice(half * HALF, (half + 1) * HALF)
                    act.wait_ge(unit_done, u0 + 2 * J_QK + half + 1)
                    A(q_sb[:, tok], PU[:, half, 0, :], ACT.Copy, scale=DK ** -0.5)
                    A(k_sb[:, tok], PU[:, half, 1, :], ACT.Copy).then_inc(unit_free[half], 1)
                exps(0, 3)
                A(qb[:, :], b_sb[:, :], ACT.Exp, scale=1.0 / 16).then_inc(qb_exp, 1)
                A(el[:, :], b_sb[:, P - 1:SEQ:P], ACT.Exp, scale=1.0 / 16).then_inc(el_ready, 1)
                ahead(J_V)
                for half in range(2):
                    act.wait_ge(unit_done, u0 + 2 * J_V + half + 1)
                    A(v_sb[:, 4 * half:4 * half + 4, :], PU[:, half, :, :].rearrange("p a (b n) -> p (a b) n", b=2),
                      ACT.Copy).then_inc(unit_free[half], 1)
                act.wait_ge(g_done, g0 + H_KT + 1)
                A(kdT[:, :], PG[:, 1, :], ACT.Copy).then_inc(g_free[1], 1)
                exps(3, 6)
                ahead(J_CA)
                to_tmp(J_CA, 0, 4, 1)
                exps(6, 8)
                to_tmp(J_CA, 1, 5, 1)
                ahead(J_CB)
                for half in range(2):
                    to_tmp(J_CB, half, 6 + half, 1)
                for half in range(2):
                    act.wait_ge(g_done, g0 + H_O + half + 1)
                    for c in range(4):
                        if not (first and half == 0 and c == 0):
                            act.wait_ge(o_sq, 8 * h + 4 * half + c)
                        A(junk_o[:, :], PG[:, half, c * DV:(c + 1) * DV], ACT.Square,
                          accum_out=st[:, 4 * half + c:4 * half + c + 1]).then_inc(o_sq, 1)
                    act.wait_ge(o_rs, 2 * h + half + 1)
                    for c in range(4):
                        last = A(ON[:, 4 * half + c, :], PG[:, half, c * DV:(c + 1) * DV], ACT.Copy,
                                 scale=st[:, 20 + 4 * half + c:21 + 4 * half + c])
                    last.then_inc(g_free[half], 1)
                ahead(J_G0)
                for k, half in ((0, 0), (0, 1), (1, 0)):
                    to_gate(h, k, half)
                    if (k, half) == (0, 1):
                        ahead(J_G1)

            head(0, True)
            with act.Fori(1, HEADS) as h:
                head(h, False)

            for half in range(2):
                act.wait_ge(unit_done, U_GP - 1 + half)
                for k in GP_KS:
                    if k >= KT - 2:
                        act.wait_ge(g_free[k % 2], G_LN // 2)
                        src = og[:, k % 2, half * HALF:(half + 1) * HALF]
                    else:
                        act.wait_ge(ot_full, 16 * (KT - 2))
                        src = OTF[:, k, half * HALF:(half + 1) * HALF]
                    A(XH[:, k, half * HALF:(half + 1) * HALF], src, ACT.Copy).then_inc(xt_hi, 1)
                if half == 0:
                    to_gate(HEADS - 1, 1, 1)

            def gp_ahead(e):
                s = S_GP + e + 1
                hi(s % 2, full(s, 0), U_GP + 2 * e)

            def store_m(e, half):
                if e == 0:
                    act.wait_ge(m_ready, half + 1)
                else:
                    act.wait_ge(unit_free[half], U_GP // 2 + e + 1)
                act.dma_start(m_d[2 * e:2 * e + 2, :, half * HALF:(half + 1) * HALF].rearrange("a p t -> p a t"),
                              mt[:, half, :, :]).then_inc(m_stored[half], 16)

            gp_ahead(0)
            for half in range(2):
                act.wait_ge(unit_done, U_GP + half + 1)
                act.wait_ge(gate_stored[half], 32 * HEADS)
                A(mt[:, half, :, :], PU[:, half, :, :], ACT.Copy).then_inc(unit_free[half], 1)
            gp_ahead(1)
            for e in range(2):
                for half in range(2):
                    store_m(e, half)
            gp_ahead(2)
            for k in range(KT):
                if k < KT - 1:
                    act.wait_ge(centred, k + 1)
                else:
                    for p in range(2):
                        act.wait_ge(g_free[p], G_LN // 2 + 1)
                if k == 0:
                    A(vr[:, :, :].rearrange("p a n -> p (a n)"), CB[:, CPLACE[0], :], ACT.Square).then_inc(sq_ready, 1)
                    continue
                if k >= 3:
                    act.wait_ge(sq_sum, k - 2)
                A(sq[:, k % 2, :], CB[:, CPLACE[k], :], ACT.Square).then_inc(sq_ready, 1)
            for half in range(2):
                store_m(2, half)
            gp_ahead(3)
            for k in range(KT):
                if k < KT - 1:
                    act.wait_ge(scaled, k + 1)
                else:
                    act.wait_ge(g_free[1], G_LN // 2 + 2)
                c = CB[:, CPLACE[k], :]
                A(c, c, ACT.Silu, scale=cols[:, V_LG + k:V_LG + k + 1],
                  bias=cols[:, V_LB + k:V_LB + k + 1]).then_inc(c_act, 1)
            for half in range(2):
                act.wait_ge(unit_done, U_CP - 1 + half)
                for k in CT_KS:
                    act.wait_ge(c_act, k + 1)
                    A(XH[:, k, half * HALF:(half + 1) * HALF], CB[:, CPLACE[k], half * HALF:(half + 1) * HALF],
                      ACT.Copy).then_inc(xt_hi, 1)
                store_m(3, half)

            for i in range(4):
                s = S_CP + i + 1
                hi(s % 2, full(s, 0), U_CP + 2 * i)
                if i == 0:
                    act.wait_ge(ct_lo, 2 * KT)
                for r in range(2):
                    ohi(i, r, O_CP, G_CP + 16 * i)
                for half in range(2):
                    act.wait_ge(mm_t, 2 * i + half + 1)
                    A(H[:, :, 0, half * HALF:(half + 1) * HALF], hf[:, :, :], ACT.Copy).then_inc(h_hi, 1)
            hi((S_FFN2 + 1) % 2, full(S_FFN2 + 1, 0), U_CP + 8)

            def s1(t):
                square1(t, 8, G_CP // 2 + 24 + 4 * (t // 4), junk_s)

            def s2(t):
                square2(t, 16, junk_s)

            def sc(t):
                scale(t, 16)

            s1(0), s1(1), s2(0), s1(2), s2(1), s1(3), s2(2), s1(4), s2(3)
            sc(0), s1(5), sc(1), s2(4), sc(2), s1(6), sc(3), s2(5), s1(7)
            u_fill(U_N2A, V_FFN2, 0)
            s2(6), sc(4), s2(7), sc(5), sc(6), sc(7)

            def ffn2_last(i, ahead, g):
                for t in range(4):
                    square1(t, 16, g + 4 * (t // 4), junk_w)
                evacuate(i, 2, U_FFN2)
                evacuate(i, 3, U_FFN2)
                for t in range(4, 8):
                    square1(t, 16, g + 4 * (t // 4), junk_w)

            ffn(S_FFN2, U_FFN2, G_FFN2, O_FFN2, V_FFN2, ffn2_last)

        @block.vector
        def _(dve):
            TT_, STT, TS = dve.tensor_tensor, dve.scalar_tensor_tensor, dve.tensor_scalar

            posts = [0]

            def post(t, q0):
                f = FACC[:, t * D:(t + 1) * D]
                dve.wait_ge(rs1, q0 + t + 1)
                dve.wait_ge(x_full[t % 3], 16 * ((3, 3, 2)[t % 3] * (q0 // 8) + t // 3 + 1))
                third = xt_s if q0 == 8 else xt_w
                res = third[:, :] if t % 3 == 2 else xt[:, t % 3, :]
                r = st[:, 4 + t % 4:5 + t % 4]
                if t in POOL_TILES:
                    dve.wait_ge(pre_mul, len(POOL_TILES) * q0 // 8 + POOL_TILES.index(t) + 1)
                    STT(f, f, r, res, ALU.mult, ALU.add).then_inc(x_new, 1)
                    return
                dve.wait_ge(gb_full, 2 * q0 + 16)
                posts[0] += 1
                STT(f, f, r, gB[:, :], ALU.mult, ALU.mult).then_inc(post_a, 1)
                dve.wait_ge(post_a, posts[0])
                TT_(f, f, res, ALU.add).then_inc(x_new, 1)

            def fill(banks, free, gain, half, hi0, fps=range(4)):
                for fp in fps:
                    for fi in range(2):
                        f = 2 * fp + fi
                        dve.wait_ge(xt_hi, hi0 + 8 * half + f + 1)
                        last = STT(XL[:, f, half * HALF:(half + 1) * HALF], banks(fp % 2, fi),
                                   cols[:, gain + f:gain + f + 1], XH[:, f, half * HALF:(half + 1) * HALF],
                                   ALU.mult, ALU.subtract)
                    last.then_inc(free[fp % 2], 1)

            def u_fill(gain, half, hi0, fps=range(4)):
                fill(lambda p, b: PU[:, p, b, :], unit_free, gain, half, hi0, fps)

            def g_fill(gain, half, hi0):
                fill(lambda p, b: PG[:, p, b * 512:(b + 1) * 512], g_free, gain, half, hi0)

            def add_out(t, g, first=False):
                for n in range(2):
                    f = FACC[:, t * D + n * 512:t * D + (n + 1) * 512]
                    dve.wait_ge(g_done, g + 2 * t + n + 1)
                    src = PG[:, t % 2, n * 512:(n + 1) * 512]
                    op = dve.tensor_copy(f, src) if first else TT_(f, src, f, ALU.add)
                    op.then_inc(g_free[t % 2], 1)

            def hidden(i, idx, u0, hu0):
                p, a, half = idx % 2, idx % 2, idx // 2
                sg0 = hu0 - 8 * (hu0 > HU_CP)
                dve.wait_ge(sg_ready, sg0 + 4 * i + idx + 1)
                TT_(hf[:, p, :], PU[:, p, 1, :], sgt[:, p, :], ALU.mult).then_inc(unit_free[p], 1)
                dve.wait_ge(h_hi, hu0 + 4 * i + idx + 1)
                tok = slice(half * HALF, (half + 1) * HALF)
                TT_(H[:, a, 1, tok], hf[:, p, :], H[:, a, 0, tok], ALU.subtract).then_inc(h_lo, 1)

            def ffn(u0, g0, hu0, gain, hi0, last_turn):
                def rest(i, g):
                    hidden(i, 2, u0, hu0)
                    for t in (0, 1):
                        add_out(t, g, isinstance(i, int))
                    hidden(i, 3, u0, hu0)
                    for t in range(2, 8):
                        add_out(t, g, isinstance(i, int))

                hidden(0, 0, u0, hu0)
                g_fill(gain, 1, hi0)
                hidden(0, 1, u0, hu0)
                rest(0, g0 + 4)
                with dve.Fori(1, FPAIRS - 1) as i:
                    hidden(i, 0, u0, hu0)
                    hidden(i, 1, u0, hu0)
                    rest(i, g0 + 4 + 16 * i)
                i = FPAIRS - 1
                for idx in (0, 1):
                    hidden(i, idx, u0, hu0)
                last_turn(i, g0 + 4 + 16 * i)

            def scale(t):
                f = FACC[:, t * D:(t + 1) * D]
                dve.wait_ge(rs2, t + 1)
                TS(f, f, st[:, 20 + t % 4:21 + t % 4], None, ALU.mult).then_inc(xn_ready, 1)

            scale(0)
            dve.wait_ge(cols_ps, 1)
            dve.tensor_copy(cols[:, 0:8], PG[:, 1, 0:8]).then_inc(cols_ready, 1)
            for t in range(1, 4):
                scale(t)
            dve.wait_ge(cols_ready, 1)
            u_fill(V_FFN1, 0, 0, (0, 1))
            dve.wait_ge(w_hi, 1)
            TT_(w_l[:, 0, :, :], w_raw[:, 0, :, :], w_h[:, 0, :, :], ALU.subtract).then_inc(w_lo, 1)
            u_fill(V_FFN1, 0, 0, (2, 3))
            dve.wait_ge(cols_ps, 2)
            dve.tensor_copy(cols[:, 8:VROWS], PG[:, 0, 8:VROWS]).then_inc(cols_ready, 1)
            dve.tensor_copy(cw[:, :], PG[:, 0, 512:512 + 8 * TAPS]).then_inc(cols_ready, 1)
            for t in range(4, 8):
                scale(t)
            dve.wait_ge(mask_in, 16)
            dve.tensor_copy(masks[:, :, :], mask_rows[:, :, :]).then_inc(cols_ready, 1)

            def ffn1_last(i, g):
                def ps(t):
                    post(t, 0)

                def add(t):
                    add_out(t, g + 4 * (t // 4))

                add(0), add(1), ps(0), add(2), ps(1), add(3), ps(2), ps(3)
                hidden(i, 2, U_FFN1, HU_FFN1)
                g_fill(V_MIX, 0, 16)
                hidden(i, 3, U_FFN1, HU_FFN1)
                add(4), add(5), ps(4), add(6), ps(5), add(7), ps(6), ps(7)

            ffn(U_FFN1, G_FFN1, HU_FFN1, V_FFN1, 0, ffn1_last)
            dve.wait_ge(const_set, 3)
            dve.wait_ge(cols_ready, 4)
            dve.memset(A_sb[:, :, :], 0.0).then_inc(gla_zero, 1)
            for a in range(2):
                dve.memset(ub[:, a, 0:TAPS - 1], 0.0).then_inc(conv_free, 1)
            u_fill(V_MIX, 1, 16)
            dve.memset(S_sb[:, 0, :], 0.0).then_inc(gla_zero, 1)

            bc = b_sb[:, :].rearrange("p (c n) -> p c n", n=P)

            def head(h):
                g0 = G_HEAD + 16 * h
                gf = G_HEAD // 2 + 8 * h
                un = U_HEAD // 2 + 8 * h

                def minus(m):
                    r = R[:, m % 3, :]
                    if m == 0:
                        TT_(r.rearrange("p (c n) -> p c n", n=P), bc[:, :, P - 1:P].to_broadcast([P, TT, P]), bc,
                            ALU.subtract).then_inc(d_ready, 1)
                        return
                    n = 1 << (m - 1)
                    bv = b_sb[:, :].rearrange("p (c s n) -> p c s n", s=2, n=n)
                    rv = r.rearrange("p (c s n) -> p c s n", s=2, n=n)
                    mid = bv[:, :, 0, n - 1:n].to_broadcast([P, SEQ // (2 * n), n])
                    TT_(rv[:, :, 1, :], bv[:, :, 1, :], mid, ALU.subtract)
                    TT_(rv[:, :, 0, :], mid, bv[:, :, 0, :], ALU.subtract).then_inc(d_ready, 1)

                def times(m):
                    dve.wait_ge(e_ready, 8 * h + m + 1)
                    r = R[:, m % 3, :]
                    if m == 0:
                        TT_(r, r, k_sb[:, :], ALU.mult).then_inc(t_ready, 1)
                        return
                    n = 1 << (m - 1)
                    rv, qv, kv = [y.rearrange("p (c s n) -> p c s n", s=2, n=n) for y in (r, q_sb[:, :], k_sb[:, :])]
                    TT_(rv[:, :, 1, :], rv[:, :, 1, :], qv[:, :, 1, :], ALU.mult)
                    TT_(rv[:, :, 0, :], rv[:, :, 0, :], kv[:, :, 0, :], ALU.mult).then_inc(t_ready, 1)

                def select(lv):
                    dve.wait_ge(gla_zero, 2)
                    if lv:
                        dve.wait_ge(g_free[(lv - 1) % 2], gf + (H_LV + lv - 1) // 2 + 1)
                    dve.wait_ge(g_done, g0 + H_LV + lv + 1)
                    dve.nop(nofuse=True)
                    if lv == 7:
                        dve.copy_predicated(A_sb[:, :, :], masks[:, lv:lv + 1, :].to_broadcast([P, TT, P]),
                                            PG[:, 1, :].rearrange("p (c n) -> p c n", n=P)).then_inc(g_free[1], 1)
                        return
                    n = 1 << lv
                    right = "p c (s a n) -> p c s a n"
                    dve.copy_predicated(
                        A_sb[:, :, :].rearrange(right, a=2, n=n)[:, :, :, 1, :],
                        masks[:, lv:lv + 1, :].rearrange(right, a=2, n=n)[:, :, :, 1, :].to_broadcast([P, TT, P // (2 * n), n]),
                        PG[:, lv % 2, 0:SEQ // 2].rearrange("p (c s n) -> p c s n", c=TT, n=n)).then_inc(g_free[lv % 2], 1)

                dve.wait_ge(g_done, g0 + H_LG + 1)
                dve.wait_ge(lg_act, 4 * h + 2)
                TS(R[:, 1, :], PG[:, 0, :], cols[:, ds(V_BG + h, 1)], 0.0, ALU.add, ALU.min).then_inc(g_free[0], 1)
                dve.wait_ge(g_free[0], gf + 1)
                dve.wait_ge(lg_act, 4 * h + 4)
                TT_(R[:, 1, :], R[:, 1, :], R[:, 0, :], ALU.subtract).then_inc(la_done, 1)
                dve.wait_ge(la_done, h + 1)
                for c in range(TT):
                    tok = slice(c * P, (c + 1) * P)
                    last = dve.tensor_tensor_scan(b_sb[:, tok], one_c[:, 0:1].to_broadcast([P, P]), R[:, 1, tok], 0.0,
                                                  ALU.mult, ALU.add)
                last.then_inc(b_done, 1)
                dve.wait_ge(b_done, h + 1)
                for m in range(3):
                    minus(m)
                for half in range(2):
                    dve.wait_ge(unit_free[half], un + J_QK + 1)
                for m in range(3):
                    times(m)
                dve.wait_ge(qb_exp, h + 1)
                TT_(qb[:, :], qb[:, :], q_sb[:, :], ALU.mult).then_inc(qb_ready, 1)
                dve.wait_ge(g_done, g0 + H_KT + 1)
                minus(3)
                select(0)
                minus(4)
                select(1)
                minus(5)
                for m in (3, 4, 5):
                    times(m)
                select(2)
                minus(6)
                select(3)
                minus(7)
                select(4)
                times(6)
                times(7)
                select(5)
                select(6)
                select(7)
                dve.wait_ge(el_ready, h + 1)
                n = 0
                for c in range(TT - 1):
                    if c in (0, 4):
                        dve.wait_ge(g_done, g0 + H_ST + c // 4 + 1)
                    if c == 4:
                        dve.wait_ge(g_free[0], gf + 6)
                    elif c:
                        dve.wait_ge(state_step, 5 * h + n)
                    op = STT(S_sb[:, c + 1, :], S_sb[:, c, :], el[:, c:c + 1], PG[:, c // 4, (c % 4) * DV:(c % 4 + 1) * DV],
                             ALU.mult, ALU.add)
                    if c in (3, 6):
                        op.then_inc(g_free[c // 4], 1)
                    else:
                        op.then_inc(state_step, 1)
                        n += 1

                def conv(a):
                    dve.wait_ge(pool_mul, 8 * h + 6 + 2 * a)
                    if not isinstance(h, int):
                        dve.wait_ge(c_stored[a], 16 * h)
                    per = 2 * TAPS - 1
                    for w in range(TAPS):
                        for half in range(2):
                            n = 2 * w + half
                            o = acc[:, a, half * HALF:(half + 1) * HALF]
                            src = ub[:, a, half * HALF + w:half * HALF + w + HALF]
                            tap = cw[:, ds(8 * w + a + 2 * h, 1)]
                            if w == 0:
                                op = TS(o, src, tap, cols[:, ds(V_CB + a + 2 * h, 1)], ALU.mult, ALU.add)
                            else:
                                dve.wait_ge(conv_step, per * (2 * h + a) + n - 1)
                                op = STT(o, src, tap, o, ALU.mult, ALU.add)
                            op.then_inc(conv_step if n < per else conv_free, 1)

                conv(0)
                for d in range(2):
                    dve.wait_ge(g_done, g0 + H_OT + d + 1)
                    dve.wait_ge(pool_mul, 8 * h + 4)
                    STT(og[:, d, :], PG[:, d, :], cols[:, V_GN + d:V_GN + d + 1], og[:, d, :], ALU.mult, ALU.mult)\
                        .then_inc(g_free[d], 1)
                conv(1)

            head(0)
            with dve.Fori(1, HEADS) as h:
                head(h)

            def gated(e, half):
                dve.wait_ge(gt_full[half], 16 * (e + 1))
                if e == 0:
                    m = mt[:, half, :, :]
                    dve.wait_ge(unit_free[half], U_GP // 2 + 1)
                    TT_(m, m, gt[:, half, :, :], ALU.mult).then_inc(m_ready, 1)
                    return
                dve.wait_ge(unit_done, U_GP + 2 * e + half + 1)
                dve.wait_ge(m_stored[half], 16 * e)
                TT_(mt[:, half, :, :], PU[:, half, :, :], gt[:, half, :, :], ALU.mult).then_inc(unit_free[half], 1)

            vrf = vr[:, :, :].rearrange("p a n -> p (a n)")

            def c_tile(k):
                return CB[:, CPLACE[k], :]

            gated(0, 0)
            gated(0, 1)
            for k in (KT - 2, KT - 1):
                dve.wait_ge(c_late, 32)
                dve.wait_ge(c_sum, k - 1)
                TT_(vrf, vrf, c_tile(k), ALU.add).then_inc(c_sum, 1)
            gated(1, 0)
            gated(1, 1)
            def square_sum(k):
                dve.wait_ge(sq_ready, k + 1)
                if k > 1:
                    dve.wait_ge(sq_sum, k - 1)
                TT_(vrf, vrf, sq[:, k % 2, :], ALU.add).then_inc(sq_sum, 1)

            dve.wait_ge(g_done, G_LN + 2)
            for k in range(KT):
                if k < KT - 1:
                    v = c_tile(k).rearrange("p (a n) -> p a n", a=2)
                    TT_(v, v, PG[:, :, 0:512], ALU.subtract).then_inc(centred, 1)
                else:
                    for half in range(2):
                        v = CB[:, CPLACE[k], half * HALF:(half + 1) * HALF]
                        TT_(v, v, PG[:, half, 0:512], ALU.subtract).then_inc(g_free[half], 1)
                if k >= 2:
                    square_sum(k - 1)
            square_sum(KT - 1)
            gated(2, 0)
            dve.wait_ge(g_done, G_LN + 3)
            TS(st[:, 0:TT], PG[:, 0, 0:TT], EPS, None, ALU.add).then_inc(g_free[0], 1)
            gated(2, 1)
            dve.wait_ge(rs_ready, 1)
            for c in range(TT):
                last = TS(vr[:, c // 4, (c % 4) * P:(c % 4 + 1) * P], ident[:, :], st[:, 8 + c:9 + c], float(D),
                          ALU.mult, ALU.mult)
            last.then_inc(diag_ready, 1)
            dve.wait_ge(g_done, G_LN + 4)
            for k in range(KT):
                TT_(c_tile(k), c_tile(k), PG[:, 1, :], ALU.mult).then_inc(scaled if k < KT - 1 else g_free[1], 1)
            gated(3, 0)
            for half in range(2):
                for n, k in enumerate(CT_KS):
                    tok = slice(half * HALF, (half + 1) * HALF)
                    dve.wait_ge(xt_hi, 48 + 8 * half + n + 1)
                    TT_(XL[:, k, tok], CB[:, CPLACE[k], tok], XH[:, k, tok], ALU.subtract).then_inc(ct_lo, 1)
                if half == 0:
                    gated(3, 1)

            def post2(t):
                post(t, 8)

            for i in range(4):
                for half in range(2):
                    n = 2 * i + half
                    dve.wait_ge(unit_done, U_CP + n + 1)
                    dve.wait_ge(gt_full[half], 64 + 16 * (i + 1))
                    TT_(gt[:, half, :, :], PU[:, half, :, :], gt[:, half, :, :], ALU.mult).then_inc(unit_free[half], 1)
                    dve.wait_ge(unit_free[half], U_CP // 2 + i + 1)
                    dve.wait_ge(mt_full[half], 16 * (i + 1))
                    TT_(hf[:, :, :], gt[:, half, :, :], mt[:, half, :, :], ALU.add).then_inc(mm_t, 1)
                    dve.wait_ge(h_hi, HU_CP + n + 1)
                    if half:
                        add_out(0, G_CP + 16 * i, i == 0)
                    tok = slice(half * HALF, (half + 1) * HALF)
                    TT_(H[:, :, 1, tok], hf[:, :, :], H[:, :, 0, tok], ALU.subtract).then_inc(h_lo, 1)
                for t in range(1, TT):
                    add_out(t, G_CP + 16 * i, i == 0)
                    if i == 3:
                        post2(t - 1)
            u_fill(V_FFN2, 0, 64)
            post2(7)

            def ffn2_last(i, g):
                def ps(t):
                    post(t, 16)

                def add(t):
                    add_out(t, g)

                add(0), add(1), ps(0), add(2), ps(1), add(3), ps(2), ps(3)
                for idx in (2, 3):
                    hidden(i, idx, U_FFN2, HU_FFN2)
                add(4), add(5), ps(4), add(6), ps(5), add(7), ps(6), ps(7)

            ffn(U_FFN2, G_FFN2, HU_FFN2, V_FFN2, 64, ffn2_last)

        @block.gpsimd
        def _(pool):
            PT, PS = pool.tensor_tensor, pool.tensor_scalar

            def lo(s, par, nblk=2):
                pool.wait_ge(w_hi, s + 1)
                c = slice(0, nblk * P)
                PT(w_l[:, par, :, c], w_raw[:, par, :, c], w_h[:, par, :, c], ALU.subtract).then_inc(w_lo, 1)

            def olo(o, a):
                pool.wait_ge(o_hi, o + 1)
                PT(o_l[:, a, :], o_raw[:, a, :], o_h[:, a, :], ALU.subtract).then_inc(o_lo, 1)

            def rstd(src, dst, n, scale, pows, done, eps=EPS):
                pool.nop(nofuse=True)
                PS(src, src, scale, eps, ALU.mult, ALU.add).then_inc(pow_in, 1)
                pool.wait_ge(pow_in, pows)
                PT(dst, src, half_c[:, 0:n], ALU.pow).then_inc(done, 1)

            def rs(kind, t, q0, pows):
                j = t % 4
                if kind == 1:
                    if t >= 4:
                        pool.wait_ge(x_new, q0 + t - 3)
                    pool.wait_ge(sq1, q0 + t + 1)
                    m = 1.0 if q0 == 8 else 4.0
                    rstd(st[:, j:j + 1], st[:, 4 + j:5 + j], 1, m / D, pows, rs1, m * EPS)
                    if t in POOL_TILES:
                        f = FACC[:, t * D:(t + 1) * D]
                        pool.wait_ge(gb_full, 2 * q0 + 16)
                        PT(f, f, gB[:, :], ALU.mult).then_inc(pre_mul, 1)
                else:
                    if q0 == 0 and t >= 4:
                        pool.wait_ge(xn_ready, t - 3)
                    pool.wait_ge(sq2, q0 + t + 1)
                    rstd(st[:, 12 + j:13 + j], st[:, 20 + j:21 + j], 1, 1.0 / D, pows, rs2)

            def staggered(q0, p0, ts, pows):
                for t in (*ts, None):
                    if t is not None:
                        pows += 1
                        rs(1, t, q0, pows)
                    if t is None or t > ts[0]:
                        pows += 1
                        rs(2, ts[-1] if t is None else t - 1, p0, pows)

            pool.memset(vec_rows[:, :], 0.0).then_inc(rows_zero, 1)
            pool.memset(cw_rows[:, :, :], 0.0).then_inc(rows_zero, 1)
            pool.memset(half_c[:, :], -0.5).then_inc(const_set, 1)
            pool.memset(one_c[:, :], 1.0).then_inc(const_set, 1)
            pool.memset(ones_m[:, :], 1.0 / D).then_inc(const_set, 1)
            pool.wait_ge(const_set, 3)
            for t in range(8):
                rs(2, t, 0, t + 1)
            pool.wait_ge(w_lo, 1)
            lo(1, 1)

            def ffn(s0, o0):
                with pool.Fori(0, FPAIRS - 1) as i:
                    for a in range(2):
                        olo(o0 + 2 * i + a, a)
                    for a in range(2):
                        lo(s0 + 2 * i + 2 + a, (s0 + a) % 2)
                for a in range(2):
                    olo(o0 + 2 * (FPAIRS - 1) + a, a)

            ffn(S_FFN1, O_FFN1)
            staggered(0, 8, range(4), 8)
            lo(S_HEAD, S_HEAD % 2)
            lo(S_HEAD + 1, (S_HEAD + 1) % 2, 1)
            staggered(0, 8, range(4, 8), 16)

            def head(h, first):
                s0 = S_HEAD + 8 * h
                un = U_HEAD // 2 + 8 * h

                def ahead(j, nblk=2):
                    lo(s0 + j + 1, (S_HEAD + j + 1) % 2, nblk)

                def og_mul(d, half, p, n):
                    pool.wait_ge(unit_free[p], n)
                    PT(og[:, d, half * HALF:(half + 1) * HALF], tmp[:, p, 0, :], tmp[:, p, 1, :], ALU.mult)\
                        .then_inc(pool_mul, 1)

                if first:
                    og_mul(0, 0, 0, U_X // 2 + 1)
                    og_mul(1, 0, 1, U_X // 2 + 1)
                    og_mul(0, 1, 0, U_HEAD // 2 + 2)
                    ahead(J_OG1)
                    og_mul(1, 1, 1, U_HEAD // 2 + 2)
                    ahead(J_QK)
                else:
                    ahead(J_OG0, 1)
                    pool.wait_ge(ot_stored, 16 * h)
                    for d, j in ((0, J_OG0), (1, J_OG1)):
                        for half in range(2):
                            og_mul(d, half, half, un + j + 1)
                        ahead(j + 1)
                ahead(J_V)
                ahead(J_CA)
                for a, j in ((0, J_CA), (1, J_CB)):
                    pool.wait_ge(conv_free, 2 * h + a + 1)
                    for half in range(2):
                        pool.wait_ge(unit_free[half], un + j + 1)
                        PT(ub[:, a, TAPS - 1 + half * HALF:TAPS - 1 + (half + 1) * HALF], tmp[:, half, 0, :],
                           tmp[:, half, 1, :], ALU.mult).then_inc(pool_mul, 1)
                    if a == 0:
                        ahead(J_CB)
                for half in range(2):
                    pool.wait_ge(o_sq, 8 * h + 4 * half + 4)
                    rstd(st[:, 4 * half:4 * half + 4], st[:, 20 + 4 * half:24 + 4 * half], 4, 1.0 / DV,
                         24 + 2 * h + half + 1, o_rs)
                ahead(J_G0)
                ahead(J_G1)

            head(0, True)
            with pool.Fori(1, HEADS) as h:
                head(h, False)

            for half in range(2):
                tok = slice(half * HALF, (half + 1) * HALF)
                for n, k in enumerate(GP_KS):
                    pool.wait_ge(xt_hi, 32 + 8 * half + n + 1)
                    src = og[:, k % 2, tok] if k >= KT - 2 else OTF[:, k, tok]
                    PT(XL[:, k, tok], src, XH[:, k, tok], ALU.subtract).then_inc(ot_lo, 1)
            lo(S_GP + 1, (S_GP + 1) % 2)
            vrf = vr[:, :, :].rearrange("p a n -> p (a n)")
            pool.wait_ge(c_early, 16 * (KT - 2))
            for k in range(1, KT - 2):
                if k > 1:
                    pool.wait_ge(c_sum, k - 1)
                PT(vrf, CB[:, CPLACE[0], :] if k == 1 else vrf, CB[:, CPLACE[k], :], ALU.add).then_inc(c_sum, 1)
            lo(S_GP + 2, (S_GP + 2) % 2)
            lo(S_GP + 3, (S_GP + 3) % 2)
            pool.wait_ge(g_free[0], G_LN // 2 + 2)
            PT(st[:, 8:8 + TT], st[:, 0:TT], half_c[:, :], ALU.pow).then_inc(rs_ready, 1)
            lo(S_CP, S_CP % 2)
            for i in range(4):
                lo(S_CP + i + 1, (S_CP + i + 1) % 2)
                for r in range(2):
                    olo(O_CP + 2 * i + r, r)
            staggered(8, 16, range(8), 32)
            lo(S_FFN2 + 1, (S_FFN2 + 1) % 2)
            ffn(S_FFN2, O_FFN2)
            for t in range(8):
                rs(1, t, 16, 48 + t + 1)


INPUTS = ["x", "ffn1_pre_g", "ffn1_w_in", "ffn1_w_out", "ffn1_post_g", "mix_pre_g", "w_mix_in", "gla_w_gate_up",
          "gla_b_gate", "gla_norm_g", "gla_w_proj", "conv_dw_w", "conv_dw_b", "conv_ln_g", "conv_ln_b",
          "conv_w_proj", "w_mix_out", "mix_post_g", "ffn2_pre_g", "ffn2_w_in", "ffn2_w_out", "ffn2_post_g"]


def kernel(**inputs):
    import numpy as np
    import concourse.bacc as bacc
    from concourse.bass_utils import run_bass_kernel_spmd

    nc = bacc.Bacc("TRN2", target_bir_lowering=False, num_devices=1)
    j, i = np.arange(P)[:, None], np.arange(P)[None, :]
    levels = [(j // (2 * n) == i // (2 * n)) & (j % (2 * n) < n) & (i % (2 * n) >= n) for n in (1 << l for l in range(7))]
    masks = np.stack(levels + [i == j], axis=1).astype(np.float32)
    arrays = {f"in_{n}": np.ascontiguousarray(inputs[n]) for n in INPUTS}
    arrays["c_ident"] = np.eye(P, dtype=np.float32)
    arrays["c_masks"] = np.ascontiguousarray(masks)
    args = [nc.dram_tensor(n, a.shape, mybir.dt.from_np(a.dtype), kind="ExternalInput").ap() for n, a in arrays.items()]
    out = nc.dram_tensor("out_dram", (1, SEQ, D), mybir.dt.float32, kind="ExternalOutput").ap()
    build(nc, *args, out)
    r = run_bass_kernel_spmd(nc, [arrays], core_ids=[0])
    return r.results[0]["out_dram"]
```
